# Optimizing a Trainium2 kernel written in Bass

```python
import math
import jax, jax.numpy as jnp
from jax import lax
import numpy as np

D_MODEL = 1024
BATCH = 1
SEQ = 128
DEPTH = 1
DEC_BATCH = 1
DEC_SEQ = 1024
PAST_LEN = 128

GRID_W = 64
D_MIX = D_MODEL
N_DIR = 2
D_RWKV = D_MIX // 2
HEAD_DIM = 64
N_RWKV_HEADS = D_RWKV // HEAD_DIM
DECAY_LORA = 64
ICLR_LORA = 64
GATE_LORA = 128
D_SSM = D_MIX - D_RWKV
SSM_GROUP = 16
N_SSM_GROUPS = D_SSM // SSM_GROUP
SSM_STATE = 64
D_FF = 4 * D_MODEL
N_MOD = 6
RMS_EPS = 1e-6
GN_EPS = 64e-5
OFF_R = 0
OFF_K = OFF_R + D_RWKV
OFF_V = OFF_K + D_RWKV
OFF_WD = OFF_V + D_RWKV
OFF_AD = OFF_WD + N_DIR * DECAY_LORA
OFF_GD = OFF_AD + N_DIR * ICLR_LORA
OFF_U = OFF_GD + GATE_LORA
D_IN_PROJ = OFF_U + D_SSM

kernel_name = "hybrid_rwkv7_s5_flow_step"

def rms_norm(x, g):
    x32 = x.astype(jnp.float32)
    y = x32 * lax.rsqrt(jnp.mean(x32 * x32, axis=-1, keepdims=True) + RMS_EPS)
    return (y * g.astype(jnp.float32)).astype(x.dtype)

def grid_pos_embed(n_tok, d):
    rows = n_tok // GRID_W
    nf = d // 4
    omega = 1.0 / (10000.0 ** (jnp.arange(nf, dtype=jnp.float32) / nf))
    ang_r = jnp.arange(rows, dtype=jnp.float32)[:, None] * omega
    ang_c = jnp.arange(GRID_W, dtype=jnp.float32)[:, None] * omega
    e_r = jnp.concatenate([jnp.sin(ang_r), jnp.cos(ang_r)], axis=-1)
    e_c = jnp.concatenate([jnp.sin(ang_c), jnp.cos(ang_c)], axis=-1)
    pe = jnp.concatenate([jnp.broadcast_to(e_r[:, None], (rows, GRID_W, d // 2)),
                          jnp.broadcast_to(e_c[None], (rows, GRID_W, d // 2))], axis=-1)
    return pe.reshape(rows * GRID_W, d)

def _heads(x):
    return x.reshape(x.shape[:-1] + (N_RWKV_HEADS, HEAD_DIM))

def rwkv7_mix(z, s0, decay_base, w_decay_up, iclr_base, w_iclr_up, w_gate_up,
              k_k, k_a, r_k, lnx_g, lnx_b):
    f32 = jnp.float32
    bsz, t = z.shape[0], z.shape[1]
    zf = z.astype(f32)
    r = zf[..., OFF_R:OFF_K]
    k = zf[..., OFF_K:OFF_V]
    v = zf[..., OFF_V:OFF_WD]
    wd = zf[..., OFF_WD:OFF_AD].reshape(bsz, t, N_DIR, DECAY_LORA)
    ad = zf[..., OFF_AD:OFF_GD].reshape(bsz, t, N_DIR, ICLR_LORA)
    gd = zf[..., OFF_GD:OFF_U]
    logw = -jax.nn.softplus(-(decay_base.astype(f32)
                              + jnp.einsum('btdr,drc->btdc', jnp.tanh(wd), w_decay_up.astype(f32)))) - 0.5
    w = jnp.exp(-jnp.exp(logw))
    a = jax.nn.sigmoid(iclr_base.astype(f32)
                       + jnp.einsum('btdr,drc->btdc', ad, w_iclr_up.astype(f32)))
    g = jax.nn.sigmoid(gd) @ w_gate_up.astype(f32)
    kk = _heads(k * k_k.astype(f32))
    kk = (kk / jnp.maximum(jnp.linalg.norm(kk, axis=-1, keepdims=True), 1e-12)).reshape(bsz, t, D_RWKV)
    k_dir = k[:, :, None] * (1.0 + (a - 1.0) * k_a.astype(f32))
    b_dir = kk[:, :, None] * a

    def two(x):
        return jnp.broadcast_to(x[:, :, None], (bsz, t, N_DIR, D_RWKV))

    def seq(x):
        x = jnp.stack([x[:, :, 0], jnp.flip(x[:, :, 1], axis=1)], axis=0)
        return jnp.moveaxis(_heads(x), 2, 0)

    xs = (seq(two(r)), seq(w), seq(k_dir), seq(two(v)), seq(two(-kk)), seq(b_dir))

    def step(S, inp):
        r_t, w_t, k_t, v_t, ma_t, b_t = inp
        sa = jnp.einsum('dbhij,dbhj->dbhi', S, ma_t)
        S = S * w_t[..., None, :] + sa[..., None] * b_t[..., None, :] + v_t[..., None] * k_t[..., None, :]
        return S, jnp.einsum('dbhij,dbhj->dbhi', S, r_t)

    s_last, ys = lax.scan(step, jnp.moveaxis(s0.astype(f32), 1, 0), xs)
    y = jnp.moveaxis(ys[:, 0] + jnp.flip(ys[:, 1], axis=0), 0, 1)
    mu = jnp.mean(y, axis=-1, keepdims=True)
    var = jnp.mean(jnp.square(y - mu), axis=-1, keepdims=True)
    y = ((y - mu) * lax.rsqrt(var + GN_EPS)).reshape(bsz, t, D_RWKV) * lnx_g.astype(f32) + lnx_b.astype(f32)
    bonus = jnp.sum(_heads(r) * _heads(k) * r_k.astype(f32), axis=-1, keepdims=True) * _heads(v)
    y = (y + bonus.reshape(bsz, t, D_RWKV)) * g
    return y.astype(z.dtype), jnp.moveaxis(s_last, 0, 1)

def s5_mix(u, h0_re, h0_im, lam_re, lam_im, log_dt, b_re, b_im, c_re, c_im, d_skip, w_glu, b_glu):
    f32 = jnp.float32
    bsz, t = u.shape[0], u.shape[1]
    uf = u.astype(f32)
    ug = uf.reshape(bsz, t, N_SSM_GROUPS, SSM_GROUP)
    lam = lax.complex(lam_re.astype(f32), lam_im.astype(f32))
    dt = jnp.exp(log_dt.astype(f32))
    lam_dt = lam[None] * dt[..., None]
    lam_bar = jnp.exp(lam_dt)
    b_mat = lax.complex(b_re.astype(f32), b_im.astype(f32))
    b_bar = ((lam_bar - 1.0) / lam[None])[..., None] * b_mat
    bu = jnp.einsum('dgph,btgh->dbtgp', b_bar, ug)
    bu = jnp.stack([bu[0], jnp.flip(bu[1], axis=1)], axis=0)
    a_el = jnp.broadcast_to(lam_bar[:, None, None], (N_DIR, 1, t, N_SSM_GROUPS, SSM_STATE))

    def combine(e1, e2):
        a1, x1 = e1
        a2, x2 = e2
        return a2 * a1, a2 * x1 + x2

    _, h = lax.associative_scan(combine, (a_el, bu), axis=2)
    h0 = jnp.moveaxis(lax.complex(h0_re.astype(f32), h0_im.astype(f32)), 1, 0)
    tpos = jnp.arange(1, t + 1, dtype=f32)
    decay_pow = jnp.exp(lam_dt[:, None] * tpos[None, :, None, None])
    h = h + decay_pow[:, None] * h0[:, :, None]
    h_last = jnp.moveaxis(h[:, :, -1], 0, 1)
    c_mat = lax.complex(c_re.astype(f32), c_im.astype(f32))
    y = jnp.real(jnp.einsum('dghp,dbtgp->dbtgh', c_mat, h))
    y = (y[0] + jnp.flip(y[1], axis=1)).reshape(bsz, t, D_SSM) + d_skip.astype(f32) * uf
    y = jax.nn.gelu(y)
    y = y * jax.nn.sigmoid(y @ w_glu.astype(f32) + b_glu.astype(f32))
    return y.astype(u.dtype), jnp.real(h_last), jnp.imag(h_last)

def trunk_layer(x, cond, st_rwkv, st_re, st_im, lp):
    mod = jax.nn.silu(cond) @ lp['w_ada'] + lp['b_ada']
    sh1, sc1, g1, sh2, sc2, g2 = jnp.split(mod[:, None, :], N_MOD, axis=-1)
    h = rms_norm(x, lp['norm1_g']) * (1.0 + sc1) + sh1
    z = h @ lp['w_in']
    y_r, s_r = rwkv7_mix(z, st_rwkv, lp['decay_base'], lp['w_decay_up'], lp['iclr_base'],
                         lp['w_iclr_up'], lp['w_gate_up'], lp['k_k'], lp['k_a'], lp['r_k'],
                         lp['lnx_g'], lp['lnx_b'])
    y_s, s_re, s_im = s5_mix(z[..., OFF_U:], st_re, st_im, lp['ssm_lambda_re'], lp['ssm_lambda_im'],
                             lp['ssm_log_dt'], lp['ssm_b_re'], lp['ssm_b_im'], lp['ssm_c_re'],
                             lp['ssm_c_im'], lp['ssm_d'], lp['w_glu'], lp['b_glu'])
    x = x + g1 * (jnp.concatenate([y_r, y_s], axis=-1) @ lp['w_out'])
    h = rms_norm(x, lp['norm2_g']) * (1.0 + sc2) + sh2
    x = x + g2 * (jnp.square(jax.nn.relu(h @ lp['w_ff1'])) @ lp['w_ff2'])
    return x, s_r, s_re, s_im

def setup_inputs(seed: int = 0) -> dict:
    key = jax.random.key(seed)
    ks = iter(jax.random.split(key, 48))

    def nrm(shape, scale):
        return jax.random.normal(next(ks), shape, jnp.float32) * scale

    L = DEPTH
    lam_im_base = jnp.broadcast_to(math.pi * jnp.arange(SSM_STATE, dtype=jnp.float32),
                                   (L, N_SSM_GROUPS, SSM_STATE))
    return {
        'x_prompt': nrm((BATCH, SEQ, D_MODEL), 1.0),
        'x_sample': nrm((DEC_BATCH, DEC_SEQ, D_MODEL), 1.0),
        'c': nrm((DEC_BATCH, D_MODEL), 1.0),
        'c_ctx': nrm((D_MODEL,), 1.0),
        'state_rwkv': nrm((DEC_BATCH, L, N_DIR, N_RWKV_HEADS, HEAD_DIM, HEAD_DIM), 0.3),
        'state_ssm_re': nrm((DEC_BATCH, L, N_DIR, N_SSM_GROUPS, SSM_STATE), 0.5),
        'state_ssm_im': nrm((DEC_BATCH, L, N_DIR, N_SSM_GROUPS, SSM_STATE), 0.5),
        'norm1_g': 1.0 + nrm((L, D_MODEL), 0.05),
        'norm2_g': 1.0 + nrm((L, D_MODEL), 0.05),
        'w_ada': nrm((L, D_MODEL, N_MOD * D_MODEL), 0.5 * D_MODEL ** -0.5),
        'b_ada': nrm((L, N_MOD * D_MODEL), 0.01),
        'w_in': nrm((L, D_MODEL, D_IN_PROJ), D_MODEL ** -0.5),
        'decay_base': nrm((L, N_DIR, D_RWKV), 0.5),
        'w_decay_up': nrm((L, N_DIR, DECAY_LORA, D_RWKV), DECAY_LORA ** -0.5),
        'iclr_base': nrm((L, N_DIR, D_RWKV), 0.5),
        'w_iclr_up': nrm((L, N_DIR, ICLR_LORA, D_RWKV), ICLR_LORA ** -0.5),
        'w_gate_up': nrm((L, GATE_LORA, D_RWKV), GATE_LORA ** -0.5),
        'k_k': 0.85 + nrm((L, D_RWKV), 0.05),
        'k_a': 1.0 + nrm((L, D_RWKV), 0.05),
        'r_k': nrm((L, N_RWKV_HEADS, HEAD_DIM), 0.1),
        'lnx_g': 1.0 + nrm((L, D_RWKV), 0.05),
        'lnx_b': nrm((L, D_RWKV), 0.01),
        'ssm_lambda_re': -0.5 + nrm((L, N_SSM_GROUPS, SSM_STATE), 0.02),
        'ssm_lambda_im': lam_im_base + nrm((L, N_SSM_GROUPS, SSM_STATE), 0.02),
        'ssm_log_dt': jax.random.uniform(next(ks), (L, N_DIR, N_SSM_GROUPS), jnp.float32,
                                         math.log(1e-3), math.log(1e-1)),
        'ssm_b_re': nrm((L, N_DIR, N_SSM_GROUPS, SSM_STATE, SSM_GROUP), (2 * SSM_GROUP) ** -0.5),
        'ssm_b_im': nrm((L, N_DIR, N_SSM_GROUPS, SSM_STATE, SSM_GROUP), (2 * SSM_GROUP) ** -0.5),
        'ssm_c_re': nrm((L, N_DIR, N_SSM_GROUPS, SSM_GROUP, SSM_STATE), SSM_STATE ** -0.5),
        'ssm_c_im': nrm((L, N_DIR, N_SSM_GROUPS, SSM_GROUP, SSM_STATE), SSM_STATE ** -0.5),
        'ssm_d': nrm((L, D_SSM), 0.5),
        'w_glu': nrm((L, D_SSM, D_SSM), D_SSM ** -0.5),
        'b_glu': nrm((L, D_SSM), 0.01),
        'w_out': nrm((L, D_MIX, D_MODEL), D_MIX ** -0.5),
        'w_ff1': nrm((L, D_MODEL, D_FF), D_MODEL ** -0.5),
        'w_ff2': nrm((L, D_FF, D_MODEL), D_FF ** -0.5),
        'norm_f_g': 1.0 + nrm((D_MODEL,), 0.05),
    }

def reference(x_prompt, x_sample, c, c_ctx, state_rwkv, state_ssm_re, state_ssm_im,
              norm1_g, norm2_g, w_ada, b_ada, w_in, decay_base, w_decay_up, iclr_base, w_iclr_up,
              w_gate_up, k_k, k_a, r_k, lnx_g, lnx_b, ssm_lambda_re, ssm_lambda_im, ssm_log_dt,
              ssm_b_re, ssm_b_im, ssm_c_re, ssm_c_im, ssm_d, w_glu, b_glu, w_out, w_ff1, w_ff2,
              norm_f_g):
    n_ctx_req = x_prompt.shape[0]
    xp = x_prompt
    cond_ctx = c_ctx[None]
    zero_rwkv = jnp.zeros((n_ctx_req, N_DIR, N_RWKV_HEADS, HEAD_DIM, HEAD_DIM), jnp.float32)
    zero_ssm = jnp.zeros((n_ctx_req, N_DIR, N_SSM_GROUPS, SSM_STATE), jnp.float32)
    n_tok = x_sample.shape[1]
    xs = x_sample + grid_pos_embed(n_tok, D_MODEL).astype(x_sample.dtype)[None]
    new_rwkv, new_re, new_im = [], [], []
    for l in range(DEPTH):
        lp = dict(norm1_g=norm1_g[l], norm2_g=norm2_g[l], w_ada=w_ada[l], b_ada=b_ada[l], w_in=w_in[l],
                  decay_base=decay_base[l], w_decay_up=w_decay_up[l], iclr_base=iclr_base[l],
                  w_iclr_up=w_iclr_up[l], w_gate_up=w_gate_up[l], k_k=k_k[l], k_a=k_a[l], r_k=r_k[l],
                  lnx_g=lnx_g[l], lnx_b=lnx_b[l], ssm_lambda_re=ssm_lambda_re[l],
                  ssm_lambda_im=ssm_lambda_im[l], ssm_log_dt=ssm_log_dt[l], ssm_b_re=ssm_b_re[l],
                  ssm_b_im=ssm_b_im[l], ssm_c_re=ssm_c_re[l], ssm_c_im=ssm_c_im[l], ssm_d=ssm_d[l],
                  w_glu=w_glu[l], b_glu=b_glu[l], w_out=w_out[l], w_ff1=w_ff1[l], w_ff2=w_ff2[l])
        xp, s_r, s_re, s_im = trunk_layer(xp, cond_ctx, zero_rwkv, zero_ssm, zero_ssm, lp)
        new_rwkv.append(s_r)
        new_re.append(s_re)
        new_im.append(s_im)
        xs, _, _, _ = trunk_layer(xs, c, state_rwkv[:, l], state_ssm_re[:, l], state_ssm_im[:, l], lp)
    y_prompt = rms_norm(xp, norm_f_g)
    y_sample = rms_norm(xs, norm_f_g)
    new_state_rwkv = jnp.stack(new_rwkv, axis=1)
    new_state_ssm_re = jnp.stack(new_re, axis=1)
    new_state_ssm_im = jnp.stack(new_im, axis=1)
    return (y_prompt, y_sample, new_state_rwkv, new_state_ssm_re, new_state_ssm_im)


_drawn_inputs = setup_inputs


def setup_inputs(seed=0):
    import zlib

    import numpy as np

    out = dict(_drawn_inputs(seed))
    spreads = {}
    factors = {'state_rwkv': 8.0,
     'state_ssm_re': 3.186,
     'state_ssm_im': 3.346,
     'norm2_g': 2.946,
     'b_ada': 2.935,
     'k_k': 6.492,
     'lnx_g': 8.0,
     'lnx_b': 64.0,
     'ssm_c_re': 3.037,
     'ssm_c_im': 3.007,
     'w_glu': 7.019,
     'b_glu': 200.0}
    for name, (base, spread) in spreads.items():
        noise = np.random.default_rng([zlib.crc32(name.encode()), seed]).standard_normal(out[name].shape)
        drawn = base * np.exp(spread * noise) if base else spread * noise
        out[name] = __import__('jax').numpy.asarray(drawn.astype(out[name].dtype))
    for name, factor in factors.items():
        out[name] = (out[name] * factor).astype(out[name].dtype)
    return out
```

```python
import math
from contextlib import ExitStack

import numpy as np
import concourse.bass as bass
from concourse import mybir
from concourse.alu_op_type import AluOpType as ALU

F32 = mybir.dt.float32
BF16 = mybir.dt.bfloat16
ACT = mybir.ActivationFunctionType
ds = bass.ds

P = 128
D = 1024
KD = D // P
NLAT, NCTX = 1024, 128
T = NLAT + NCTX
LB = NLAT // P
NB = T // P
HEAD = 64
DR = 512
DS = 512
NCT = DR // P
FF = 4 * D
G, GC, NS = 32, 16, 64
CH = 8
LC, CC = NLAT // CH, NCTX // CH
NC_ = LC + CC
SUP = 16
NSUP = NC_ // SUP
GB = 8
NBATCH = G // GB
TG = 3
TW = T // TG
OFF_R, OFF_K, OFF_V = 0, DR, 2 * DR
OFF_WD, OFF_AD, OFF_GD, OFF_U = 3 * DR, 3 * DR + 128, 3 * DR + 256, 3 * DR + 384
D_IN = OFF_U + DS
RMS_EPS, GN_EPS = 1e-6, 64e-5
NLEV = 6
DECAY = -math.exp(-0.5)


class Arena:

    def __init__(self, nc, words):
        self.t = nc.alloc_sbuf_tensor("arena", [P, words], F32)
        self.words, self.at = words, 0

    def take(self, *shape, dt=F32, parts=P):
        n = int(np.prod(shape))
        words = n if dt == F32 else (n + 1) // 2
        assert self.at + words <= self.words, (self.at, words, shape)
        v = self.t[0:parts, self.at:self.at + words]
        self.at += words
        if dt != F32:
            v = v.bitcast(dt)
        names = [f"d{i}" for i in range(len(shape))]
        if len(shape) > 1:
            v = v.rearrange(f"p ({' '.join(names)}) -> p {' '.join(names)}",
                            **{m: s for m, s in zip(names[1:], shape[1:])})
        return v


class Events:

    def __init__(self, nc, ctx, stage):
        self.nc, self.ctx, self.stage, self.sems = nc, ctx, stage, {}

    def __call__(self, name, *index):
        key = "_".join([self.stage, name, *map(str, index)])
        if key not in self.sems:
            self.sems[key] = self.ctx.enter_context(self.nc.semaphore(key))
        return self.sems[key]


def split_mm(nc, out, whi, wlo, xhi, xlo, first, last):
    nc.tensor.matmul(out, whi, xhi, start=first, stop=False)
    nc.tensor.matmul(out, wlo, xhi, start=False, stop=False)
    return nc.tensor.matmul(out, whi, xlo, start=False, stop=last)


def need(eng, sem, value):
    if not isinstance(value, int) or value > 0:
        eng.wait_ge(sem, value)


def rounds(eng, n, body):
    body(0)
    with eng.Fori(1, n) as i:
        body(i)


class Chain:

    def __init__(self, sem, base=0):
        self.sem, self.base, self.n = sem, base, 0

    def step(self, ins):
        ins.then_inc(self.sem, 1)
        self.n += 1
        return self.n

    def settle(self, eng):
        eng.wait_ge(self.sem, self.base + self.n)


def stage_modulation(nc, M, ins):
    A, ps = M.arena, M.ps
    keep = A.at
    cc = A.take(KD, 2)
    th = A.take(KD, 2)
    sc = A.take(KD, 2)
    wst = [A.take(KD, 512) for _ in range(2)]
    mod = A.take(6 * D, parts=2)
    bada = A.take(6 * D, parts=2)
    g12 = A.take(2, KD)
    with ExitStack() as ctx:
        ev = Events(nc, ctx, "mod")
        block = ctx.enter_context(nc.Block())

        @block.sync
        def _(sp):
            sp.dma_start(M.const[:, :], ins["consts"]).then_inc(ev("const"), 16)
            sp.dma_start(cc, ins["cond"]).then_inc(ev("cond"), 16)
            sp.dma_start(bada, ins["b_ada"]).then_inc(ev("bias"), 16)
            sp.dma_start(g12, ins["norm_g"]).then_inc(ev("bias"), 16)

            def load(q, j):
                sp.dma_start(wst[q], ins["w_ada"][:, :, ds(j * 512, 512)]).then_inc(ev("w_loaded", q), 16)
            load(0, 0)
            load(1, 1)
            with sp.Fori(0, 5) as i:
                for q in range(2):
                    sp.wait_ge(ev("products", q), i + 1)
                    load(q, i * 2 + (q + 2))
            for q in range(2):
                sp.wait_ge(ev("stored", q), 6)
            for n in range(2):
                sp.dma_start(ins["gates"][n], mod[0:2, (2 + 3 * n) * D:(3 + 3 * n) * D]).then_inc(ev("gates"), 16)
            sp.wait_ge(ev("gates"), 32)

        @block.scalar
        def _(act):
            act.wait_ge(ev("cond"), 16)
            nc.scalar.activation(th, cc, ACT.Tanh, scale=0.5).then_inc(ev("tanh"), 1)

        @block.tensor
        def _(pe):
            pe.wait_ge(ev("silu"), 1)

            def multiply(i):
                for q in range(2):
                    pe.wait_ge(ev("w_loaded", q), i * 16 + 16)
                    need(pe, ev("stored", q), i)
                    for k in range(KD):
                        last = nc.tensor.matmul(ps[0:2, q, :], sc[:, k, :], wst[q][:, k, :],
                                                start=(k == 0), stop=(k == KD - 1))
                    last.then_inc(ev("products", q), 1)
            rounds(pe, 6, multiply)
            for q in range(2):
                pe.wait_ge(ev("stored", q), 6)
            n = 0
            for part in (0, 1, 3, 4):
                for k in range(KD):
                    last = nc.tensor.transpose(ps[:, 2, 2 * n:2 * n + 2],
                                               mod[0:2, part * D + k * P:part * D + (k + 1) * P], M.ident[0:2, 0:2])
                    n += 1
            last.then_inc(ev("cols_t"), 1)

        @block.vector
        def _(dve):
            dve.wait_ge(ev("tanh"), 1)
            dve.wait_ge(ev("cond"), 16)
            nc.vector.scalar_tensor_tensor(out=sc, in0=th, scalar=1.0, in1=cc, op0=ALU.add,
                                           op1=ALU.mult).then_inc(ev("two_silu"), 1)
            dve.wait_ge(ev("two_silu"), 1)
            nc.vector.tensor_scalar(sc, sc, 0.5, None, ALU.mult).then_inc(ev("silu"), 1)
            dve.wait_ge(ev("bias"), 32)
            with dve.Fori(0, 6) as i:
                for q in range(2):
                    dve.wait_ge(ev("products", q), i + 1)
                    cols = ds((i * 2 + q) * 512, 512)
                    nc.vector.tensor_tensor(mod[0:2, cols], ps[0:2, q, :], bada[0:2, cols],
                                            ALU.add).then_inc(ev("stored", q), 1)
            dve.wait_ge(ev("cols_t"), 1)
            cols = ps[:, 2, 0:64].rearrange("p (q k w) -> p q k w", q=4, k=KD)
            for n in range(2):
                nc.vector.tensor_copy(M.shift[n], cols[:, 2 * n]).then_inc(ev("shift"), 1)
                nc.vector.scalar_tensor_tensor(out=M.scale[n], in0=cols[:, 2 * n + 1], scalar=1.0,
                                               in1=g12[:, n, :].unsqueeze(2).broadcast_to([P, KD, 2]),
                                               op0=ALU.add, op1=ALU.mult).then_inc(ev("scale"), 1)
    clear(nc, ev)
    A.at = keep


def stage_norm(nc, M, name, src, pos, which, hT):
    A, ps = M.arena, M.ps
    keep = A.at
    xt = [A.take(D) for _ in range(2)]
    pt = [A.take(D) for _ in range(2)]
    xn = [A.take(D) for _ in range(2)]
    hf = [A.take(KD, P) for _ in range(2)]
    ss = [A.take(1) for _ in range(2)]
    ms = [A.take(1) for _ in range(2)]
    rs = [A.take(1) for _ in range(2)]
    hi, lo = hT
    per_load = 32 if pos is not None else 16
    with ExitStack() as ctx:
        ev = Events(nc, ctx, name)
        block = ctx.enter_context(nc.Block())

        @block.sync
        def _(sp):
            def load(q, b):
                sp.dma_start(xt[q], src[ds(b, 1)].squeeze(0) if not isinstance(b, int) else src[b]).then_inc(ev("loaded", q), 16)
                if pos is not None:
                    sp.dma_start(pt[q], pos[ds(b, 1)].squeeze(0) if not isinstance(b, int) else pos[b]).then_inc(ev("loaded", q), 16)
            load(0, 0)
            load(1, 1)
            with sp.Fori(0, 3) as i:
                for q in range(2):
                    sp.wait_ge(ev("normed", q), i + 1)
                    load(q, i * 2 + (q + 2))
            sp.wait_ge(ev("normed", 0), 4)
            load(0, LB)

        @block.scalar
        def _(act):
            def norm(q, n):
                act.wait_ge(ev("added", q) if pos is not None else ev("loaded", q),
                            n + 1 if pos is not None else n * 16 + 16)
                need(act, ev("transposed", q), n)
                nc.scalar.activation(xn[q], xt[q], ACT.Square, accum_out=ss[q]).then_inc(ev("squares", q), 1)
                act.wait_ge(ev("squares", q), n + 1)
                nc.scalar.activation(ms[q], ss[q], ACT.Copy, scale=1.0 / D, bias=RMS_EPS).then_inc(ev("mean_sq", q), 1)
                act.wait_ge(ev("rstd", q), n + 1)
                nc.scalar.activation(xn[q], xt[q], ACT.Copy, scale=rs[q]).then_inc(ev("normed", q), 1)

            def high(q, n, b):
                act.wait_ge(ev("modulated", q), n + 1)
                nc.scalar.activation(hi[:, :, ds(b * P, P)], hf[q], ACT.Copy).then_inc(ev("high", q), 1)

            def two(i):
                norm(0, i)
                norm(1, i)
                high(0, i, i * 2)
                high(1, i, i * 2 + 1)
            rounds(act, 4, two)
            norm(0, 4)
            high(0, 4, LB)

        @block.gpsimd
        def _(pool):
            def rstd(q, n):
                pool.wait_ge(ev("mean_sq", q), n + 1)
                nc.gpsimd.tensor_tensor(rs[q], ms[q], M.neg_half, ALU.pow).then_inc(ev("rstd", q), 1)

            def low(q, n, b):
                pool.wait_ge(ev("high", q), n + 1)
                nc.gpsimd.tensor_tensor(lo[:, :, ds(b * P, P)], hf[q], hi[:, :, ds(b * P, P)],
                                        ALU.subtract).then_inc(ev("low", q), 1)
            with pool.Fori(0, 4) as i:
                rstd(0, i)
                rstd(1, i)
                low(0, i, i * 2)
                low(1, i, i * 2 + 1)
            rstd(0, 4)
            low(0, 4, LB)

        @block.tensor
        def _(pe):
            def turn(q, n):
                pe.wait_ge(ev("normed", q), n + 1)
                need(pe, ev("modulated", q), n)
                for k in range(KD):
                    last = nc.tensor.transpose(ps[:, 2 * q + k // 4, (k % 4) * P:(k % 4 + 1) * P],
                                               xn[q][:, k * P:(k + 1) * P], M.ident)
                last.then_inc(ev("transposed", q), 1)

            def two(i):
                turn(0, i)
                turn(1, i)
            rounds(pe, 4, two)
            turn(0, 4)

        @block.vector
        def _(dve):
            def add(q, n):
                if pos is not None:
                    dve.wait_ge(ev("loaded", q), n * per_load + per_load)
                    nc.vector.tensor_tensor(xt[q], xt[q], pt[q], ALU.add).then_inc(ev("added", q), 1)

            def modulate(q, n, w):
                dve.wait_ge(ev("transposed", q), n + 1)
                need(dve, ev("high", q), n)
                need(dve, ev("low", q), n)
                for k in range(KD):
                    last = nc.vector.tensor_scalar(hf[q][:, k, :], ps[:, 2 * q + k // 4, (k % 4) * P:(k % 4 + 1) * P],
                                                   M.scale[which][:, k, w:w + 1], M.shift[which][:, k, w:w + 1],
                                                   ALU.mult, ALU.add)
                last.then_inc(ev("modulated", q), 1)

            def two(i):
                add(0, i)
                add(1, i)
                modulate(0, i, 0)
                modulate(1, i, 0)
            rounds(dve, 4, two)
            add(0, 4)
            modulate(0, 4, 1)
    clear(nc, ev)
    A.at = keep


def clear(nc, ev):
    with nc.Block() as block:
        @block.gpsimd
        def _(pool):
            for s in ev.sems.values():
                pool.sem_clear(s)


def stage_u(nc, M, ins):
    A, ps = M.arena, M.ps
    keep = A.at
    wst = A.take(KD, DS)
    whi, wlo = A.take(KD, DS, dt=BF16), A.take(KD, DS, dt=BF16)
    u_lat = A.take(G, CH, GC)
    u_tok = A.take(DS)
    u_raw = A.take(CH, G, GC, parts=CC)
    u_ctx = A.take(G, CH, GC, parts=CC)
    with ExitStack() as ctx:
        ev = Events(nc, ctx, "u")
        block = ctx.enter_context(nc.Block())

        @block.sync
        def _(sp):
            sp.dma_start(wst, ins["w_in"][:, :, OFF_U:OFF_U + DS]).then_inc(ev("w"), 16)
            sp.wait_ge(ev("ctx_out"), 1)
            sp.dma_start(ins["u_bounce"], u_tok).then_inc(ev("bounced"), 16)
            sp.wait_ge(ev("bounced"), 16)
            sp.dma_start(u_raw.rearrange("c s g n -> c (s g n)"),
                         ins["u_bounce"].rearrange("(c s) n -> c (s n)", s=CH)).then_inc(ev("ctx_in"), 16)

        @block.scalar
        def _(act):
            act.wait_ge(ev("w"), 16)
            nc.scalar.activation(whi, wst, ACT.Copy).then_inc(ev("hi"), 1)
            act.wait_ge(ev("ctx_in"), 16)
            nc.scalar.activation(u_ctx, u_raw.rearrange("c s g n -> c g s n"), ACT.Copy).then_inc(ev("ctx"), 1)
            for g in range(0, G, 3):
                n = min(3, G - g)
                act.wait_ge(ev("turned"), g // 3 + 1)
                nc.scalar.activation(M.u[:, g:g + n, :], ps[:, 2 + g // 3 % 2, 0:n * NC_].rearrange("p (g c) -> p g c", g=n),
                                     ACT.Copy).then_inc(ev("u"), 1)

        @block.gpsimd
        def _(pool):
            pool.wait_ge(ev("hi"), 1)
            nc.gpsimd.tensor_tensor(wlo, wst, whi, ALU.subtract).then_inc(ev("lo"), 1)

        @block.tensor
        def _(pe):
            pe.wait_ge(ev("lo"), 1)

            def project(q, n, col):
                need(pe, ev("stored", q), n)
                for k in range(KD):
                    last = split_mm(nc, ps[:, q, :], M.hi[:, k, col], M.lo[:, k, col], whi[:, k, :], wlo[:, k, :],
                                    k == 0, k == KD - 1)
                last.then_inc(ev("product", q), 1)

            def two(i):
                for q in range(2):
                    project(q, i, ds(i * 2 + q, LC, CH))
            rounds(pe, CH // 2, two)
            project(0, CH // 2, slice(NLAT, T))
            pe.wait_ge(ev("stored", 1), CH // 2)
            pe.wait_ge(ev("stored", 0), CH // 2)
            pe.wait_ge(ev("ctx"), 1)
            for g in range(G):
                b = g // 3
                if g % 3 == 0 and b >= 2:
                    pe.wait_ge(ev("u"), b - 1)
                o = g % 3 * NC_
                nc.tensor.transpose(ps[:, 2 + b % 2, o:o + LC], u_lat[:, g].rearrange("p s c -> p (s c)"), M.ident)
                last = nc.tensor.transpose(ps[:, 2 + b % 2, o + LC:o + NC_], u_ctx[:, g].rearrange("p s c -> p (s c)"),
                                           M.ident[0:CC, 0:CC])
                if g % 3 == 2 or g == G - 1:
                    last.then_inc(ev("turned"), 1)

        @block.vector
        def _(dve):
            with dve.Fori(0, CH // 2) as i:
                for q in range(2):
                    dve.wait_ge(ev("product", q), i + 1)
                    nc.vector.tensor_copy(u_lat[:, :, ds(i * 2 + q, 1), :], ps[:, q, :].rearrange("p (g x c) -> p g x c", g=G, x=1)).then_inc(ev("stored", q), 1)
            dve.wait_ge(ev("product", 0), CH // 2 + 1)
            nc.vector.tensor_copy(u_tok, ps[:, 0, :]).then_inc(ev("ctx_out"), 1)
    clear(nc, ev)
    A.at = keep


def complex_product(ops, eng, c, out, a, b, t, neg_im=False, done=None):
    c.step(ops.tensor_tensor(t[0], a[0], b[0], ALU.mult))
    c.step(ops.tensor_tensor(t[1], a[1], b[1], ALU.mult))
    c.settle(eng)
    c.step(ops.tensor_tensor(out[0], t[0], t[1], ALU.subtract))
    c.settle(eng)
    c.step(ops.tensor_tensor(t[0], a[0], b[1], ALU.mult))
    c.step(ops.tensor_tensor(t[1], a[1], b[0], ALU.mult))
    c.settle(eng)
    if neg_im:
        last = ops.scalar_tensor_tensor(out=out[1], in0=t[0], scalar=-1.0, in1=t[1], op0=ALU.mult, op1=ALU.subtract)
    else:
        last = ops.tensor_tensor(out[1], t[0], t[1], ALU.add)
    if done is not None:
        last.then_inc(done, 1)
    else:
        c.step(last)
        c.settle(eng)


def stage_s5_tables(nc, M, ins):
    A, ps = M.arena, M.ps
    S = M.s5 = Memory()
    two = lambda *s: (A.take(*s), A.take(*s))
    S.in_table = two(CH, G)
    S.tap_table = two(2 * CH - 1, G)
    S.out_table = two(CH, G)
    S.sup_pow = two(SUP, G)
    S.chunk = two(G)
    S.sup = two(G)
    S.b = two(G, GC)
    S.c = two(G, GC)
    S.h0 = two(G)
    S.d = A.take(G, parts=GC)
    S.final = A.take(2, G)
    keep = A.at
    par = A.take(3, G)
    b_raw = two(G, GC)
    pw = two(CH + 1, G)
    lam, lim, ldt = (par[:, n, :] for n in range(3))
    dt, are, aim, mag, red, k1, den, q0, q1 = (A.take(G) for _ in range(9))
    sin, cos = A.take(G), A.take(G)
    power = A.take(G).bitcast(mybir.dt.int32)
    t = (A.take(G * SUP), A.take(G * SUP))
    with ExitStack() as ctx:
        ev = Events(nc, ctx, "s5t")
        block = ctx.enter_context(nc.Block())

        @block.sync
        def _(sp):
            for v, n in ((par, "ssm_par"), (b_raw[0], "ssm_b_re"), (b_raw[1], "ssm_b_im"), (S.c[0], "ssm_c_re"),
                         (S.c[1], "ssm_c_im"), (S.h0[0], "ssm_h_re"), (S.h0[1], "ssm_h_im"), (S.d, "ssm_d")):
                sp.dma_start(v, ins[n]).then_inc(ev("in"), 16)

        @block.vector
        def _(dve):
            c = Chain(ev("dve"))
            ts, tt, stt = nc.vector.tensor_scalar, nc.vector.tensor_tensor, nc.vector.scalar_tensor_tensor

            def op(ins_):
                c.step(ins_)
                c.settle(dve)

            def horner(v, x, coefficients):
                op(ts(v, x, coefficients[0], coefficients[1], ALU.mult, ALU.add))
                for a in coefficients[2:]:
                    op(tt(v, v, x, ALU.mult))
                    op(ts(v, v, a, None, ALU.add))

            def whole(v, x, scale):
                op(ts(v, x, scale, 12582912.0, ALU.mult, ALU.add))
                op(ts(v, v, 12582912.0, None, ALU.subtract))
            f32 = lambda x: float(np.float32(x))

            def exponential(v, x):
                whole(q0, x, 1.0 / math.log(2.0))
                op(ts(q0, q0, -126.0, 127.0, ALU.max, ALU.min))
                op(stt(out=q1, in0=q0, scalar=-0.693359375, in1=x, op0=ALU.mult, op1=ALU.add))
                op(stt(out=q1, in0=q0, scalar=2.12194440e-4, in1=q1, op0=ALU.mult, op1=ALU.add))
                horner(v, q1, [1 / math.factorial(n) for n in range(8, -1, -1)])
                op(ts(q0, q0, 127.0, None, ALU.add))
                op(ts(power, q0, 8388608.0, None, ALU.mult))
                op(tt(v, v, power.bitcast(F32), ALU.mult))
            dve.wait_ge(ev("in"), 8 * 16)
            exponential(dt, ldt)
            op(tt(aim, lim, dt, ALU.mult))
            op(tt(are, lam, dt, ALU.mult))
            exponential(mag, are)
            whole(q0, aim, 1.0 / (2 * math.pi))
            op(stt(out=red, in0=q0, scalar=-6.28125, in1=aim, op0=ALU.mult, op1=ALU.add))
            op(stt(out=red, in0=q0, scalar=-f32(2 * math.pi - 6.28125), in1=red, op0=ALU.mult, op1=ALU.add))
            op(stt(out=red, in0=q0, scalar=-f32(2 * math.pi - 6.28125 - f32(2 * math.pi - 6.28125)), in1=red,
                   op0=ALU.mult, op1=ALU.add))
            op(ts(red, red, 0.25, None, ALU.mult))
            op(tt(k1, red, red, ALU.mult))
            horner(sin, k1, [(-1) ** n / math.factorial(2 * n + 1) for n in range(5, -1, -1)])
            op(tt(sin, sin, red, ALU.mult))
            horner(cos, k1, [(-1) ** n / math.factorial(2 * n) for n in range(6, -1, -1)])
            for _ in range(2):
                op(tt(cos, cos, sin, ALU.mult))
                op(tt(q0, sin, sin, ALU.mult))
                op(ts(sin, cos, 2.0, None, ALU.mult))
                op(ts(cos, q0, -2.0, 1.0, ALU.mult, ALU.add))
            op(nc.vector.memset(pw[0][:, 0, :], 1.0))
            op(nc.vector.memset(pw[1][:, 0, :], 0.0))
            op(nc.vector.tensor_tensor(pw[0][:, 1, :], mag, cos, ALU.mult))
            op(nc.vector.tensor_tensor(pw[1][:, 1, :], mag, sin, ALU.mult))

            def powers(tab, known, upto):
                n = upto - known
                sc = [v[:, 0:n * G].rearrange("p (n g) -> p n g", n=n) for v in t]
                complex_product(nc.vector, dve, c, [v[:, known + 1:upto + 1, :] for v in tab], [v[:, 1:n + 1, :] for v in tab],
                                [v[:, known:known + 1, :].broadcast_to([P, n, G]) for v in tab], sc)
            powers(pw, 1, 2)
            powers(pw, 2, 4)
            powers(pw, 4, 8)
            for n in range(2):
                op(nc.vector.tensor_copy(S.chunk[n], pw[n][:, 8, :]))
                op(nc.vector.memset(S.sup_pow[n][:, 0, :], 1.0 - n))
                op(nc.vector.tensor_copy(S.sup_pow[n][:, 1, :], pw[n][:, 8, :]))
            powers(S.sup_pow, 1, 2)
            powers(S.sup_pow, 2, 4)
            powers(S.sup_pow, 4, 8)
            powers(S.sup_pow, 8, 15)
            sc = [v[:, 0:G] for v in t]
            complex_product(nc.vector, dve, c, S.sup, [v[:, 15, :] for v in S.sup_pow], S.chunk, sc)
            fwd, bwd = slice(0, 64), slice(64, P)
            for n in range(2):
                op(nc.vector.tensor_copy(S.in_table[n][fwd], pw[n][fwd, 7::-1, :]))
                op(nc.vector.tensor_copy(S.in_table[n][bwd], pw[n][bwd, 0:8, :]))
                op(nc.vector.memset(S.tap_table[n], 0.0))
                op(nc.vector.tensor_copy(S.tap_table[n][fwd, 7:15, :], pw[n][fwd, 0:8, :]))
                op(nc.vector.tensor_copy(S.tap_table[n][bwd, 0:8, :], pw[n][bwd, 7::-1, :]))
                op(nc.vector.tensor_copy(S.out_table[n][fwd], pw[n][fwd, 1:9, :]))
                op(nc.vector.tensor_copy(S.out_table[n][bwd], pw[n][bwd, 8:0:-1, :]))
            op(nc.vector.tensor_tensor(den, lam, lam, ALU.mult))
            op(nc.vector.tensor_tensor(q0, lim, lim, ALU.mult))
            op(nc.vector.tensor_tensor(den, den, q0, ALU.add))
            op(nc.vector.reciprocal(den, den))
            op(nc.vector.tensor_tensor(cos, lam, den, ALU.mult))
            op(nc.vector.tensor_tensor(sin, lim, den, ALU.mult))
            op(nc.vector.tensor_scalar(sin, sin, -1.0, None, ALU.mult))
            op(nc.vector.tensor_scalar(q0, pw[0][:, 1, :], 1.0, None, ALU.subtract))
            complex_product(nc.vector, dve, c, (k1, red), (q0, pw[1][:, 1, :]), (cos, sin), sc)
            sc = [v[:, 0:G * GC].rearrange("p (g c) -> p g c", g=G) for v in t]
            complex_product(nc.vector, dve, c, S.b, b_raw, [v.unsqueeze(2).broadcast_to([P, G, GC]) for v in (k1, red)], sc)
    clear(nc, ev)
    A.at = keep


def stage_s5(nc, M, ins, outs):
    A, ps, S = M.arena, M.ps, M.s5
    M.y_lat = A.take(CH, DS)
    keep = A.at
    y_ctx = A.take(CH, P, parts=CC)
    two = lambda *s: (A.take(*s), A.take(*s))
    bst = two(GB, GC)
    h = two(GB, CH, GC)
    f = two(GB, 2 * CH - 1, GC)
    gout = two(GB, CH, GC)
    wx = A.take(GB, 2, P)
    strip = A.take(GB, 2 * CH - 1, GC, parts=GC)
    toe = A.take(GB, P)
    uf = A.take(GB, NC_)
    xs = A.take(2, GB, NSUP, SUP)
    e = A.take(2, GB, NSUP)
    sn = A.take(2, GB, NC_)
    tv = two(GB * NC_)
    tg = two(GB // 2 * (2 * CH - 1) * GC)
    ta, tb = A.take(2, GB, NSUP), A.take(2, GB, NSUP)
    dd = A.take(GB, GC, parts=GC)
    fwd, bwd = slice(0, 64), slice(64, P)
    with ExitStack() as ctx:
        ev = Events(nc, ctx, "s5")
        block = ctx.enter_context(nc.Block())

        @block.sync
        def _(sp):
            with sp.Fori(0, NBATCH) as i:
                sp.wait_ge(ev("strip"), i + 1)
                for s in range(CH):
                    sp.dma_start(toe[s * GC:(s + 1) * GC, :, :].rearrange("p g (t c) -> p g t c", t=CH),
                                 strip[:, :, 7 - s:15 - s, :]).then_inc(ev("toeplitz"), 16)
                sp.wait_ge(ev("y_ctx"), i * 2 + 2)
                sp.dma_start(ins["y_bounce"].rearrange("(c t) n -> c t n", t=CH)[:, :, ds(i * P, P)], y_ctx).then_inc(ev("ctx_sent"), 16)
            sp.wait_ge(ev("ctx_sent"), NBATCH * 16)
            sp.wait_ge(ev("final"), NBATCH)
            sp.dma_start(outs["ssm"], S.final).then_inc(ev("out"), 16)
            sp.wait_ge(ev("out"), 16)

        @block.gpsimd
        def _(pool):
            HG = GB // 2
            nc.gpsimd.memset(tg[0][:, 0:1], 0.0).then_inc(ev("begun"), 1)
            def batch(i):
                pool.wait_ge(ev("begun"), 1)
                need(pool, ev("tap_bank"), i * 4)
                for half in range(2):
                    gs = ds(i * GB + half * HG, HG)
                    shape = [P, HG, 2 * CH - 1, GC]
                    b4 = [v[:, gs, :].unsqueeze(2).broadcast_to(shape) for v in S.c]
                    p4 = [v[:, :, gs].rearrange("p m g -> p g m").unsqueeze(3).broadcast_to(shape) for v in S.tap_table]
                    fh = [v[:, half * HG:(half + 1) * HG] for v in f]
                    sc = [v.rearrange("p (g m c) -> p g m c", g=HG, c=GC) for v in tg]
                    mult = lambda o, x, y: nc.gpsimd.tensor_tensor(o, x, y, ALU.mult)
                    mult(fh[0], b4[0], p4[0])
                    mult(fh[1], b4[0], p4[1])
                    mult(sc[0], b4[1], p4[1])
                    mult(sc[1], b4[1], p4[0]).then_inc(ev("f_products", half), 1)
                    pool.wait_ge(ev("f_products", half), i + 1)
                    nc.gpsimd.tensor_tensor(fh[0], fh[0], sc[0], ALU.subtract)
                    nc.gpsimd.tensor_tensor(fh[1], fh[1], sc[1], ALU.add).then_inc(ev("f_sums", half), 1)
                    pool.wait_ge(ev("f_sums", half), i + 1)
                    nc.gpsimd.tensor_tensor(fh[1], M.zero.unsqueeze(2).unsqueeze(3).broadcast_to(shape),
                                            fh[1], ALU.subtract).then_inc(ev("f"), 1)
            rounds(pool, NBATCH, batch)

        @block.scalar
        def _(act):
            def batch(i):
                gs = ds(i * GB, GB)
                need(act, ev("y_bank"), i * 4)
                nc.scalar.activation(uf, M.u[:, gs, :], ACT.Copy).then_inc(ev("staged"), 1)
                for n in range(2):
                    need(act, ev("tap_bank"), i * 4)
                    nc.scalar.activation(bst[n], S.b[n][:, gs, :], ACT.Copy).then_inc(ev("staged"), 1)
                for b in range(4):
                    act.wait_ge(ev("h_turned"), i * 4 + b + 1)
                    nc.scalar.activation(wx[:, 2 * b:2 * b + 2].rearrange("p g n l -> p (g n l)"), ps[:, b, :],
                                         ACT.Copy).then_inc(ev("wx"), 1)
                act.wait_ge(ev("sprev"), i * 2 + 2)
                xn = xs.rearrange("p n g s i -> p (n g) (s i)")
                so = sn.rearrange("p n g c -> p (n g) c")
                nc.scalar.activation(so[fwd], xn[fwd], ACT.Copy).then_inc(ev("natural"), 1)
                nc.scalar.activation(so[bwd, :, 0:LC], xn[bwd, :, 0:LC][:, :, ::-1], ACT.Copy).then_inc(ev("natural"), 1)
                nc.scalar.activation(so[bwd, :, LC:NC_], xn[bwd, :, LC:NC_][:, :, ::-1], ACT.Copy).then_inc(ev("natural"), 1)
                need(act, ev("ctx_sent"), i * 16)
                for b in range(2):
                    act.wait_ge(ev("y_bank"), i * 4 + 2 * b + 2)
                    nc.scalar.activation(y_ctx[:, :, 64 * b:64 * b + 64].rearrange("p t (g c) -> p g t c", g=4),
                                         ps[0:CC, 2 * b + 1, :].rearrange("p (g t c) -> p g t c", g=4, t=CH),
                                         ACT.Copy).then_inc(ev("y_ctx"), 1)
            rounds(act, NBATCH, batch)

        @block.tensor
        def _(pe):
            def batch(i):
                pe.wait_ge(ev("h"), i + 1)
                need(pe, ev("y_ctx"), i * 2)
                need(pe, ev("y_lat"), i * 2)
                for b in range(4):
                    for j in range(4):
                        last = nc.tensor.transpose(ps[:, b, j * P:(j + 1) * P],
                                                   h[j % 2][:, 2 * b + j // 2].rearrange("p s c -> p (s c)"), M.ident)
                    last.then_inc(ev("h_turned"), 1)
                pe.wait_ge(ev("f"), i * 2 + 2)
                pe.wait_ge(ev("staged"), i * 3 + 3)
                for b in range(4):
                    if b == 0:
                        need(pe, ev("x_read"), i * 6)
                        need(pe, ev("strip_read"), i * 4)
                    for j in range(2):
                        g = 2 * b + j
                        o = ps[0:GC, 4 + b, j * 256:j * 256 + 240]
                        for n in range(2):
                            last = nc.tensor.matmul(o, bst[n][:, g, :], f[n][:, g].rearrange("p m c -> p (m c)"),
                                                    start=(n == 0), stop=(n == 1))
                    last.then_inc(ev("tap_bank"), 1)
                pe.wait_ge(ev("wx"), i * 4 + 4)
                pe.wait_ge(ev("strip_read"), i * 4 + 4)
                for n in range(2):
                    for b in range(3):
                        for g in range(3 * b, min(3 * b + 3, GB)):
                            o = slice(g % 3 * NC_, (g % 3 + 1) * NC_)
                            nc.tensor.matmul(ps[fwd, 4 * n + b, o], wx[:, g, n, fwd], uf[:, g, :], start=True, stop=True)
                            mid = o.start + LC
                            nc.tensor.matmul(ps[bwd, 4 * n + b, o.start:mid], wx[:, g, n, bwd], uf[:, g, 0:LC][:, ::-1],
                                             start=True, stop=True)
                            last = nc.tensor.matmul(ps[bwd, 4 * n + b, mid:o.stop], wx[:, g, n, bwd],
                                                    uf[:, g, LC:NC_][:, ::-1], start=True, stop=True)
                        last.then_inc(ev("x_bank"), 1)
                pe.wait_ge(ev("x_read"), i * 6 + 6)
                pe.wait_ge(ev("natural"), i * 3 + 3)
                pe.wait_ge(ev("toeplitz"), i * (16 * CH) + 16 * CH)
                pe.wait_ge(ev("gout"), i + 1)
                for b in range(2):
                    for rows, bank in ((slice(0, LC), 2 * b), (slice(LC, NC_), 2 * b + 1)):
                        m = rows.stop - rows.start
                        for j in range(4):
                            g = 4 * b + j
                            o = ps[0:m, bank, j * P:(j + 1) * P]
                            nc.tensor.matmul(o, uf[:, g, rows], toe[:, g, :], start=True, stop=False)
                            nc.tensor.matmul(o, sn[:, 0, g, rows], gout[0][:, g].rearrange("p t c -> p (t c)"), start=False, stop=False)
                            last = nc.tensor.matmul(o, sn[:, 1, g, rows], gout[1][:, g].rearrange("p t c -> p (t c)"), start=False, stop=True)
                        last.then_inc(ev("y_bank"), 1)
            rounds(pe, NBATCH, batch)

        @block.vector
        def _(dve):
            K = S5_DVE_STEPS
            def batch(i):
                c = Chain(ev("dve"), i * K)
                gs = ds(i * GB, GB)

                def table(tab, n):
                    return [v[:, :, gs].rearrange("p m g -> p g m").unsqueeze(3).broadcast_to([P, GB, n, GC]) for v in tab]

                def mat(m, n):
                    return [v[:, gs, :].unsqueeze(2).broadcast_to([P, GB, n, GC]) for v in m]
                sc = [v[:, 0:GB * CH * GC].rearrange("p (g s c) -> p g s c", g=GB, s=CH) for v in tv]
                need(dve, ev("h_turned"), i * 4)
                complex_product(nc.vector, dve, c, h, mat(S.b, CH), table(S.in_table, CH), sc, done=ev("h"))
                dve.wait_ge(ev("h"), i + 1)
                need(dve, ev("y_bank"), i * 4)
                complex_product(nc.vector, dve, c, gout, mat(S.c, CH), table(S.out_table, CH), sc, neg_im=True,
                                done=ev("gout"))
                dve.wait_ge(ev("gout"), i + 1)
                need(dve, ev("toeplitz"), i * (16 * CH))
                c.step(nc.vector.tensor_tensor(dd, M.ident[0:GC, 0:GC].unsqueeze(1).broadcast_to([GC, GB, GC]),
                                               S.d[:, gs].unsqueeze(2).broadcast_to([GC, GB, GC]), ALU.mult))
                for b in range(4):
                    dve.wait_ge(ev("tap_bank"), i * 4 + b + 1)
                    src = ps[0:GC, 4 + b, :].rearrange("p (g x) -> p g x", g=2)[:, :, 0:240]
                    nc.vector.tensor_copy(strip[:, 2 * b:2 * b + 2].rearrange("p g m c -> p g (m c)"), src).then_inc(ev("strip_read"), 1)
                dve.wait_ge(ev("strip_read"), i * 4 + 4)
                c.settle(dve)
                nc.vector.tensor_tensor(strip[:, :, 7, :], strip[:, :, 7, :], dd, ALU.add).then_inc(ev("strip"), 1)
                need(dve, ev("natural"), i * 3)
                for n in range(2):
                    for b in range(3):
                        g0, g1 = 3 * b, min(3 * b + 3, GB)
                        dve.wait_ge(ev("x_bank"), i * 6 + 3 * n + b + 1)
                        nc.vector.tensor_copy(xs[:, n, g0:g1].rearrange("p g s i -> p (g s i)"),
                                              ps[:, 4 * n + b, 0:(g1 - g0) * NC_]).then_inc(ev("x_read"), 1)
                dve.wait_ge(ev("x_read"), i * 6 + 6)
                rot = lambda v, n: v[:, gs].unsqueeze(1).unsqueeze(3).broadcast_to([P, 2, GB, n])

                def advance(dst, src, lam, n):
                    a, b = ta[:, :, :, 0:n], tb[:, :, :, 0:n]
                    c.step(nc.vector.tensor_tensor(a, rot(lam[0], n), src, ALU.mult))
                    c.step(nc.vector.tensor_tensor(b, rot(lam[1], n), src, ALU.mult))
                    c.settle(dve)
                    c.step(nc.vector.tensor_tensor(dst, dst, a, ALU.add))
                    c.settle(dve)
                    c.step(nc.vector.tensor_tensor(dst[:, 0], dst[:, 0], b[:, 1], ALU.subtract))
                    c.step(nc.vector.tensor_tensor(dst[:, 1], dst[:, 1], b[:, 0], ALU.add))
                    c.settle(dve)
                for k in range(1, SUP):
                    advance(xs[:, :, :, :, k], xs[:, :, :, :, k - 1], S.chunk, NSUP)
                c.step(nc.vector.memset(e, 0.0))
                c.settle(dve)
                for n in range(2):
                    c.step(nc.vector.tensor_copy(e[:, n, :, 0], S.h0[n][:, gs]))
                c.step(nc.vector.tensor_copy(e[:, :, :, 1:NSUP - 1], xs[:, :, :, 0:NSUP - 2, SUP - 1]))
                nc.vector.tensor_copy(S.final[:, :, gs], xs[:, :, :, NSUP - 1, SUP - 1]).then_inc(ev("final"), 1)
                c.settle(dve)
                for j in range(NSUP - 2):
                    advance(e[:, :, :, j + 1:j + 2], e[:, :, :, j:j + 1], S.sup, 1)
                pos = lambda n: S.sup_pow[n][:, :, gs].rearrange("p i g -> p g i").unsqueeze(2).broadcast_to([P, GB, NSUP, SUP])
                est = lambda n: e[:, n].unsqueeze(3).broadcast_to([P, GB, NSUP, SUP])
                sc3 = [v.rearrange("p (g s i) -> p g s i", g=GB, s=NSUP) for v in tv]
                for n, (x0, x1, sign) in enumerate(((0, 0, ALU.subtract), (0, 1, ALU.add))):
                    c.step(nc.vector.tensor_tensor(sc3[0], pos(0), est(n), ALU.mult))
                    c.step(nc.vector.tensor_tensor(sc3[1], pos(1), est(1 - n), ALU.mult))
                    c.settle(dve)
                    c.step(nc.vector.tensor_tensor(sc3[0], sc3[0], sc3[1], sign))
                    c.settle(dve)
                    c.step(nc.vector.tensor_tensor(sc3[0][:, :, :, 1:SUP], sc3[0][:, :, :, 1:SUP],
                                                   xs[:, n, :, :, 0:SUP - 1], ALU.add))
                    c.settle(dve)
                    nc.vector.tensor_copy(xs[:, n], sc3[0]).then_inc(ev("sprev"), 1)
                    dve.wait_ge(ev("sprev"), i * 2 + n + 1)
                for b in range(2):
                    dve.wait_ge(ev("y_bank"), i * 4 + 2 * b + 1)
                    nc.vector.tensor_copy(M.y_lat[:, :, ds(i * P + 64 * b, 64)].rearrange("p t (g c) -> p g t c", g=4),
                                          ps[:, 2 * b, :].rearrange("p (g t c) -> p g t c", g=4, t=CH)).then_inc(ev("y_lat"), 1)
                assert c.n == K or K == 0, c.n
            rounds(dve, NBATCH, batch)

    clear(nc, ev)
    A.at = keep


S5_DVE_STEPS = 133


def stage_glu(nc, M, ins):
    A, ps = M.arena, M.ps
    keep = A.at
    K4 = DS // P
    wst = A.take(K4, DS)
    whi, wlo = A.take(K4, DS, dt=BF16), A.take(K4, DS, dt=BF16)
    bias = A.take(K4)
    y_nat = A.take(DS)
    yt = A.take(K4, T)
    g1 = A.take(K4, T)
    yhi, ylo = A.take(K4, T, dt=BF16), A.take(K4, T, dt=BF16)
    with ExitStack() as ctx:
        ev = Events(nc, ctx, "glu")
        block = ctx.enter_context(nc.Block())

        @block.sync
        def _(sp):
            sp.dma_start(wst, ins["w_glu"]).then_inc(ev("w"), 16)
            sp.dma_start(bias, ins["b_glu"]).then_inc(ev("w"), 16)
            sp.dma_start(y_nat, ins["y_bounce"]).then_inc(ev("ctx"), 16)

        @block.tensor
        def _(pe):
            for t in range(CH + 1):
                if t >= 2:
                    pe.wait_ge(ev("turned_read"), t - 1)
                if t == CH:
                    pe.wait_ge(ev("ctx"), 16)
                for k in range(K4):
                    src = M.y_lat[:, t, k * P:(k + 1) * P] if t < CH else y_nat[:, k * P:(k + 1) * P]
                    last = nc.tensor.transpose(ps[:, t % 2, k * P:(k + 1) * P], src, M.ident)
                last.then_inc(ev("turned"), 1)
            pe.wait_ge(ev("turned_read"), CH + 1)
            pe.wait_ge(ev("w_lo"), 1)
            pe.wait_ge(ev("y_lo"), K4)
            for o in range(K4):
                if o >= 2:
                    pe.wait_ge(ev("tanh_z"), o - 1)
                for g in range(TG):
                    for k in range(K4):
                        cols = slice(g * TW, (g + 1) * TW)
                        last = split_mm(nc, ps[:, 3 * (o % 2) + g, 0:TW], whi[:, k, o * P:(o + 1) * P],
                                        wlo[:, k, o * P:(o + 1) * P], yhi[:, k, cols], ylo[:, k, cols], k == 0, k == K4 - 1)
                last.then_inc(ev("z"), 1)

        @block.vector
        def _(dve):
            for t in range(CH + 1):
                dve.wait_ge(ev("turned"), t + 1)
                src = ps[:, t % 2, :].rearrange("p (k c) -> p k c", k=K4)
                dst = yt[:, :, t:NLAT:CH] if t < CH else yt[:, :, NLAT:T]
                nc.vector.tensor_copy(dst, src).then_inc(ev("turned_read"), 1)
            dve.wait_ge(ev("w"), 32)
            nc.vector.tensor_scalar(bias, bias, 0.5, None, ALU.mult).then_inc(ev("bias"), 1)
            c = Chain(ev("dve"))
            for k in range(K4):
                dve.wait_ge(ev("square"), k + 1)
                c.step(nc.vector.tensor_scalar(g1[:, k], g1[:, k], 0.044715, 1.0, ALU.mult, ALU.add))
                c.settle(dve)
                nc.vector.tensor_tensor(g1[:, k], g1[:, k], yt[:, k], ALU.mult).then_inc(ev("cubic"), 1)
            for k in range(K4):
                dve.wait_ge(ev("tanh"), k + 1)
                c.step(nc.vector.scalar_tensor_tensor(out=g1[:, k], in0=g1[:, k], scalar=1.0, in1=yt[:, k],
                                                      op0=ALU.add, op1=ALU.mult))
                c.settle(dve)
                nc.vector.tensor_scalar(yt[:, k], g1[:, k], 0.5, None, ALU.mult).then_inc(ev("gelu"), 1)
            for o in range(K4):
                dve.wait_ge(ev("tanh_z"), o + 1)
                c.step(nc.vector.tensor_scalar(g1[:, o], g1[:, o], 0.5, 0.5, ALU.mult, ALU.add))
                c.settle(dve)
                nc.vector.tensor_tensor(g1[:, o], g1[:, o], yt[:, o], ALU.mult).then_inc(ev("out"), 1)

        @block.scalar
        def _(act):
            act.wait_ge(ev("w"), 32)
            nc.scalar.activation(whi, wst, ACT.Copy).then_inc(ev("w_hi"), 1)
            act.wait_ge(ev("turned_read"), CH + 1)
            for k in range(K4):
                nc.scalar.activation(g1[:, k], yt[:, k], ACT.Square).then_inc(ev("square"), 1)
            for k in range(K4):
                act.wait_ge(ev("cubic"), k + 1)
                nc.scalar.activation(g1[:, k], g1[:, k], ACT.Tanh, scale=math.sqrt(2 / math.pi)).then_inc(ev("tanh"), 1)
            for k in range(K4):
                act.wait_ge(ev("gelu"), k + 1)
                nc.scalar.activation(yhi[:, k], yt[:, k], ACT.Copy).then_inc(ev("y_hi"), 1)
            act.wait_ge(ev("bias"), 1)
            for o in range(K4):
                act.wait_ge(ev("z"), o + 1)
                nc.scalar.activation(g1[:, o].rearrange("p (g c) -> p g c", g=TG), ps[:, 3 * (o % 2):3 * (o % 2) + 3, 0:TW],
                                     ACT.Tanh, bias=bias[:, o:o + 1], scale=0.5).then_inc(ev("tanh_z"), 1)
                act.wait_ge(ev("out"), o + 1)
                nc.scalar.activation(M.ys_hi[:, o], g1[:, o], ACT.Copy).then_inc(ev("out_hi"), 1)

        @block.gpsimd
        def _(pool):
            pool.wait_ge(ev("w_hi"), 1)
            nc.gpsimd.tensor_tensor(wlo, wst, whi, ALU.subtract).then_inc(ev("w_lo"), 1)
            for k in range(K4):
                pool.wait_ge(ev("y_hi"), k + 1)
                nc.gpsimd.tensor_tensor(ylo[:, k], yt[:, k], yhi[:, k], ALU.subtract).then_inc(ev("y_lo"), 1)
            for o in range(K4):
                pool.wait_ge(ev("out_hi"), o + 1)
                nc.gpsimd.tensor_tensor(M.ys_lo[:, o], g1[:, o], M.ys_hi[:, o], ALU.subtract).then_inc(ev("out_lo"), 1)
    clear(nc, ev)
    A.at = keep


def wide(ps, bank):
    return ps[:, bank:bank + TG, 0:TW]


def stage_lora(nc, M, ins):
    A, ps = M.arena, M.ps
    keep = A.at
    wst = A.take(KD, 3, P)
    whi, wlo = A.take(KD, 3, P, dt=BF16), A.take(KD, 3, P, dt=BF16)
    f = A.take(3, T)
    with ExitStack() as ctx:
        ev = Events(nc, ctx, "lora")
        block = ctx.enter_context(nc.Block())

        @block.sync
        def _(sp):
            sp.dma_start(wst.rearrange("p k a n -> p k (a n)"), ins["w_in"][:, :, OFF_WD:OFF_U]).then_inc(ev("w"), 16)

        @block.scalar
        def _(act):
            act.wait_ge(ev("w"), 16)
            nc.scalar.activation(whi, wst, ACT.Copy).then_inc(ev("w_hi"), 1)
            for n, (func, scale) in enumerate(((ACT.Tanh, 1.0), (ACT.Copy, 1.0), (ACT.Tanh, 0.5))):
                act.wait_ge(ev("z"), n + 1)
                nc.scalar.activation(f[:, n].rearrange("p (g c) -> p g c", g=TG), wide(ps, 3 * (n % 2)), func,
                                     scale=scale).then_inc(ev("f"), 1)
            for n in range(3):
                act.wait_ge(ev("f"), 3)
                if n == 2:
                    act.wait_ge(ev("sigmoid"), 1)
                nc.scalar.activation(M.lora_hi[:, n], f[:, n], ACT.Copy).then_inc(ev("hi"), 1)

        @block.gpsimd
        def _(pool):
            pool.wait_ge(ev("w_hi"), 1)
            nc.gpsimd.tensor_tensor(wlo, wst, whi, ALU.subtract).then_inc(ev("w_lo"), 1)
            for n in range(3):
                pool.wait_ge(ev("hi"), n + 1)
                nc.gpsimd.tensor_tensor(M.lora_lo[:, n], f[:, n], M.lora_hi[:, n], ALU.subtract).then_inc(ev("lo"), 1)

        @block.vector
        def _(dve):
            dve.wait_ge(ev("f"), 3)
            nc.vector.tensor_scalar(f[:, 2], f[:, 2], 0.5, 0.5, ALU.mult, ALU.add).then_inc(ev("sigmoid"), 1)

        @block.tensor
        def _(pe):
            pe.wait_ge(ev("w_lo"), 1)
            for n in range(3):
                if n == 2:
                    pe.wait_ge(ev("f"), 1)
                for g in range(TG):
                    cols = slice(g * TW, (g + 1) * TW)
                    for k in range(KD):
                        last = split_mm(nc, ps[:, 3 * (n % 2) + g, 0:TW], whi[:, k, n], wlo[:, k, n],
                                        M.hi[:, k, cols], M.lo[:, k, cols], k == 0, k == KD - 1)
                last.then_inc(ev("z"), 1)
    clear(nc, ev)
    A.at = keep


def stage_prepare(nc, M, ins, ct):
    A, ps, R = M.arena, M.ps, M.rwkv
    keep = A.at
    wst = A.take(KD, P)
    whi = [A.take(KD, P, dt=BF16) for _ in range(2)]
    wlo = [A.take(KD, P, dt=BF16) for _ in range(2)]
    up = A.take(3, P)
    r, k, kn, a, lw, c_, e, t = (A.take(T) for _ in range(8))
    m, tot = A.take(NB), A.take(NB)
    hb = A.take(4)
    omka = A.take(1)
    par = R.par
    tiles = lambda v: v.rearrange("p (b t) -> p b t", b=NB)
    three = lambda v: v.rearrange("p (g c) -> p g c", g=TG)
    with ExitStack() as ctx:
        ev = Events(nc, ctx, "prep")
        block = ctx.enter_context(nc.Block())
        tt, ts, stt = nc.vector.tensor_tensor, nc.vector.tensor_scalar, nc.vector.scalar_tensor_tensor

        @block.sync
        def _(sp):
            sp.dma_start(par, ins["par"][ds(ct, 1)].squeeze(0)).then_inc(ev("par"), 16)
            sp.dma_start(up, ins["up"][ds(ct, 1)].squeeze(0)).then_inc(ev("up"), 16)
            for n, off in enumerate((OFF_R, OFF_K, OFF_V)):
                if n:
                    sp.wait_ge(ev("w_lo"), n)
                sp.dma_start(wst, ins["w_in"][:, :, ds(ct * P + off, P)]).then_inc(ev("w"), 16)

        @block.gpsimd
        def _(pool):
            pool.wait_ge(ev("up_hi"), 1)
            nc.gpsimd.tensor_tensor(R.up_lo, up, R.up_hi, ALU.subtract).then_inc(ev("up_lo"), 1)
            for n in range(3):
                pool.wait_ge(ev("w_hi"), n + 1)
                nc.gpsimd.tensor_tensor(wlo[n % 2], wst, whi[n % 2], ALU.subtract).then_inc(ev("w_lo"), 1)

        @block.tensor
        def _(pe):
            for n in range(2):
                pe.wait_ge(ev("w_lo"), n + 1)
                for g in range(TG):
                    cols = slice(g * TW, (g + 1) * TW)
                    for q in range(KD):
                        last = split_mm(nc, ps[:, 3 * n + g, 0:TW], whi[n][:, q], wlo[n][:, q],
                                        M.hi[:, q, cols], M.lo[:, q, cols], q == 0, q == KD - 1)
                last.then_inc(ev("rk"), 1)
            pe.wait_ge(ev("w_lo"), 3)
            for b in range(NB):
                if b == 8:
                    pe.wait_ge(ev("r"), 1)
                bank = (6, 7, 0)[b // 4]
                for q in range(KD):
                    cols = slice(b * P, (b + 1) * P)
                    last = split_mm(nc, ps[:, bank, b % 4 * P:(b % 4 + 1) * P], M.hi[:, q, cols], M.lo[:, q, cols],
                                    whi[0][:, q], wlo[0][:, q], q == 0, q == KD - 1)
                if b % 4 == 3 or b == 8:
                    last.then_inc(ev("v_bank"), 1)
            pe.wait_ge(ev("square"), 1)
            pe.wait_ge(ev("k"), 1)
            for g in range(TG):
                last = nc.tensor.matmul(ps[:, 3 + g, 0:TW], M.head_ones, e[:, g * TW:(g + 1) * TW], start=True, stop=True)
            last.then_inc(ev("norm"), 1)
            pe.wait_ge(ev("rkr"), 1)
            pe.wait_ge(ev("v"), 3)
            for b in range(NB):
                last = nc.tensor.matmul(ps[:, 6, 2 * b:2 * b + 2], c_[:, b * P:(b + 1) * P], M.head_ind, start=True, stop=True)
            last.then_inc(ev("bonus"), 1)
            pe.wait_ge(ev("up_lo"), 1)
            for d in range(2):
                rows = slice(64 * d, 64 * d + 64)
                for n in range(2):
                    if d == 0 and n == 1:
                        pe.wait_ge(ev("sqrt"), 1)
                    if d == 1:
                        pe.wait_ge(ev("tanh"), n + 1)
                    for g in range(TG):
                        cols = slice(g * TW, (g + 1) * TW)
                        last = split_mm(nc, ps[:, 3 * n + g, 0:TW], R.up_hi[rows, n], R.up_lo[rows, n],
                                        M.lora_hi[rows, n, cols], M.lora_lo[rows, n, cols], True, True)
                    last.then_inc(ev("lora"), 1)

        @block.scalar
        def _(act):
            act.wait_ge(ev("up"), 16)
            nc.scalar.activation(R.up_hi, up, ACT.Copy).then_inc(ev("up_hi"), 1)
            for n in range(3):
                act.wait_ge(ev("w"), 16 * n + 16)
                if n == 2:
                    act.wait_ge(ev("rk"), 1)
                nc.scalar.activation(whi[n % 2], wst, ACT.Copy).then_inc(ev("w_hi"), 1)
            act.wait_ge(ev("rk"), 1)
            nc.scalar.activation(three(r), wide(ps, 0), ACT.Copy).then_inc(ev("r"), 1)
            act.wait_ge(ev("kk"), 1)
            nc.scalar.activation(e, t, ACT.Square).then_inc(ev("square"), 1)
            for n, bank in enumerate((6, 7, 0)):
                act.wait_ge(ev("v_bank"), n + 1)
                w = 4 if n < 2 else 1
                nc.scalar.activation(R.v[:, 4 * n:4 * n + w, :].rearrange("p b c -> p (b c)"), ps[:, bank, 0:w * P],
                                     ACT.Copy).then_inc(ev("v"), 1)
            act.wait_ge(ev("norm"), 1)
            nc.scalar.activation(three(a), wide(ps, 3), ACT.Sqrt).then_inc(ev("sqrt"), 1)
            act.wait_ge(ev("bonus"), 1)
            nc.scalar.activation(R.bonus, ps[:, 6, 0:2 * NB], ACT.Copy).then_inc(ev("bonus_read"), 1)
            act.wait_ge(ev("half_bias"), 1)
            for d in range(2):
                if d == 1:
                    act.wait_ge(ev("x"), 4)
                else:
                    act.wait_ge(ev("kn"), 1)
                for n, v in enumerate((lw, a)):
                    act.wait_ge(ev("lora"), 2 * d + n + 1)
                    nc.scalar.activation(three(v), wide(ps, 3 * n), ACT.Tanh, bias=hb[:, 2 * n + d:2 * n + d + 1],
                                         scale=0.5).then_inc(ev("tanh"), 1)
                act.wait_ge(ev("sums"), d + 1)
                order = ((lw, 1.0), (c_, 1.0), (c_, -1.0)) if d == 0 else ((c_, -1.0), (lw, -1.0), (lw, 1.0))
                for n, (v, sign) in enumerate(order):
                    if n == 2:
                        act.wait_ge(ev("x"), 4 * d + 1)
                    nc.scalar.activation((e, t, e)[n], v, ACT.Exp, scale=sign).then_inc(ev("exp"), 1)
                nc.scalar.activation(R.pre[d] if d == 0 else R.post[d], m, ACT.Exp).then_inc(ev("edge"), 1)
                nc.scalar.activation(R.post[d] if d == 0 else R.pre[d], tot, ACT.Exp).then_inc(ev("edge"), 1)

        @block.vector
        def _(dve):
            c = Chain(ev("dve"))

            def op(ins_):
                c.step(ins_)
                c.settle(dve)
            dve.wait_ge(ev("par"), 16)
            op(ts(omka, par[:, 1:2], -1.0, 1.0, ALU.mult, ALU.add))
            ts(hb, par[:, 3:7], 0.5, None, ALU.mult).then_inc(ev("half_bias"), 1)
            dve.wait_ge(ev("rk"), 2)
            nc.vector.tensor_copy(three(k), wide(ps, 3)).then_inc(ev("k"), 1)
            dve.wait_ge(ev("k"), 1)
            ts(t, k, par[:, 0:1], None, ALU.mult).then_inc(ev("kk"), 1)
            dve.wait_ge(ev("r"), 1)
            stt(out=c_, in0=r, scalar=par[:, 2:3], in1=k, op0=ALU.mult, op1=ALU.mult).then_inc(ev("rkr"), 1)
            dve.wait_ge(ev("sqrt"), 1)
            op(ts(a, a, 1e-12, None, ALU.max))
            op(nc.vector.reciprocal(a, a))
            tt(kn, t, a, ALU.mult).then_inc(ev("kn"), 1)
            dve.wait_ge(ev("bonus"), 1)
            for d in range(2):
                x = R.x[d]
                dve.wait_ge(ev("tanh"), 2 * d + 2)
                c.step(ts(lw, lw, DECAY / 2, DECAY / 2, ALU.mult, ALU.add))
                c.step(ts(a, a, 0.5, 0.5, ALU.mult, ALU.add))
                c.settle(dve)
                if d == 1:
                    dve.wait_ge(ev("exp"), 3)
                    dve.wait_ge(ev("edge"), 2)
                for b in range(NB):
                    s = slice(b * P, (b + 1) * P)
                    c.step(nc.vector.tensor_tensor_scan(c_[:, s], M.one.broadcast_to([P, P]), lw[:, s], 0.0, ALU.mult, ALU.add))
                c.settle(dve)
                op(nc.vector.tensor_copy(m, tiles(c_)[:, :, 63]))
                op(tt(tiles(c_), tiles(c_), m.unsqueeze(2).broadcast_to([P, NB, P]), ALU.subtract))
                c.step(nc.vector.tensor_copy(tot, tiles(c_)[:, :, P - 1]))
                tt(lw, c_, lw, ALU.subtract).then_inc(ev("sums"), 1)
                dve.wait_ge(ev("sums"), d + 1)
                op(stt(out=x[:, :, 2, :], in0=tiles(kn), scalar=-1.0, in1=tiles(a), op0=ALU.mult, op1=ALU.mult))
                op(ts(x[:, :, 3, :], tiles(a), par[:, 1:2], omka, ALU.mult, ALU.add))
                op(tt(x[:, :, 3, :], x[:, :, 3, :], tiles(k), ALU.mult))
                for n, (src, v) in enumerate(((kn, e), (r, t))):
                    dve.wait_ge(ev("exp"), 3 * d + n + 1)
                    tt(x[:, :, n, :], tiles(src), tiles(v), ALU.mult).then_inc(ev("x"), 1)
                dve.wait_ge(ev("exp"), 3 * d + 3)
                for n in (2, 3):
                    tt(x[:, :, n, :], x[:, :, n, :], tiles(e), ALU.mult).then_inc(ev("x"), 1)
                dve.wait_ge(ev("edge"), 2 * d + 2)
                op(nc.vector.tensor_copy(R.step[d], R.post[d]))
                if d == 0:
                    op(tt(R.step[d][:, 0:LB - 1], R.post[d][:, 0:LB - 1], R.pre[d][:, 1:LB], ALU.mult))
                else:
                    op(tt(R.step[d][:, 1:LB], R.post[d][:, 1:LB], R.pre[d][:, 0:LB - 1], ALU.mult))
    clear(nc, ev)
    A.at = keep


def stage_chunks(nc, M, ins, outs, ct):
    A, ps, R = M.arena, M.ps, M.rwkv
    keep = A.at
    D2, H2 = range(2), range(2)
    st = [A.take(4, P) for _ in D2]
    vs = [A.take(P) for _ in D2]
    mt = [[A.take(4, P) for _ in H2] for _ in D2]
    tm = [A.take(3, P) for _ in D2]
    lo = [A.take(2, NLEV, 64) for _ in D2]
    xx = [A.take(2, 2, 64) for _ in D2]
    qs = [A.take(2, 64) for _ in D2]
    rs = [A.take(2, 64) for _ in D2]
    u = [A.take(2, 64) for _ in D2]
    p = [A.take(64) for _ in D2]
    pt = [A.take(64) for _ in D2]
    h0 = A.take(2, 64)
    fin = A.take(2, 64)
    half = [slice(0, 64), slice(64, P)]
    flat = lambda v: v.rearrange("p h c -> p (h c)")
    with ExitStack() as ctx:
        ev = Events(nc, ctx, "chunk")
        block = ctx.enter_context(nc.Block())

        def tiles_of(eng, body):
            body(0, (LB, LB))
            with eng.Fori(0, LB) as i:
                body(i + 1, (i, eng.snap(LB - 1 - i)))

        def first(eng):
            eng.wait_ge(ev("y_clear"), 1)

        @block.sync
        def _(sp):
            sp.dma_start(h0, ins["state"][ds(ct, 1)].squeeze(0)).then_inc(ev("h0"), 16)
            sp.wait_ge(ev("final"), 2)
            sp.dma_start(outs["rwkv"][ds(ct, 1)].squeeze(0), fin).then_inc(ev("out"), 16)
            sp.wait_ge(ev("out"), 16)

        @block.gpsimd
        def _(pool):
            nc.gpsimd.memset(R.y, 0.0).then_inc(ev("y_clear"), 1)
            for d in D2:
                nc.gpsimd.memset(p[d], 0.0).then_inc(ev("p_clear"), 1)

            def body(n, tile):
                for d in D2:
                    first(pool)
                    need(pool, ev("state", d), n)
                    nc.gpsimd.tensor_copy(st[d].rearrange("p m t -> p (m t)"),
                                          R.x[d][:, ds(tile[d], 1)].rearrange("p b m t -> p (b m t)")).then_inc(ev("st", d), 1)
                    nc.gpsimd.tensor_copy(vs[d], R.v[:, ds(tile[d], 1), :].rearrange("p b c -> p (b c)")).then_inc(ev("vs", d), 1)
                for d in D2:
                    first(pool)
                    pool.wait_ge(ev("turned_read", d), n + 1)
                    need(pool, ev("q_last", d), n)
                    nc.gpsimd.tensor_tensor(lo[d], tm[d][:, 2].rearrange("p (h c) -> p h c", h=2).unsqueeze(2)
                                            .broadcast_to([P, 2, NLEV, 64]),
                                            M.level_mask[:, d].unsqueeze(1).broadcast_to([P, 2, NLEV, 64]), ALU.mult)\
                        .then_inc(ev("lo", d), 1)
                    pool.wait_ge(ev("lo", d), n + 1)
                    need(pool, ev("u_first", d), n)
                    nc.gpsimd.tensor_tensor(xx[d][:, :, 1, :], lo[d][:, :, 0, :],
                                            M.ident64.unsqueeze(1).broadcast_to([P, 2, 64]), ALU.add).then_inc(ev("xt0", d), 1)
            tiles_of(pool, body)

        @block.tensor
        def _(pe):
            def blocks(bank, col, lhs, rhs):
                for b in range(2):
                    last = nc.tensor.matmul(ps[half[b], bank, col:col + 64], lhs[half[b]], rhs[half[b]], start=True, stop=True)
                return last

            def body(n, tile):
                for d in D2:
                    B = 4 * d
                    pe.wait_ge(ev("st", d), n + 1)
                    need(pe, ev("u_second_read", d), n)
                    need(pe, ev("p_read", d), n)
                    for j in range(2):
                        last = nc.tensor.transpose(ps[:, B + 3, j * P:(j + 1) * P], st[d][:, 2 + j], M.ident)
                    for h in H2:
                        for b in range(2):
                            last = nc.tensor.matmul(ps[half[b], B + 3 - h, 256:320], st[d][half[h], 2, half[b]],
                                                    st[d][half[h], 0, half[b]], start=True, stop=True)
                    last.then_inc(ev("turned", d), 1)
                    need(pe, ev("y_read", d), n)
                    for h in H2:
                        ar = st[d][half[h], 0:2].rearrange("p m t -> p (m t)")
                        nc.tensor.matmul(ps[:, B + h, 0:256], st[d][half[h], 2], ar, start=True, stop=True)
                        nc.tensor.matmul(ps[:, B + h, 256:512], st[d][half[h], 3], ar, start=True, stop=True)\
                            .then_inc(ev("scores", d, h), 1)
                for d in D2:
                    B = 4 * d
                    first(pe)
                    pe.wait_ge(ev("xt0", d), n + 1)
                    pe.wait_ge(ev("turned_read", d), n + 1)
                    for h in H2:
                        last = blocks(B + 2, 64 * h, xx[d][:, h, 1], M.ident64)
                    last.then_inc(ev("x0", d), 1)
                for l in range(1, NLEV):
                    for d in D2:
                        B = 4 * d
                        first(pe)
                        pe.wait_ge(ev("x", d, l - 1), n + 1)
                        for h in H2:
                            last = blocks(B + 2, 64 * h, lo[d][:, h, l], xx[d][:, h, 0])
                        last.then_inc(ev("q", d, l) if l < NLEV - 1 else ev("q_last", d), 1)
                    for d in D2:
                        B = 4 * d
                        first(pe)
                        pe.wait_ge(ev("q_read", d, l), n + 1)
                        if l == 1:
                            pe.wait_ge(ev("turned_read", d), n + 1)
                        for h in H2:
                            if l < NLEV - 1:
                                blocks(B + 3, 128 * h, xx[d][:, h, 1], qs[d][:, h])
                            last = blocks(B + 3, 128 * h + 64, qs[d][:, h], xx[d][:, h, 1])
                        last.then_inc(ev("xq", d, l), 1)
                for d in D2:
                    B = 4 * d
                    pe.wait_ge(ev("vs", d), n + 1)
                    need(pe, ev("p", d), n)
                    pe.wait_ge(ev("x", d, NLEV - 1), n + 1)
                    for h in H2:
                        nc.tensor.matmul(ps[:, B + 2 + h, 0:64], st[d][half[h], 0], p[d][half[h]], start=True, stop=False)
                        last = nc.tensor.matmul(ps[:, B + 2 + h, 0:64], mt[d][h][:, 2], vs[d][:, 64 * h:64 * h + 64],
                                                start=False, stop=True)
                    last.then_inc(ev("rhs", d), 1)
                for d in D2:
                    B, F = 4 * d, half[d]
                    first(pe)
                    pe.wait_ge(ev("x", d, NLEV - 1), n + 1)
                    pe.wait_ge(ev("rhs_read", d), n + 1)
                    for h in H2:
                        last = nc.tensor.matmul(ps[F, B + 3, 64 * h:64 * h + 64], xx[d][F, h, 1], rs[d][F, h], start=True, stop=True)
                    last.then_inc(ev("u_head", d), 1)
                for d in D2:
                    B, F, S = 4 * d, half[d], half[1 - d]
                    first(pe)
                    pe.wait_ge(ev("u_head_read", d), n + 1)
                    for h in H2:
                        last = nc.tensor.matmul(ps[S, B + 2, 64 * h:64 * h + 64], mt[d][h][F, 0, S], u[d][F, h], start=True, stop=True)
                    last.then_inc(ev("cross", d), 1)
                for d in D2:
                    B, S = 4 * d, half[1 - d]
                    first(pe)
                    pe.wait_ge(ev("cross_read", d), n + 1)
                    for h in H2:
                        last = nc.tensor.matmul(ps[S, B + 3, 64 * h:64 * h + 64], xx[d][S, h, 1], rs[d][S, h], start=True, stop=True)
                    last.then_inc(ev("u_first", d), 1)
                for d in D2:
                    B = 4 * d
                    pe.wait_ge(ev("u_second_read", d), n + 1)
                    for h in H2:
                        o = ps[half[h], B + 2, 0:64]
                        nc.tensor.matmul(o, tm[d][:, 0, half[h]], u[d][:, h], start=True, stop=False)
                        last = nc.tensor.matmul(o, tm[d][:, 1, half[h]], vs[d][:, half[h]], start=False, stop=True)
                    last.then_inc(ev("p_sum", d), 1)
                    for h in H2:
                        o = ps[:, B + h, 0:64]
                        nc.tensor.matmul(o, st[d][half[h], 1], p[d][half[h]], start=True, stop=False)
                        nc.tensor.matmul(o, mt[d][h][:, 1], u[d][:, h], start=False, stop=False)
                        last = nc.tensor.matmul(o, mt[d][h][:, 3], vs[d][:, half[h]], start=False, stop=True)
                    last.then_inc(ev("state", d), 1)
            pe.wait_ge(ev("p_clear"), 2)
            tiles_of(pe, body)

        @block.scalar
        def _(act):
            def body(n, tile):
                for d in D2:
                    B = 4 * d
                    act.wait_ge(ev("turned", d), n + 1)
                    nc.scalar.activation(tm[d].rearrange("p m t -> p (m t)")[:, 0:2 * P + 64], ps[:, B + 3, 0:2 * P + 64], ACT.Copy)
                    nc.scalar.activation(tm[d][:, 2, 64:P], ps[:, B + 2, 256:320], ACT.Copy).then_inc(ev("turned_read", d), 1)
                for d in D2:
                    act.wait_ge(ev("x0", d), n + 1)
                    nc.scalar.activation(xx[d][:, :, 0, :], ps[:, 4 * d + 2, 0:P].rearrange("p (h c) -> p h c", h=2), ACT.Copy)\
                        .then_inc(ev("x", d, 0), 1)
                for l in range(1, NLEV):
                    for d in D2:
                        act.wait_ge(ev("q", d, l) if l < NLEV - 1 else ev("q_last", d), n + 1)
                        nc.scalar.activation(flat(qs[d]), ps[:, 4 * d + 2, 0:P], ACT.Copy).then_inc(ev("q_read", d, l), 1)
                for d in D2:
                    act.wait_ge(ev("rhs", d), n + 1)
                    nc.scalar.activation(rs[d], ps[:, 4 * d + 2:4 * d + 4, 0:64], ACT.Copy).then_inc(ev("rhs_read", d), 1)
            tiles_of(act, body)

        @block.vector
        def _(dve):
            tt = nc.vector.tensor_tensor
            dve.wait_ge(ev("y_clear"), 1)
            dve.wait_ge(ev("h0"), 16)

            def body(n, tile):
                for d in D2:
                    for h in H2:
                        dve.wait_ge(ev("scores", d, h), n + 1)
                        tt(mt[d][h], ps[:, 4 * d + h, :].rearrange("p (m t) -> p m t", m=4), M.score_mask[:, d], ALU.mult)\
                            .then_inc(ev("masked", d, h), 1)
                for l in range(1, NLEV):
                    for d in D2:
                        dve.wait_ge(ev("xq", d, l), n + 1)
                        z = ps[:, 4 * d + 3, 0:256].rearrange("p (h m c) -> p h m c", h=2, m=2)
                        ms = slice(0, 2) if l < NLEV - 1 else slice(1, 2)
                        tt(xx[d][:, :, ms], xx[d][:, :, ms], z[:, :, ms], ALU.add).then_inc(ev("x", d, l), 1)
                for d in D2:
                    F = half[d]
                    dve.wait_ge(ev("u_head", d), n + 1)
                    nc.vector.tensor_copy(flat(u[d][F]), ps[F, 4 * d + 3, 0:P]).then_inc(ev("u_head_read", d), 1)
                for d in D2:
                    S = half[1 - d]
                    dve.wait_ge(ev("cross", d), n + 1)
                    tt(flat(rs[d][S]), flat(rs[d][S]), ps[S, 4 * d + 2, 0:P], ALU.add).then_inc(ev("cross_read", d), 1)
                for d in D2:
                    S = half[1 - d]
                    dve.wait_ge(ev("u_first", d), n + 1)
                    nc.vector.tensor_copy(flat(u[d][S]), ps[S, 4 * d + 3, 0:P]).then_inc(ev("u_second_read", d), 1)
                for d in D2:
                    dve.wait_ge(ev("p_sum", d), n + 1)
                    tt(pt[d], ps[:, 4 * d + 2, 0:64], p[d], ALU.add).then_inc(ev("p_read", d), 1)
                    first(dve)
                    dve.wait_ge(ev("state", d), n + 1)
                    dve.wait_ge(ev("p_read", d), n + 1)
                    if isinstance(n, int):
                        nc.vector.tensor_scalar(fin[:, d], pt[d], R.post[d][:, LB:LB + 1], None, ALU.mult).then_inc(ev("final"), 1)
                        begin = (0, LB - 1)[d]
                        nc.vector.tensor_scalar(p[d], h0[:, d], R.pre[d][:, begin:begin + 1], None, ALU.mult).then_inc(ev("p", d), 1)
                    else:
                        tt(p[d], pt[d], R.step[d][:, ds(tile[d], 1)].broadcast_to([P, 64]), ALU.mult).then_inc(ev("p", d), 1)
                    first(dve)
                    if d == 1:
                        dve.wait_ge(ev("y_read", 0), n + 1)
                    need(dve, ev("y_read", 1), n)
                    y = R.y[:, ds(tile[d], 1), :].rearrange("p b (h c) -> p (b h) c", h=2)
                    tt(y, y, ps[:, 4 * d:4 * d + 2, 0:64], ALU.add).then_inc(ev("y_read", d), 1)
            tiles_of(dve, body)
    clear(nc, ev)
    A.at = keep


def stage_finish(nc, M, ins, ct):
    A, ps, R = M.arena, M.ps, M.rwkv
    keep = A.at
    NH = 2 * NB
    g = A.take(NB, P)
    t = A.take(NB, P)
    ln = A.take(2, P)
    mean, var, rstd = A.take(NH), A.take(NH), A.take(NH)
    yt = A.take(T)
    y = R.y
    heads = lambda v: v.rearrange("p b (h c) -> p (b h) c", h=2)
    row = lambda n: ln[:, n:n + 1, :].broadcast_to([P, NB, P])
    each = lambda v: v.unsqueeze(2).broadcast_to([P, NH, HEAD])
    with ExitStack() as ctx:
        ev = Events(nc, ctx, "fin")
        block = ctx.enter_context(nc.Block())
        tt, ts = nc.vector.tensor_tensor, nc.vector.tensor_scalar

        @block.sync
        def _(sp):
            sp.dma_start(ln, ins["ln"][ds(ct, 1)].squeeze(0)).then_inc(ev("ln"), 16)

        @block.tensor
        def _(pe):
            for b in range(NB):
                cols = slice(b * P, (b + 1) * P)
                last = split_mm(nc, ps[:, b // 4, b % 4 * P:(b % 4 + 1) * P], M.lora_hi[:, 2, cols], M.lora_lo[:, 2, cols],
                                R.up_hi[:, 2], R.up_lo[:, 2], True, True)
                if b % 4 == 3 or b == NB - 1:
                    last.then_inc(ev("gate"), 1)
            pe.wait_ge(ev("y"), 1)
            for b in range(NB):
                last = nc.tensor.transpose(ps[:, 4 + b // 4, b % 4 * P:(b % 4 + 1) * P], y[:, b], M.ident)
                if b % 4 == 3 or b == NB - 1:
                    last.then_inc(ev("turned"), 1)

        @block.scalar
        def _(act):
            for n in range(3):
                w = 4 if n < 2 else 1
                act.wait_ge(ev("gate"), n + 1)
                nc.scalar.activation(g[:, 4 * n:4 * n + w].rearrange("p b c -> p (b c)"), ps[:, n, 0:w * P], ACT.Copy)\
                    .then_inc(ev("gate_read"), 1)
            act.wait_ge(ev("centred"), 1)
            nc.scalar.activation(t, y, ACT.Square).then_inc(ev("square"), 1)
            act.wait_ge(ev("turned_read"), 3)
            nc.scalar.activation(M.yr_hi[:, ds(ct, 1)].rearrange("p a t -> p (a t)"), yt, ACT.Copy).then_inc(ev("hi"), 1)

        @block.gpsimd
        def _(pool):
            pool.wait_ge(ev("var"), 1)
            nc.gpsimd.tensor_tensor(rstd, var, M.neg_half.broadcast_to([P, NH]), ALU.pow).then_inc(ev("rstd"), 1)
            pool.wait_ge(ev("hi"), 1)
            nc.gpsimd.tensor_tensor(M.yr_lo[:, ds(ct, 1)].rearrange("p a t -> p (a t)"), yt,
                                    M.yr_hi[:, ds(ct, 1)].rearrange("p a t -> p (a t)"), ALU.subtract).then_inc(ev("lo"), 1)

        @block.vector
        def _(dve):
            c = Chain(ev("dve"))

            def op(ins_):
                c.step(ins_)
                c.settle(dve)
            op(nc.vector.reduce_sum(mean, heads(y), mybir.AxisListType.X))
            op(ts(mean, mean, 1.0 / HEAD, None, ALU.mult))
            tt(heads(y), heads(y), each(mean), ALU.subtract).then_inc(ev("centred"), 1)
            dve.wait_ge(ev("square"), 1)
            op(nc.vector.reduce_sum(var, heads(t), mybir.AxisListType.X))
            ts(var, var, 1.0 / HEAD, GN_EPS, ALU.mult, ALU.add).then_inc(ev("var"), 1)
            dve.wait_ge(ev("rstd"), 1)
            c.step(tt(heads(t), heads(R.v), each(R.bonus), ALU.mult))
            op(tt(heads(y), heads(y), each(rstd), ALU.mult))
            dve.wait_ge(ev("ln"), 16)
            op(tt(y, y, row(0), ALU.mult))
            op(tt(y, y, row(1), ALU.add))
            op(tt(y, y, t, ALU.add))
            dve.wait_ge(ev("gate_read"), 3)
            tt(y, y, g, ALU.mult).then_inc(ev("y"), 1)
            for n in range(3):
                w = (4 if n < 2 else 1) * P
                dve.wait_ge(ev("turned"), n + 1)
                nc.vector.tensor_copy(yt[:, 4 * n * P:4 * n * P + w], ps[:, 4 + n, 0:w]).then_inc(ev("turned_read"), 1)
    clear(nc, ev)
    A.at = keep


def stage_rwkv(nc, M, ins, outs):
    A = M.arena
    R = M.rwkv = Memory()
    M.yr_hi, M.yr_lo = A.take(NCT, T, dt=BF16), A.take(NCT, T, dt=BF16)
    keep = A.at
    M.lora_hi, M.lora_lo = A.take(3, T, dt=BF16), A.take(3, T, dt=BF16)
    stage_lora(nc, M, ins)
    R.x = [A.take(NB, 4, P) for _ in range(2)]
    R.v, R.y = A.take(NB, P), A.take(NB, P)
    R.bonus = A.take(2 * NB)
    R.pre, R.post, R.step = ([A.take(NB) for _ in range(2)] for _ in range(3))
    R.par = A.take(7)
    R.up_hi, R.up_lo = A.take(3, P, dt=BF16), A.take(3, P, dt=BF16)
    with nc.Fori(0, NCT) as ct:
        stage_prepare(nc, M, ins, ct)
        stage_chunks(nc, M, ins, outs, ct)
        stage_finish(nc, M, ins, ct)
    A.at = keep


def pairs(eng, body):
    def two(i):
        body(0, i, i * 2, 0)
        body(1, i, i * 2 + 1, 0)
    rounds(eng, LB // 2, two)
    body(0, LB // 2, LB, 1)


def stage_out(nc, M, ins):
    A, ps = M.arena, M.ps
    keep = A.at
    wst = A.take(KD, 512)
    whi = [A.take(KD, 512, dt=BF16) for _ in range(2)]
    wlo = [A.take(KD, 512, dt=BF16) for _ in range(2)]
    gate = A.take(2, D)
    xt, pt, t = ([A.take(D) for _ in range(2)] for _ in range(3))
    with ExitStack() as ctx:
        ev = Events(nc, ctx, "out")
        block = ctx.enter_context(nc.Block())

        @block.sync
        def _(sp):
            sp.dma_start(gate, ins["gates"][0].partition_broadcast(P)).then_inc(ev("gate"), 16)
            for h in range(2):
                if h:
                    sp.wait_ge(ev("w_lo"), 1)
                sp.dma_start(wst, ins["w_out"][:, :, h * 512:(h + 1) * 512]).then_inc(ev("w"), 16)

            def tile(q, n, b, w):
                need(sp, ev("stored", q), n * 16)
                sp.dma_start(xt[q], ins["x"][ds(b, 1)].squeeze(0)).then_inc(ev("x", q), 16)
                sp.dma_start(pt[q], ins["pos"][ds(b, 1)].squeeze(0)).then_inc(ev("x", q), 16)
            pairs(sp, tile)

        @block.scalar
        def _(act):
            for h in range(2):
                act.wait_ge(ev("w"), 16 * h + 16)
                nc.scalar.activation(whi[h], wst, ACT.Copy).then_inc(ev("w_hi"), 1)

            def tile(q, n, b, w):
                act.wait_ge(ev("sum", q), n + 1)
                act.dma_start(ins["x1"][ds(b, 1)].squeeze(0), xt[q]).then_inc(ev("stored", q), 16)
            pairs(act, tile)
            act.wait_ge(ev("stored", 0), 16 * 5)
            act.wait_ge(ev("stored", 1), 16 * 4)

        @block.gpsimd
        def _(pool):
            for h in range(2):
                pool.wait_ge(ev("w_hi"), h + 1)
                nc.gpsimd.tensor_tensor(wlo[h], wst, whi[h], ALU.subtract).then_inc(ev("w_lo"), 1)

            def tile(q, n, b, w):
                pool.wait_ge(ev("x", q), n * 32 + 32)
                nc.gpsimd.tensor_tensor(xt[q], xt[q], pt[q], ALU.add).then_inc(ev("x_pos", q), 1)
            pairs(pool, tile)

        @block.tensor
        def _(pe):
            pe.wait_ge(ev("w_lo"), 2)

            def tile(q, n, b, w):
                need(pe, ev("gated", q), n)
                cols = ds(b * P, P)
                for h in range(2):
                    for k in range(KD):
                        hi, lo = (M.yr_hi, M.yr_lo) if k < NCT else (M.ys_hi, M.ys_lo)
                        last = split_mm(nc, ps[:, 2 * q + h, :], hi[:, k % NCT, cols], lo[:, k % NCT, cols],
                                        whi[h][:, k], wlo[h][:, k], k == 0, k == KD - 1)
                last.then_inc(ev("product", q), 1)
            pairs(pe, tile)

        @block.vector
        def _(dve):
            dve.wait_ge(ev("gate"), 16)

            def tile(q, n, b, w):
                dve.wait_ge(ev("product", q), n + 1)
                need(dve, ev("sum", q), n)
                nc.vector.tensor_tensor(t[q].rearrange("p (h c) -> p h c", h=2), ps[:, 2 * q:2 * q + 2, :],
                                        gate[:, w].rearrange("p (h c) -> p h c", h=2), ALU.mult).then_inc(ev("gated", q), 1)
                dve.wait_ge(ev("x_pos", q), n + 1)
                dve.wait_ge(ev("gated", q), n + 1)
                nc.vector.tensor_tensor(xt[q], xt[q], t[q], ALU.add).then_inc(ev("sum", q), 1)
            pairs(dve, tile)
    clear(nc, ev)
    A.at = keep


def stage_mlp(nc, M, ins):
    A, ps = M.arena, M.ps
    FW = 512
    ROUNDS, O = FF // FW, FW // P
    M.acc = A.take(NB, D)
    keep = A.at
    w1s = A.take(KD, FW)
    w2s = A.take(O, D)
    w1hi, w1lo = A.take(KD, FW, dt=BF16), A.take(KD, FW, dt=BF16)
    w2hi, w2lo = A.take(O, D, dt=BF16), A.take(O, D, dt=BF16)
    f = [A.take(T) for _ in range(2)]
    hhi, hlo = A.take(O, T, dt=BF16), A.take(O, T, dt=BF16)
    with ExitStack() as ctx:
        ev = Events(nc, ctx, "mlp")
        block = ctx.enter_context(nc.Block())

        @block.sync
        def _(sp):
            def load1(j):
                sp.dma_start(w1s, ins["w_ff1"][:, :, ds(j * FW, FW)]).then_inc(ev("w1"), 16)

            def load2(j):
                sp.dma_start(w2s, ins["w_ff2"][:, ds(j * O, O), :]).then_inc(ev("w2"), 16)
            load1(0)
            load2(0)
            with sp.Fori(0, ROUNDS - 1) as j:
                sp.wait_ge(ev("w1_lo"), j + 1)
                load1(j + 1)
                sp.wait_ge(ev("w2_lo"), j + 1)
                load2(j + 1)

        @block.gpsimd
        def _(pool):
            nc.gpsimd.memset(M.acc, 0.0).then_inc(ev("acc_clear"), 1)
            with pool.Fori(0, ROUNDS) as j:
                pool.wait_ge(ev("w1_hi"), j + 1)
                nc.gpsimd.tensor_tensor(w1lo, w1s, w1hi, ALU.subtract).then_inc(ev("w1_lo"), 1)
                pool.wait_ge(ev("w2_hi"), j + 1)
                nc.gpsimd.tensor_tensor(w2lo, w2s, w2hi, ALU.subtract).then_inc(ev("w2_lo"), 1)

        @block.scalar
        def _(act):
            def split1(j):
                act.wait_ge(ev("w1"), j * 16 + 16)
                nc.scalar.activation(w1hi, w1s, ACT.Copy).then_inc(ev("w1_hi"), 1)

            def body(j, more):
                act.wait_ge(ev("w2"), j * 16 + 16)
                need(act, ev("ff2"), j * (2 * NB))
                nc.scalar.activation(w2hi, w2s, ACT.Copy).then_inc(ev("w2_hi"), 1)
                for o in range(O):
                    act.wait_ge(ev("ff1"), j * O + (o + 1))
                    if o >= 2:
                        act.wait_ge(ev("h_lo"), j * O + (o - 1))
                    else:
                        need(act, ev("h_lo"), j * O)
                    nc.scalar.activation(f[o % 2].rearrange("p (g c) -> p g c", g=TG), wide(ps, 3 * (o % 2)),
                                         ACT.Relu).then_inc(ev("relu"), 1)
                    act.wait_ge(ev("square"), j * O + (o + 1))
                    nc.scalar.activation(hhi[:, o], f[o % 2], ACT.Copy).then_inc(ev("h_hi"), 1)
                if more:
                    split1(j + 1)
            split1(0)
            rounds(act, ROUNDS - 1, lambda j: body(j, True))
            body(ROUNDS - 1, False)

        @block.vector
        def _(dve):
            dve.wait_ge(ev("acc_clear"), 1)
            with dve.Fori(0, ROUNDS) as j:
                for o in range(O):
                    dve.wait_ge(ev("relu"), j * O + (o + 1))
                    nc.vector.tensor_tensor(f[o % 2], f[o % 2], f[o % 2], ALU.mult).then_inc(ev("square"), 1)
                    dve.wait_ge(ev("h_hi"), j * O + (o + 1))
                    nc.vector.tensor_tensor(hlo[:, o], f[o % 2], hhi[:, o], ALU.subtract).then_inc(ev("h_lo"), 1)
                for b in range(NB):
                    for h in range(2):
                        n = 2 * b + h
                        dve.wait_ge(ev("ff2"), j * (2 * NB) + (n + 1))
                        a = M.acc[:, b, h * 512:(h + 1) * 512]
                        nc.vector.tensor_tensor(a, a, ps[:, 6 + h, :], ALU.add).then_inc(ev("acc"), 1)

        @block.tensor
        def _(pe):
            with pe.Fori(0, ROUNDS) as j:
                pe.wait_ge(ev("w1_lo"), j + 1)
                for o in range(O):
                    if o >= 2:
                        pe.wait_ge(ev("relu"), j * O + (o - 1))
                    for g in range(TG):
                        cols = slice(g * TW, (g + 1) * TW)
                        for k in range(KD):
                            last = split_mm(nc, ps[:, 3 * (o % 2) + g, 0:TW], w1hi[:, k, o * P:(o + 1) * P],
                                            w1lo[:, k, o * P:(o + 1) * P], M.hi[:, k, cols], M.lo[:, k, cols],
                                            k == 0, k == KD - 1)
                    last.then_inc(ev("ff1"), 1)
                pe.wait_ge(ev("w2_lo"), j + 1)
                pe.wait_ge(ev("h_lo"), j * O + O)
                for b in range(NB):
                    cols = slice(b * P, (b + 1) * P)
                    for h in range(2):
                        n = 2 * b + h
                        if n >= 2:
                            pe.wait_ge(ev("acc"), j * (2 * NB) + (n - 1))
                        for k in range(O):
                            last = split_mm(nc, ps[:, 6 + h, :], hhi[:, k, cols], hlo[:, k, cols],
                                            w2hi[:, k, h * 512:(h + 1) * 512], w2lo[:, k, h * 512:(h + 1) * 512],
                                            k == 0, k == O - 1)
                        last.then_inc(ev("ff2"), 1)
    clear(nc, ev)
    A.at = keep


def stage_last(nc, M, ins, outs):
    A = M.arena
    keep = A.at
    gate, gf = A.take(2, D), A.take(D)
    xt = [A.take(D) for _ in range(2)]
    junk = [A.take(D) for _ in range(2)]
    ss, ms, rs = ([A.take(1) for _ in range(2)] for _ in range(3))
    with ExitStack() as ctx:
        ev = Events(nc, ctx, "last")
        block = ctx.enter_context(nc.Block())

        @block.sync
        def _(sp):
            sp.dma_start(gate, ins["gates"][1].partition_broadcast(P)).then_inc(ev("gate"), 16)
            sp.dma_start(gf, ins["norm_f_g"]).then_inc(ev("gate"), 16)

            def tile(q, n, b, w):
                need(sp, ev("stored", q), n * 16)
                sp.dma_start(xt[q], ins["x1"][ds(b, 1)].squeeze(0)).then_inc(ev("x", q), 16)
            pairs(sp, tile)

        @block.gpsimd
        def _(pool):
            def tile(q, n, b, w):
                pool.wait_ge(ev("mean_sq", q), n + 1)
                nc.gpsimd.tensor_tensor(rs[q], ms[q], M.neg_half, ALU.pow).then_inc(ev("rstd", q), 1)
                pool.wait_ge(ev("y", q), n + 1)
                pool.dma_start(outs["y"][ds(b, 1)].squeeze(0), xt[q]).then_inc(ev("stored", q), 16)
            pairs(pool, tile)
            pool.wait_ge(ev("stored", 0), 16 * 5)
            pool.wait_ge(ev("stored", 1), 16 * 4)

        @block.scalar
        def _(act):
            def tile(q, n, b, w):
                act.wait_ge(ev("sum", q), n + 1)
                nc.scalar.activation(junk[q], xt[q], ACT.Square, accum_out=ss[q]).then_inc(ev("squares", q), 1)
                act.wait_ge(ev("squares", q), n + 1)
                need(act, ev("rstd", q), n)
                nc.scalar.activation(ms[q], ss[q], ACT.Copy, scale=1.0 / D, bias=RMS_EPS).then_inc(ev("mean_sq", q), 1)
            pairs(act, tile)

        @block.vector
        def _(dve):
            dve.wait_ge(ev("gate"), 32)

            def add(q, n, b, w):
                a = M.acc[:, ds(b, 1)].rearrange("p b c -> p (b c)")
                nc.vector.tensor_tensor(a, a, gate[:, w], ALU.mult).then_inc(ev("gated", q), 1)
                dve.wait_ge(ev("x", q), n * 16 + 16)
                dve.wait_ge(ev("gated", q), n + 1)
                nc.vector.tensor_tensor(xt[q], xt[q], a, ALU.add).then_inc(ev("sum", q), 1)

            def scale(q, n):
                dve.wait_ge(ev("rstd", q), n + 1)
                dve.wait_ge(ev("squares", q), n + 1)
                nc.vector.scalar_tensor_tensor(out=xt[q], in0=xt[q], scalar=rs[q], in1=gf, op0=ALU.mult,
                                               op1=ALU.mult).then_inc(ev("y", q), 1)
            with dve.Fori(0, LB // 2) as i:
                add(0, i, i * 2, 0)
                add(1, i, i * 2 + 1, 0)
                scale(0, i)
                scale(1, i)
            add(0, LB // 2, LB, 1)
            scale(0, LB // 2)
    A.at = keep


class Memory:
    pass


def program(nc, ins, outs, scratch, upto=99):
    M = Memory()
    M.arena = A = Arena(nc, 51200)
    M.ps = nc.alloc_psum_tensor("psum", [P, 8, 512], F32)
    M.const = A.take(P + 64 + 2 * 4 * P + 2 * NLEV * 64 + P + 2 + 1 + 1 + 1)
    at = 0

    def part(n, shape=None):
        nonlocal at
        v = M.const[:, at:at + n]
        at += n
        return v
    M.ident = part(P)
    M.ident64 = part(64)
    M.score_mask = part(2 * 4 * P).rearrange("p (d m t) -> p d m t", d=2, m=4)
    M.level_mask = part(2 * NLEV * 64).rearrange("p (d l t) -> p d l t", d=2, l=NLEV)
    M.head_ones = part(P)
    M.head_ind = part(2)
    M.neg_half = part(1)
    M.one = part(1)
    M.zero = part(1)
    M.scale = [A.take(KD, 2) for _ in range(2)]
    M.shift = [A.take(KD, 2) for _ in range(2)]
    ins.update(scratch)
    stage_modulation(nc, M, ins)
    M.hi = A.take(KD, T, dt=BF16)
    M.lo = A.take(KD, T, dt=BF16)
    stage_norm(nc, M, "norm1", ins["x"], ins["pos"], 0, (M.hi, M.lo))
    keep_front = A.at
    stage_s5_tables(nc, M, ins)
    M.u = A.take(G, NC_)
    stage_u(nc, M, ins)
    stage_s5(nc, M, ins, outs)
    if upto == 2:
        dump(nc, scratch["dbg"], [M.u, M.y_lat])
        return
    after = A.at
    A.at = keep_front
    M.ys_hi, M.ys_lo = A.take(DS // P, T, dt=BF16), A.take(DS // P, T, dt=BF16)
    front = A.at
    A.at = after
    stage_glu(nc, M, ins)
    A.at = front
    stage_rwkv(nc, M, ins, outs)
    if upto == 3:
        dump(nc, scratch["dbg"], [M.ys_hi.bitcast(F32), M.ys_lo.bitcast(F32), M.yr_hi.bitcast(F32), M.yr_lo.bitcast(F32)])
        return
    stage_out(nc, M, ins)
    A.at = keep_front
    stage_norm(nc, M, "norm2", ins["x1"], None, 1, (M.hi, M.lo))
    stage_mlp(nc, M, ins)
    stage_last(nc, M, ins, outs)


def dump(nc, dbg, views):
    with ExitStack() as ctx:
        s = ctx.enter_context(nc.semaphore("dbg"))
        block = ctx.enter_context(nc.Block())

        @block.sync
        def _(sp):
            at = 0
            for v in views:
                n = int(np.prod(v.shape[1:]))
                names = " ".join(f"d{i}" for i in range(len(v.shape) - 1))
                src = dbg[0:v.shape[0], at:at + n]
                if len(v.shape) > 2:
                    src = src.rearrange(f"p ({names}) -> p {names}", **{f"d{i}": v.shape[i + 1] for i in range(len(v.shape) - 1)})
                sp.dma_start(src, v).then_inc(s, 16)
                at += n
            sp.wait_ge(s, 16 * len(views))


def constants():
    s, t = np.meshgrid(np.arange(P), np.arange(P), indexing="ij")
    before, upto = (s < t), (s <= t)
    after, down = (s > t), (s >= t)
    score = np.stack([np.stack([before, upto, before, upto]), np.stack([after, down, after, down])])
    s, t = np.meshgrid(np.arange(P) % 64, np.arange(64), indexing="ij")
    level = np.zeros((2, NLEV, P, 64))
    for l in range(NLEV):
        b = 2 << l
        off = (s // b == t // b) & (s // (b // 2) != t // (b // 2))
        level[0, l] = off & (s < t)
        level[1, l] = off & (s > t)
    ones = np.kron(np.eye(2), np.ones((64, 64)))
    ind = np.kron(np.eye(2), np.ones((64, 1)))
    return np.concatenate([np.eye(P), np.tile(np.eye(64), (2, 1)), score.transpose(2, 0, 1, 3).reshape(P, -1),
                           level.transpose(2, 0, 1, 3).reshape(P, -1), ones, ind, np.full((P, 1), -0.5),
                           np.ones((P, 1)), np.zeros((P, 1))], axis=1).astype(np.float32)


def position_embedding():
    rows, width, nf = NLAT // 64, 64, D // 4
    omega = (np.float32(1.0) / (np.float32(10000.0) ** (np.arange(nf, dtype=np.float32) / np.float32(nf)))).astype(np.float32)
    ar = (np.arange(rows, dtype=np.float32)[:, None] * omega).astype(np.float32)
    ac = (np.arange(width, dtype=np.float32)[:, None] * omega).astype(np.float32)
    er, ec = (np.concatenate([np.sin(a), np.cos(a)], axis=-1) for a in (ar, ac))
    pe = np.concatenate([np.broadcast_to(er[:, None], (rows, width, D // 2)),
                         np.broadcast_to(ec[None], (rows, width, D // 2))], axis=-1).reshape(LB, P, D)
    return np.concatenate([pe, np.zeros((1, P, D))]).astype(np.float32)


def kernel(**inputs):
    import concourse.bacc as bacc
    from concourse.bass_utils import run_bass_kernel_spmd

    x = {k: np.asarray(v) for k, v in inputs.items()}

    def cols(v, n):
        return v.reshape(n, P).T

    a = {
        "consts": constants(),
        "pos": position_embedding(),
        "x": np.concatenate([x["x_sample"][0], x["x_prompt"][0]]).reshape(NB, P, D),
        "cond": np.stack([cols(x["c"][0], KD), cols(x["c_ctx"], KD)], axis=2),
        "norm_g": np.stack([cols(x["norm1_g"][0], KD), cols(x["norm2_g"][0], KD)], axis=1),
        "b_ada": np.stack([x["b_ada"][0]] * 2),
        "w_ada": x["w_ada"][0],
    }
    a.update(more_inputs(x, cols))
    a = {k: np.ascontiguousarray(v) for k, v in a.items()}
    nc = bacc.Bacc("TRN2", target_bir_lowering=False, num_devices=1)
    ins = {k: nc.dram_tensor("in_" + k, v.shape, F32, kind="ExternalInput").ap() for k, v in a.items()}
    for w in ("w_ada", "w_in", "w_glu", "w_out", "w_ff1", "w_ff2"):
        if w in ins:
            ins[w] = ins[w].rearrange("(k p) n -> p k n", p=P)
    shapes = {"y": (NB, P, D), "rwkv": (NCT, P, 2, 64), "ssm": (P, 2, G)}
    outs = {k: nc.dram_tensor("out_" + k, v, F32, kind="ExternalOutput").ap() for k, v in shapes.items()}
    scratch = {"x1": nc.dram_tensor("x1", (NB, P, D), F32, kind="Internal").ap(),
               "gates": nc.dram_tensor("gates", (2, 2, D), F32, kind="Internal").ap(),
               "y_bounce": nc.dram_tensor("y_bounce", (P, DS), F32, kind="Internal").ap(),
               "u_bounce": nc.dram_tensor("u_bounce", (P, DS), F32, kind="Internal").ap()}
    if UPTO < 99:
        scratch["dbg"] = nc.dram_tensor("dbg", (P, 51200), F32, kind="ExternalOutput").ap()
    program(nc, ins, outs, scratch, UPTO)
    r = run_bass_kernel_spmd(nc, [{"in_" + k: v for k, v in a.items()}], core_ids=[0]).results[0]
    y = r["out_y"].reshape(T, D)
    rw = r["out_rwkv"].reshape(NCT, 2, 64, 2, 64)
    rw = rw.transpose(3, 0, 1, 4, 2).reshape(1, 1, 2, 8, 64, 64)
    sm = r["out_ssm"].reshape(2, NS, 2, G)
    return (y[NLAT:].reshape(1, NCTX, D), y[:NLAT].reshape(1, NLAT, D), rw,
            sm[:, :, 0].transpose(0, 2, 1).reshape(1, 1, 2, G, NS),
            sm[:, :, 1].transpose(0, 2, 1).reshape(1, 1, 2, G, NS))


def more_inputs(x, cols):
    def lanes(v):
        v = v.transpose(0, 2, 1, *range(3, v.ndim))
        return v.reshape(P, *v.shape[2:])
    both = lambda v: np.broadcast_to(v[None], (2, *v.shape))
    return {
        "w_in": x["w_in"][0],
        "ssm_par": np.stack([lanes(both(x["ssm_lambda_re"][0])), lanes(both(x["ssm_lambda_im"][0])),
                             lanes(np.broadcast_to(x["ssm_log_dt"][0][:, :, None], (2, G, NS)))], axis=1),
        "ssm_b_re": lanes(x["ssm_b_re"][0]), "ssm_b_im": lanes(x["ssm_b_im"][0]),
        "ssm_c_re": lanes(x["ssm_c_re"][0].transpose(0, 1, 3, 2)),
        "ssm_c_im": lanes(x["ssm_c_im"][0].transpose(0, 1, 3, 2)),
        "ssm_h_re": lanes(x["state_ssm_re"][0, 0]), "ssm_h_im": lanes(x["state_ssm_im"][0, 0]),
        "ssm_d": x["ssm_d"][0].reshape(G, GC).T,
        "w_out": x["w_out"][0], "w_ff1": x["w_ff1"][0], "w_ff2": x["w_ff2"][0],
        "norm_f_g": np.broadcast_to(x["norm_f_g"], (P, D)),
        "w_glu": x["w_glu"][0], "b_glu": cols(x["b_glu"][0], DS // P),
        "par": np.stack([x["k_k"][0], x["k_a"][0], x["r_k"][0].reshape(DR), *x["decay_base"][0], *x["iclr_base"][0]],
                        axis=1).reshape(NCT, P, 7),
        "up": np.stack([x["w_decay_up"][0].reshape(P, DR), x["w_iclr_up"][0].reshape(P, DR), x["w_gate_up"][0]],
                       axis=1).reshape(P, 3, NCT, P).transpose(2, 0, 1, 3),
        "state": x["state_rwkv"][0, 0].reshape(2, NCT, 2, HEAD, HEAD).transpose(1, 2, 4, 0, 3).reshape(NCT, P, 2, HEAD),
        "ln": np.broadcast_to(np.stack([x["lnx_g"][0], x["lnx_b"][0]]).reshape(2, NCT, 1, P).transpose(1, 2, 0, 3),
                              (NCT, P, 2, P)),
    }


UPTO = 99
```

```python
import math
from contextlib import ExitStack

import numpy as np
import concourse.bass as bass
from concourse import mybir
from concourse.alu_op_type import AluOpType as ALU

F32 = mybir.dt.float32
BF16 = mybir.dt.bfloat16
ACT = mybir.ActivationFunctionType
ds = bass.ds

P = 128
D = 1024
KD = D // P
NLAT, NCTX = 1024, 128
T = NLAT + NCTX
LB = NLAT // P
NB = T // P
HEAD = 64
DR = 512
DS = 512
NCT = DR // P
FF = 4 * D
G, GC, NS = 32, 16, 64
CH = 8
LC, CC = NLAT // CH, NCTX // CH
NC_ = LC + CC
SUP = 16
NSUP = NC_ // SUP
GB = 8
NBATCH = G // GB
TG = 3
TW = T // TG
OFF_R, OFF_K, OFF_V = 0, DR, 2 * DR
OFF_WD, OFF_AD, OFF_GD, OFF_U = 3 * DR, 3 * DR + 128, 3 * DR + 256, 3 * DR + 384
D_IN = OFF_U + DS
RMS_EPS, GN_EPS = 1e-6, 64e-5
NLEV = 6
DECAY = -math.exp(-0.5)


class Arena:

    def __init__(self, nc, words):
        self.t = nc.alloc_sbuf_tensor("arena", [P, words], F32)
        self.words, self.at = words, 0

    def take(self, *shape, dt=F32, parts=P):
        n = int(np.prod(shape))
        words = n if dt == F32 else (n + 1) // 2
        assert self.at + words <= self.words, (self.at, words, shape)
        v = self.t[0:parts, self.at:self.at + words]
        self.at += words
        if dt != F32:
            v = v.bitcast(dt)
        names = [f"d{i}" for i in range(len(shape))]
        if len(shape) > 1:
            v = v.rearrange(f"p ({' '.join(names)}) -> p {' '.join(names)}",
                            **{m: s for m, s in zip(names[1:], shape[1:])})
        return v


class Events:

    def __init__(self, nc, ctx, stage):
        self.nc, self.ctx, self.stage, self.sems = nc, ctx, stage, {}

    def __call__(self, name, *index):
        key = "_".join([self.stage, name, *map(str, index)])
        if key not in self.sems:
            self.sems[key] = self.ctx.enter_context(self.nc.semaphore(key))
        return self.sems[key]


def split_mm(nc, out, whi, wlo, xhi, xlo, first, last):
    nc.tensor.matmul(out, whi, xhi, start=first, stop=False)
    nc.tensor.matmul(out, wlo, xhi, start=False, stop=False)
    return nc.tensor.matmul(out, whi, xlo, start=False, stop=last)


def need(eng, sem, value):
    if not isinstance(value, int) or value > 0:
        eng.wait_ge(sem, value)


def rounds(eng, n, body):
    body(0)
    with eng.Fori(1, n) as i:
        body(i)


class Chain:

    def __init__(self, sem, base=0):
        self.sem, self.base, self.n = sem, base, 0

    def step(self, ins):
        ins.then_inc(self.sem, 1)
        self.n += 1
        return self.n

    def settle(self, eng):
        eng.wait_ge(self.sem, self.base + self.n)


def stage_modulation(nc, M, ins):
    A, ps = M.arena, M.ps
    keep = A.at
    cc = A.take(KD, 2)
    th = A.take(KD, 2)
    sc = A.take(KD, 2)
    wst = [A.take(KD, 512) for _ in range(2)]
    mod = A.take(6 * D, parts=2)
    bada = A.take(6 * D, parts=2)
    g12 = A.take(2, KD)
    with ExitStack() as ctx:
        ev = Events(nc, ctx, "mod")
        block = ctx.enter_context(nc.Block())

        @block.sync
        def _(sp):
            sp.dma_start(M.const[:, :], ins["consts"]).then_inc(ev("const"), 16)
            sp.dma_start(cc, ins["cond"]).then_inc(ev("cond"), 16)
            sp.dma_start(bada, ins["b_ada"]).then_inc(ev("bias"), 16)
            sp.dma_start(g12, ins["norm_g"]).then_inc(ev("bias"), 16)

            def load(q, j):
                sp.dma_start(wst[q], ins["w_ada"][:, :, ds(j * 512, 512)]).then_inc(ev("w_loaded", q), 16)
            load(0, 0)
            load(1, 1)
            with sp.Fori(0, 5) as i:
                for q in range(2):
                    sp.wait_ge(ev("products", q), i + 1)
                    load(q, i * 2 + (q + 2))
            for q in range(2):
                sp.wait_ge(ev("stored", q), 6)
            for n in range(2):
                sp.dma_start(ins["gates"][n], mod[0:2, (2 + 3 * n) * D:(3 + 3 * n) * D]).then_inc(ev("gates"), 16)
            sp.wait_ge(ev("gates"), 32)

        @block.scalar
        def _(act):
            act.wait_ge(ev("cond"), 16)
            nc.scalar.activation(th, cc, ACT.Tanh, scale=0.5).then_inc(ev("tanh"), 1)

        @block.tensor
        def _(pe):
            pe.wait_ge(ev("silu"), 1)

            def multiply(i):
                for q in range(2):
                    pe.wait_ge(ev("w_loaded", q), i * 16 + 16)
                    need(pe, ev("stored", q), i)
                    for k in range(KD):
                        last = nc.tensor.matmul(ps[0:2, q, :], sc[:, k, :], wst[q][:, k, :],
                                                start=(k == 0), stop=(k == KD - 1))
                    last.then_inc(ev("products", q), 1)
            rounds(pe, 6, multiply)
            for q in range(2):
                pe.wait_ge(ev("stored", q), 6)
            n = 0
            for part in (0, 1, 3, 4):
                for k in range(KD):
                    last = nc.tensor.transpose(ps[:, 2, 2 * n:2 * n + 2],
                                               mod[0:2, part * D + k * P:part * D + (k + 1) * P], M.ident[0:2, 0:2])
                    n += 1
            last.then_inc(ev("cols_t"), 1)

        @block.vector
        def _(dve):
            dve.wait_ge(ev("tanh"), 1)
            dve.wait_ge(ev("cond"), 16)
            nc.vector.scalar_tensor_tensor(out=sc, in0=th, scalar=1.0, in1=cc, op0=ALU.add,
                                           op1=ALU.mult).then_inc(ev("two_silu"), 1)
            dve.wait_ge(ev("two_silu"), 1)
            nc.vector.tensor_scalar(sc, sc, 0.5, None, ALU.mult).then_inc(ev("silu"), 1)
            dve.wait_ge(ev("bias"), 32)
            with dve.Fori(0, 6) as i:
                for q in range(2):
                    dve.wait_ge(ev("products", q), i + 1)
                    cols = ds((i * 2 + q) * 512, 512)
                    nc.vector.tensor_tensor(mod[0:2, cols], ps[0:2, q, :], bada[0:2, cols],
                                            ALU.add).then_inc(ev("stored", q), 1)
            dve.wait_ge(ev("cols_t"), 1)
            cols = ps[:, 2, 0:64].rearrange("p (q k w) -> p q k w", q=4, k=KD)
            for n in range(2):
                nc.vector.tensor_copy(M.shift[n], cols[:, 2 * n]).then_inc(ev("shift"), 1)
                nc.vector.scalar_tensor_tensor(out=M.scale[n], in0=cols[:, 2 * n + 1], scalar=1.0,
                                               in1=g12[:, n, :].unsqueeze(2).broadcast_to([P, KD, 2]),
                                               op0=ALU.add, op1=ALU.mult).then_inc(ev("scale"), 1)
    clear(nc, ev)
    A.at = keep


def stage_norm(nc, M, name, src, pos, which, hT):
    A, ps = M.arena, M.ps
    keep = A.at
    xt = [A.take(D) for _ in range(2)]
    pt = [A.take(D) for _ in range(2)]
    xn = [A.take(D) for _ in range(2)]
    hf = [A.take(KD, P) for _ in range(2)]
    ss = [A.take(1) for _ in range(2)]
    ms = [A.take(1) for _ in range(2)]
    rs = [A.take(1) for _ in range(2)]
    hi, lo = hT
    per_load = 32 if pos is not None else 16
    with ExitStack() as ctx:
        ev = Events(nc, ctx, name)
        block = ctx.enter_context(nc.Block())

        @block.sync
        def _(sp):
            def load(q, b):
                sp.dma_start(xt[q], src[ds(b, 1)].squeeze(0) if not isinstance(b, int) else src[b]).then_inc(ev("loaded", q), 16)
                if pos is not None:
                    sp.dma_start(pt[q], pos[ds(b, 1)].squeeze(0) if not isinstance(b, int) else pos[b]).then_inc(ev("loaded", q), 16)
            load(0, 0)
            load(1, 1)
            with sp.Fori(0, 3) as i:
                for q in range(2):
                    sp.wait_ge(ev("normed", q), i + 1)
                    load(q, i * 2 + (q + 2))
            sp.wait_ge(ev("normed", 0), 4)
            load(0, LB)

        @block.scalar
        def _(act):
            def norm(q, n):
                act.wait_ge(ev("added", q) if pos is not None else ev("loaded", q),
                            n + 1 if pos is not None else n * 16 + 16)
                need(act, ev("transposed", q), n)
                nc.scalar.activation(xn[q], xt[q], ACT.Square, accum_out=ss[q]).then_inc(ev("squares", q), 1)
                act.wait_ge(ev("squares", q), n + 1)
                nc.scalar.activation(ms[q], ss[q], ACT.Copy, scale=1.0 / D, bias=RMS_EPS).then_inc(ev("mean_sq", q), 1)
                act.wait_ge(ev("rstd", q), n + 1)
                nc.scalar.activation(xn[q], xt[q], ACT.Copy, scale=rs[q]).then_inc(ev("normed", q), 1)

            def high(q, n, b):
                act.wait_ge(ev("modulated", q), n + 1)
                nc.scalar.activation(hi[:, :, ds(b * P, P)], hf[q], ACT.Copy).then_inc(ev("high", q), 1)

            def two(i):
                norm(0, i)
                norm(1, i)
                high(0, i, i * 2)
                high(1, i, i * 2 + 1)
            rounds(act, 4, two)
            norm(0, 4)
            high(0, 4, LB)

        @block.gpsimd
        def _(pool):
            def rstd(q, n):
                pool.wait_ge(ev("mean_sq", q), n + 1)
                nc.gpsimd.tensor_tensor(rs[q], ms[q], M.neg_half, ALU.pow).then_inc(ev("rstd", q), 1)

            def low(q, n, b):
                pool.wait_ge(ev("high", q), n + 1)
                nc.gpsimd.tensor_tensor(lo[:, :, ds(b * P, P)], hf[q], hi[:, :, ds(b * P, P)],
                                        ALU.subtract).then_inc(ev("low", q), 1)
            with pool.Fori(0, 4) as i:
                rstd(0, i)
                rstd(1, i)
                low(0, i, i * 2)
                low(1, i, i * 2 + 1)
            rstd(0, 4)
            low(0, 4, LB)

        @block.tensor
        def _(pe):
            def turn(q, n):
                pe.wait_ge(ev("normed", q), n + 1)
                need(pe, ev("modulated", q), n)
                for k in range(KD):
                    last = nc.tensor.transpose(ps[:, 2 * q + k // 4, (k % 4) * P:(k % 4 + 1) * P],
                                               xn[q][:, k * P:(k + 1) * P], M.ident)
                last.then_inc(ev("transposed", q), 1)

            def two(i):
                turn(0, i)
                turn(1, i)
            rounds(pe, 4, two)
            turn(0, 4)

        @block.vector
        def _(dve):
            def add(q, n):
                if pos is not None:
                    dve.wait_ge(ev("loaded", q), n * per_load + per_load)
                    nc.vector.tensor_tensor(xt[q], xt[q], pt[q], ALU.add).then_inc(ev("added", q), 1)

            def modulate(q, n, w):
                dve.wait_ge(ev("transposed", q), n + 1)
                need(dve, ev("high", q), n)
                need(dve, ev("low", q), n)
                for k in range(KD):
                    last = nc.vector.tensor_scalar(hf[q][:, k, :], ps[:, 2 * q + k // 4, (k % 4) * P:(k % 4 + 1) * P],
                                                   M.scale[which][:, k, w:w + 1], M.shift[which][:, k, w:w + 1],
                                                   ALU.mult, ALU.add)
                last.then_inc(ev("modulated", q), 1)

            def two(i):
                add(0, i)
                add(1, i)
                modulate(0, i, 0)
                modulate(1, i, 0)
            rounds(dve, 4, two)
            add(0, 4)
            modulate(0, 4, 1)
    clear(nc, ev)
    A.at = keep


def clear(nc, ev):
    with nc.Block() as block:
        @block.gpsimd
        def _(pool):
            for s in ev.sems.values():
                pool.sem_clear(s)


def stage_u(nc, M, ins):
    A, ps = M.arena, M.ps
    keep = A.at
    wst = A.take(KD, DS)
    whi, wlo = A.take(KD, DS, dt=BF16), A.take(KD, DS, dt=BF16)
    u_lat = A.take(G, CH, GC)
    u_tok = A.take(DS)
    u_raw = A.take(CH, G, GC, parts=CC)
    u_ctx = A.take(G, CH, GC, parts=CC)
    with ExitStack() as ctx:
        ev = Events(nc, ctx, "u")
        block = ctx.enter_context(nc.Block())

        @block.sync
        def _(sp):
            sp.dma_start(wst, ins["w_in"][:, :, OFF_U:OFF_U + DS]).then_inc(ev("w"), 16)
            sp.wait_ge(ev("ctx_out"), 1)
            sp.dma_start(ins["u_bounce"], u_tok).then_inc(ev("bounced"), 16)
            sp.wait_ge(ev("bounced"), 16)
            sp.dma_start(u_raw.rearrange("c s g n -> c (s g n)"),
                         ins["u_bounce"].rearrange("(c s) n -> c (s n)", s=CH)).then_inc(ev("ctx_in"), 16)

        @block.scalar
        def _(act):
            act.wait_ge(ev("w"), 16)
            nc.scalar.activation(whi, wst, ACT.Copy).then_inc(ev("hi"), 1)
            act.wait_ge(ev("ctx_in"), 16)
            nc.scalar.activation(u_ctx, u_raw.rearrange("c s g n -> c g s n"), ACT.Copy).then_inc(ev("ctx"), 1)
            for g in range(0, G, 3):
                n = min(3, G - g)
                act.wait_ge(ev("turned"), g // 3 + 1)
                nc.scalar.activation(M.u[:, g:g + n, :], ps[:, 2 + g // 3 % 2, 0:n * NC_].rearrange("p (g c) -> p g c", g=n),
                                     ACT.Copy).then_inc(ev("u"), 1)

        @block.gpsimd
        def _(pool):
            pool.wait_ge(ev("hi"), 1)
            nc.gpsimd.tensor_tensor(wlo, wst, whi, ALU.subtract).then_inc(ev("lo"), 1)

        @block.tensor
        def _(pe):
            pe.wait_ge(ev("lo"), 1)

            def project(q, n, col):
                need(pe, ev("stored", q), n)
                for k in range(KD):
                    last = split_mm(nc, ps[:, q, :], M.hi[:, k, col], M.lo[:, k, col], whi[:, k, :], wlo[:, k, :],
                                    k == 0, k == KD - 1)
                last.then_inc(ev("product", q), 1)

            def two(i):
                for q in range(2):
                    project(q, i, ds(i * 2 + q, LC, CH))
            rounds(pe, CH // 2, two)
            project(0, CH // 2, slice(NLAT, T))
            pe.wait_ge(ev("stored", 1), CH // 2)
            pe.wait_ge(ev("stored", 0), CH // 2)
            pe.wait_ge(ev("ctx"), 1)
            for g in range(G):
                b = g // 3
                if g % 3 == 0 and b >= 2:
                    pe.wait_ge(ev("u"), b - 1)
                o = g % 3 * NC_
                nc.tensor.transpose(ps[:, 2 + b % 2, o:o + LC], u_lat[:, g].rearrange("p s c -> p (s c)"), M.ident)
                last = nc.tensor.transpose(ps[:, 2 + b % 2, o + LC:o + NC_], u_ctx[:, g].rearrange("p s c -> p (s c)"),
                                           M.ident[0:CC, 0:CC])
                if g % 3 == 2 or g == G - 1:
                    last.then_inc(ev("turned"), 1)

        @block.vector
        def _(dve):
            with dve.Fori(0, CH // 2) as i:
                for q in range(2):
                    dve.wait_ge(ev("product", q), i + 1)
                    nc.vector.tensor_copy(u_lat[:, :, ds(i * 2 + q, 1), :], ps[:, q, :].rearrange("p (g x c) -> p g x c", g=G, x=1)).then_inc(ev("stored", q), 1)
            dve.wait_ge(ev("product", 0), CH // 2 + 1)
            nc.vector.tensor_copy(u_tok, ps[:, 0, :]).then_inc(ev("ctx_out"), 1)
    clear(nc, ev)
    A.at = keep


def complex_product(ops, eng, c, out, a, b, t, neg_im=False, done=None):
    c.step(ops.tensor_tensor(t[0], a[0], b[0], ALU.mult))
    c.step(ops.tensor_tensor(t[1], a[1], b[1], ALU.mult))
    c.settle(eng)
    c.step(ops.tensor_tensor(out[0], t[0], t[1], ALU.subtract))
    c.settle(eng)
    c.step(ops.tensor_tensor(t[0], a[0], b[1], ALU.mult))
    c.step(ops.tensor_tensor(t[1], a[1], b[0], ALU.mult))
    c.settle(eng)
    if neg_im:
        last = ops.scalar_tensor_tensor(out=out[1], in0=t[0], scalar=-1.0, in1=t[1], op0=ALU.mult, op1=ALU.subtract)
    else:
        last = ops.tensor_tensor(out[1], t[0], t[1], ALU.add)
    if done is not None:
        last.then_inc(done, 1)
    else:
        c.step(last)
        c.settle(eng)


def stage_s5_tables(nc, M, ins):
    A, ps = M.arena, M.ps
    S = M.s5 = Memory()
    two = lambda *s: (A.take(*s), A.take(*s))
    S.in_table = two(CH, G)
    S.tap_table = two(2 * CH - 1, G)
    S.out_table = two(CH, G)
    S.sup_pow = two(SUP, G)
    S.chunk = two(G)
    S.sup = two(G)
    S.b = two(G, GC)
    S.c = two(G, GC)
    S.h0 = two(G)
    S.d = A.take(G, parts=GC)
    S.final = A.take(2, G)
    keep = A.at
    par = A.take(3, G)
    b_raw = two(G, GC)
    pw = two(CH + 1, G)
    lam, lim, ldt = (par[:, n, :] for n in range(3))
    dt, are, aim, mag, red, k1, den, q0, q1 = (A.take(G) for _ in range(9))
    sin, cos = A.take(G), A.take(G)
    power = A.take(G).bitcast(mybir.dt.int32)
    t = (A.take(G * SUP), A.take(G * SUP))
    with ExitStack() as ctx:
        ev = Events(nc, ctx, "s5t")
        block = ctx.enter_context(nc.Block())

        @block.sync
        def _(sp):
            for v, n in ((par, "ssm_par"), (b_raw[0], "ssm_b_re"), (b_raw[1], "ssm_b_im"), (S.c[0], "ssm_c_re"),
                         (S.c[1], "ssm_c_im"), (S.h0[0], "ssm_h_re"), (S.h0[1], "ssm_h_im"), (S.d, "ssm_d")):
                sp.dma_start(v, ins[n]).then_inc(ev("in"), 16)

        @block.vector
        def _(dve):
            c = Chain(ev("dve"))
            ts, tt, stt = nc.vector.tensor_scalar, nc.vector.tensor_tensor, nc.vector.scalar_tensor_tensor

            def op(ins_):
                c.step(ins_)
                c.settle(dve)

            def horner(v, x, coefficients):
                op(ts(v, x, coefficients[0], coefficients[1], ALU.mult, ALU.add))
                for a in coefficients[2:]:
                    op(tt(v, v, x, ALU.mult))
                    op(ts(v, v, a, None, ALU.add))

            def whole(v, x, scale):
                op(ts(v, x, scale, 12582912.0, ALU.mult, ALU.add))
                op(ts(v, v, 12582912.0, None, ALU.subtract))
            f32 = lambda x: float(np.float32(x))

            def exponential(v, x):
                whole(q0, x, 1.0 / math.log(2.0))
                op(ts(q0, q0, -126.0, 127.0, ALU.max, ALU.min))
                op(stt(out=q1, in0=q0, scalar=-0.693359375, in1=x, op0=ALU.mult, op1=ALU.add))
                op(stt(out=q1, in0=q0, scalar=2.12194440e-4, in1=q1, op0=ALU.mult, op1=ALU.add))
                horner(v, q1, [1 / math.factorial(n) for n in range(8, -1, -1)])
                op(ts(q0, q0, 127.0, None, ALU.add))
                op(ts(power, q0, 8388608.0, None, ALU.mult))
                op(tt(v, v, power.bitcast(F32), ALU.mult))
            dve.wait_ge(ev("in"), 8 * 16)
            exponential(dt, ldt)
            op(tt(aim, lim, dt, ALU.mult))
            op(tt(are, lam, dt, ALU.mult))
            exponential(mag, are)
            whole(q0, aim, 1.0 / (2 * math.pi))
            op(stt(out=red, in0=q0, scalar=-6.28125, in1=aim, op0=ALU.mult, op1=ALU.add))
            op(stt(out=red, in0=q0, scalar=-f32(2 * math.pi - 6.28125), in1=red, op0=ALU.mult, op1=ALU.add))
            op(stt(out=red, in0=q0, scalar=-f32(2 * math.pi - 6.28125 - f32(2 * math.pi - 6.28125)), in1=red,
                   op0=ALU.mult, op1=ALU.add))
            op(ts(red, red, 0.25, None, ALU.mult))
            op(tt(k1, red, red, ALU.mult))
            horner(sin, k1, [(-1) ** n / math.factorial(2 * n + 1) for n in range(5, -1, -1)])
            op(tt(sin, sin, red, ALU.mult))
            horner(cos, k1, [(-1) ** n / math.factorial(2 * n) for n in range(6, -1, -1)])
            for _ in range(2):
                op(tt(cos, cos, sin, ALU.mult))
                op(tt(q0, sin, sin, ALU.mult))
                op(ts(sin, cos, 2.0, None, ALU.mult))
                op(ts(cos, q0, -2.0, 1.0, ALU.mult, ALU.add))
            op(nc.vector.memset(pw[0][:, 0, :], 1.0))
            op(nc.vector.memset(pw[1][:, 0, :], 0.0))
            op(nc.vector.tensor_tensor(pw[0][:, 1, :], mag, cos, ALU.mult))
            op(nc.vector.tensor_tensor(pw[1][:, 1, :], mag, sin, ALU.mult))

            def powers(tab, known, upto):
                n = upto - known
                sc = [v[:, 0:n * G].rearrange("p (n g) -> p n g", n=n) for v in t]
                complex_product(nc.vector, dve, c, [v[:, known + 1:upto + 1, :] for v in tab], [v[:, 1:n + 1, :] for v in tab],
                                [v[:, known:known + 1, :].broadcast_to([P, n, G]) for v in tab], sc)
            powers(pw, 1, 2)
            powers(pw, 2, 4)
            powers(pw, 4, 8)
            for n in range(2):
                op(nc.vector.tensor_copy(S.chunk[n], pw[n][:, 8, :]))
                op(nc.vector.memset(S.sup_pow[n][:, 0, :], 1.0 - n))
                op(nc.vector.tensor_copy(S.sup_pow[n][:, 1, :], pw[n][:, 8, :]))
            powers(S.sup_pow, 1, 2)
            powers(S.sup_pow, 2, 4)
            powers(S.sup_pow, 4, 8)
            powers(S.sup_pow, 8, 15)
            sc = [v[:, 0:G] for v in t]
            complex_product(nc.vector, dve, c, S.sup, [v[:, 15, :] for v in S.sup_pow], S.chunk, sc)
            fwd, bwd = slice(0, 64), slice(64, P)
            for n in range(2):
                op(nc.vector.tensor_copy(S.in_table[n][fwd], pw[n][fwd, 7::-1, :]))
                op(nc.vector.tensor_copy(S.in_table[n][bwd], pw[n][bwd, 0:8, :]))
                op(nc.vector.memset(S.tap_table[n], 0.0))
                op(nc.vector.tensor_copy(S.tap_table[n][fwd, 7:15, :], pw[n][fwd, 0:8, :]))
                op(nc.vector.tensor_copy(S.tap_table[n][bwd, 0:8, :], pw[n][bwd, 7::-1, :]))
                op(nc.vector.tensor_copy(S.out_table[n][fwd], pw[n][fwd, 1:9, :]))
                op(nc.vector.tensor_copy(S.out_table[n][bwd], pw[n][bwd, 8:0:-1, :]))
            op(nc.vector.tensor_tensor(den, lam, lam, ALU.mult))
            op(nc.vector.tensor_tensor(q0, lim, lim, ALU.mult))
            op(nc.vector.tensor_tensor(den, den, q0, ALU.add))
            op(nc.vector.reciprocal(den, den))
            op(nc.vector.tensor_tensor(cos, lam, den, ALU.mult))
            op(nc.vector.tensor_tensor(sin, lim, den, ALU.mult))
            op(nc.vector.tensor_scalar(sin, sin, -1.0, None, ALU.mult))
            op(nc.vector.tensor_scalar(q0, pw[0][:, 1, :], 1.0, None, ALU.subtract))
            complex_product(nc.vector, dve, c, (k1, red), (q0, pw[1][:, 1, :]), (cos, sin), sc)
            sc = [v[:, 0:G * GC].rearrange("p (g c) -> p g c", g=G) for v in t]
            complex_product(nc.vector, dve, c, S.b, b_raw, [v.unsqueeze(2).broadcast_to([P, G, GC]) for v in (k1, red)], sc)
    clear(nc, ev)
    A.at = keep


def stage_s5(nc, M, ins, outs):
    A, ps, S = M.arena, M.ps, M.s5
    M.y_lat = A.take(CH, DS)
    keep = A.at
    y_ctx = A.take(CH, P, parts=CC)
    two = lambda *s: (A.take(*s), A.take(*s))
    bst = two(GB, GC)
    h = two(GB, CH, GC)
    f = two(GB, 2 * CH - 1, GC)
    gout = two(GB, CH, GC)
    wx = A.take(GB, 2, P)
    strip = A.take(GB, 2 * CH - 1, GC, parts=GC)
    toe = A.take(GB, P)
    uf = A.take(GB, NC_)
    xs = A.take(2, GB, NSUP, SUP)
    e = A.take(2, GB, NSUP)
    sn = A.take(2, GB, NC_)
    tv = two(GB * NC_)
    tg = two(GB // 2 * (2 * CH - 1) * GC)
    ta, tb = A.take(2, GB, NSUP), A.take(2, GB, NSUP)
    dd = A.take(GB, GC, parts=GC)
    fwd, bwd = slice(0, 64), slice(64, P)
    with ExitStack() as ctx:
        ev = Events(nc, ctx, "s5")
        block = ctx.enter_context(nc.Block())

        @block.sync
        def _(sp):
            with sp.Fori(0, NBATCH) as i:
                sp.wait_ge(ev("strip"), i + 1)
                for s in range(CH):
                    sp.dma_start(toe[s * GC:(s + 1) * GC, :, :].rearrange("p g (t c) -> p g t c", t=CH),
                                 strip[:, :, 7 - s:15 - s, :]).then_inc(ev("toeplitz"), 16)
                sp.wait_ge(ev("y_ctx"), i * 2 + 2)
                sp.dma_start(ins["y_bounce"].rearrange("(c t) n -> c t n", t=CH)[:, :, ds(i * P, P)], y_ctx).then_inc(ev("ctx_sent"), 16)
            sp.wait_ge(ev("ctx_sent"), NBATCH * 16)
            sp.wait_ge(ev("final"), NBATCH)
            sp.dma_start(outs["ssm"], S.final).then_inc(ev("out"), 16)
            sp.wait_ge(ev("out"), 16)

        @block.gpsimd
        def _(pool):
            HG = GB // 2
            nc.gpsimd.memset(tg[0][:, 0:1], 0.0).then_inc(ev("begun"), 1)
            def batch(i):
                pool.wait_ge(ev("begun"), 1)
                need(pool, ev("tap_bank"), i * 4)
                for half in range(2):
                    gs = ds(i * GB + half * HG, HG)
                    shape = [P, HG, 2 * CH - 1, GC]
                    b4 = [v[:, gs, :].unsqueeze(2).broadcast_to(shape) for v in S.c]
                    p4 = [v[:, :, gs].rearrange("p m g -> p g m").unsqueeze(3).broadcast_to(shape) for v in S.tap_table]
                    fh = [v[:, half * HG:(half + 1) * HG] for v in f]
                    sc = [v.rearrange("p (g m c) -> p g m c", g=HG, c=GC) for v in tg]
                    mult = lambda o, x, y: nc.gpsimd.tensor_tensor(o, x, y, ALU.mult)
                    mult(fh[0], b4[0], p4[0])
                    mult(fh[1], b4[0], p4[1])
                    mult(sc[0], b4[1], p4[1])
                    mult(sc[1], b4[1], p4[0]).then_inc(ev("f_products", half), 1)
                    pool.wait_ge(ev("f_products", half), i + 1)
                    nc.gpsimd.tensor_tensor(fh[0], fh[0], sc[0], ALU.subtract)
                    nc.gpsimd.tensor_tensor(fh[1], fh[1], sc[1], ALU.add).then_inc(ev("f_sums", half), 1)
                    pool.wait_ge(ev("f_sums", half), i + 1)
                    nc.gpsimd.tensor_tensor(fh[1], M.zero.unsqueeze(2).unsqueeze(3).broadcast_to(shape),
                                            fh[1], ALU.subtract).then_inc(ev("f"), 1)
            rounds(pool, NBATCH, batch)

        @block.scalar
        def _(act):
            def batch(i):
                gs = ds(i * GB, GB)
                need(act, ev("y_bank"), i * 4)
                nc.scalar.activation(uf, M.u[:, gs, :], ACT.Copy).then_inc(ev("staged"), 1)
                for n in range(2):
                    need(act, ev("tap_bank"), i * 4)
                    nc.scalar.activation(bst[n], S.b[n][:, gs, :], ACT.Copy).then_inc(ev("staged"), 1)
                for b in range(4):
                    act.wait_ge(ev("h_turned"), i * 4 + b + 1)
                    nc.scalar.activation(wx[:, 2 * b:2 * b + 2].rearrange("p g n l -> p (g n l)"), ps[:, b, :],
                                         ACT.Copy).then_inc(ev("wx"), 1)
                act.wait_ge(ev("sprev"), i * 2 + 2)
                xn = xs.rearrange("p n g s i -> p (n g) (s i)")
                so = sn.rearrange("p n g c -> p (n g) c")
                nc.scalar.activation(so[fwd], xn[fwd], ACT.Copy).then_inc(ev("natural"), 1)
                nc.scalar.activation(so[bwd, :, 0:LC], xn[bwd, :, 0:LC][:, :, ::-1], ACT.Copy).then_inc(ev("natural"), 1)
                nc.scalar.activation(so[bwd, :, LC:NC_], xn[bwd, :, LC:NC_][:, :, ::-1], ACT.Copy).then_inc(ev("natural"), 1)
                need(act, ev("ctx_sent"), i * 16)
                for b in range(2):
                    act.wait_ge(ev("y_bank"), i * 4 + 2 * b + 2)
                    nc.scalar.activation(y_ctx[:, :, 64 * b:64 * b + 64].rearrange("p t (g c) -> p g t c", g=4),
                                         ps[0:CC, 2 * b + 1, :].rearrange("p (g t c) -> p g t c", g=4, t=CH),
                                         ACT.Copy).then_inc(ev("y_ctx"), 1)
            rounds(act, NBATCH, batch)

        @block.tensor
        def _(pe):
            def batch(i):
                pe.wait_ge(ev("h"), i + 1)
                need(pe, ev("y_ctx"), i * 2)
                need(pe, ev("y_lat"), i * 2)
                for b in range(4):
                    for j in range(4):
                        last = nc.tensor.transpose(ps[:, b, j * P:(j + 1) * P],
                                                   h[j % 2][:, 2 * b + j // 2].rearrange("p s c -> p (s c)"), M.ident)
                    last.then_inc(ev("h_turned"), 1)
                pe.wait_ge(ev("f"), i * 2 + 2)
                pe.wait_ge(ev("staged"), i * 3 + 3)
                for b in range(4):
                    if b == 0:
                        need(pe, ev("x_read"), i * 6)
                        need(pe, ev("strip_read"), i * 4)
                    for j in range(2):
                        g = 2 * b + j
                        o = ps[0:GC, 4 + b, j * 256:j * 256 + 240]
                        for n in range(2):
                            last = nc.tensor.matmul(o, bst[n][:, g, :], f[n][:, g].rearrange("p m c -> p (m c)"),
                                                    start=(n == 0), stop=(n == 1))
                    last.then_inc(ev("tap_bank"), 1)
                pe.wait_ge(ev("wx"), i * 4 + 4)
                pe.wait_ge(ev("strip_read"), i * 4 + 4)
                for n in range(2):
                    for b in range(3):
                        for g in range(3 * b, min(3 * b + 3, GB)):
                            o = slice(g % 3 * NC_, (g % 3 + 1) * NC_)
                            nc.tensor.matmul(ps[fwd, 4 * n + b, o], wx[:, g, n, fwd], uf[:, g, :], start=True, stop=True)
                            mid = o.start + LC
                            nc.tensor.matmul(ps[bwd, 4 * n + b, o.start:mid], wx[:, g, n, bwd], uf[:, g, 0:LC][:, ::-1],
                                             start=True, stop=True)
                            last = nc.tensor.matmul(ps[bwd, 4 * n + b, mid:o.stop], wx[:, g, n, bwd],
                                                    uf[:, g, LC:NC_][:, ::-1], start=True, stop=True)
                        last.then_inc(ev("x_bank"), 1)
                pe.wait_ge(ev("x_read"), i * 6 + 6)
                pe.wait_ge(ev("natural"), i * 3 + 3)
                pe.wait_ge(ev("toeplitz"), i * (16 * CH) + 16 * CH)
                pe.wait_ge(ev("gout"), i + 1)
                for b in range(2):
                    for rows, bank in ((slice(0, LC), 2 * b), (slice(LC, NC_), 2 * b + 1)):
                        m = rows.stop - rows.start
                        for j in range(4):
                            g = 4 * b + j
                            o = ps[0:m, bank, j * P:(j + 1) * P]
                            nc.tensor.matmul(o, uf[:, g, rows], toe[:, g, :], start=True, stop=False)
                            nc.tensor.matmul(o, sn[:, 0, g, rows], gout[0][:, g].rearrange("p t c -> p (t c)"), start=False, stop=False)
                            last = nc.tensor.matmul(o, sn[:, 1, g, rows], gout[1][:, g].rearrange("p t c -> p (t c)"), start=False, stop=True)
                        last.then_inc(ev("y_bank"), 1)
            rounds(pe, NBATCH, batch)

        @block.vector
        def _(dve):
            K = S5_DVE_STEPS
            def batch(i):
                c = Chain(ev("dve"), i * K)
                gs = ds(i * GB, GB)

                def table(tab, n):
                    return [v[:, :, gs].rearrange("p m g -> p g m").unsqueeze(3).broadcast_to([P, GB, n, GC]) for v in tab]

                def mat(m, n):
                    return [v[:, gs, :].unsqueeze(2).broadcast_to([P, GB, n, GC]) for v in m]
                sc = [v[:, 0:GB * CH * GC].rearrange("p (g s c) -> p g s c", g=GB, s=CH) for v in tv]
                need(dve, ev("h_turned"), i * 4)
                complex_product(nc.vector, dve, c, h, mat(S.b, CH), table(S.in_table, CH), sc, done=ev("h"))
                dve.wait_ge(ev("h"), i + 1)
                need(dve, ev("y_bank"), i * 4)
                complex_product(nc.vector, dve, c, gout, mat(S.c, CH), table(S.out_table, CH), sc, neg_im=True,
                                done=ev("gout"))
                dve.wait_ge(ev("gout"), i + 1)
                need(dve, ev("toeplitz"), i * (16 * CH))
                c.step(nc.vector.tensor_tensor(dd, M.ident[0:GC, 0:GC].unsqueeze(1).broadcast_to([GC, GB, GC]),
                                               S.d[:, gs].unsqueeze(2).broadcast_to([GC, GB, GC]), ALU.mult))
                for b in range(4):
                    dve.wait_ge(ev("tap_bank"), i * 4 + b + 1)
                    src = ps[0:GC, 4 + b, :].rearrange("p (g x) -> p g x", g=2)[:, :, 0:240]
                    nc.vector.tensor_copy(strip[:, 2 * b:2 * b + 2].rearrange("p g m c -> p g (m c)"), src).then_inc(ev("strip_read"), 1)
                dve.wait_ge(ev("strip_read"), i * 4 + 4)
                c.settle(dve)
                nc.vector.tensor_tensor(strip[:, :, 7, :], strip[:, :, 7, :], dd, ALU.add).then_inc(ev("strip"), 1)
                need(dve, ev("natural"), i * 3)
                for n in range(2):
                    for b in range(3):
                        g0, g1 = 3 * b, min(3 * b + 3, GB)
                        dve.wait_ge(ev("x_bank"), i * 6 + 3 * n + b + 1)
                        nc.vector.tensor_copy(xs[:, n, g0:g1].rearrange("p g s i -> p (g s i)"),
                                              ps[:, 4 * n + b, 0:(g1 - g0) * NC_]).then_inc(ev("x_read"), 1)
                dve.wait_ge(ev("x_read"), i * 6 + 6)
                rot = lambda v, n: v[:, gs].unsqueeze(1).unsqueeze(3).broadcast_to([P, 2, GB, n])

                def advance(dst, src, lam, n):
                    a, b = ta[:, :, :, 0:n], tb[:, :, :, 0:n]
                    c.step(nc.vector.tensor_tensor(a, rot(lam[0], n), src, ALU.mult))
                    c.step(nc.vector.tensor_tensor(b, rot(lam[1], n), src, ALU.mult))
                    c.settle(dve)
                    c.step(nc.vector.tensor_tensor(dst, dst, a, ALU.add))
                    c.settle(dve)
                    c.step(nc.vector.tensor_tensor(dst[:, 0], dst[:, 0], b[:, 1], ALU.subtract))
                    c.step(nc.vector.tensor_tensor(dst[:, 1], dst[:, 1], b[:, 0], ALU.add))
                    c.settle(dve)
                for k in range(1, SUP):
                    advance(xs[:, :, :, :, k], xs[:, :, :, :, k - 1], S.chunk, NSUP)
                c.step(nc.vector.memset(e, 0.0))
                c.settle(dve)
                for n in range(2):
                    c.step(nc.vector.tensor_copy(e[:, n, :, 0], S.h0[n][:, gs]))
                c.step(nc.vector.tensor_copy(e[:, :, :, 1:NSUP - 1], xs[:, :, :, 0:NSUP - 2, SUP - 1]))
                nc.vector.tensor_copy(S.final[:, :, gs], xs[:, :, :, NSUP - 1, SUP - 1]).then_inc(ev("final"), 1)
                c.settle(dve)
                for j in range(NSUP - 2):
                    advance(e[:, :, :, j + 1:j + 2], e[:, :, :, j:j + 1], S.sup, 1)
                pos = lambda n: S.sup_pow[n][:, :, gs].rearrange("p i g -> p g i").unsqueeze(2).broadcast_to([P, GB, NSUP, SUP])
                est = lambda n: e[:, n].unsqueeze(3).broadcast_to([P, GB, NSUP, SUP])
                sc3 = [v.rearrange("p (g s i) -> p g s i", g=GB, s=NSUP) for v in tv]
                for n, (x0, x1, sign) in enumerate(((0, 0, ALU.subtract), (0, 1, ALU.add))):
                    c.step(nc.vector.tensor_tensor(sc3[0], pos(0), est(n), ALU.mult))
                    c.step(nc.vector.tensor_tensor(sc3[1], pos(1), est(1 - n), ALU.mult))
                    c.settle(dve)
                    c.step(nc.vector.tensor_tensor(sc3[0], sc3[0], sc3[1], sign))
                    c.settle(dve)
                    c.step(nc.vector.tensor_tensor(sc3[0][:, :, :, 1:SUP], sc3[0][:, :, :, 1:SUP],
                                                   xs[:, n, :, :, 0:SUP - 1], ALU.add))
                    c.settle(dve)
                    nc.vector.tensor_copy(xs[:, n], sc3[0]).then_inc(ev("sprev"), 1)
                    dve.wait_ge(ev("sprev"), i * 2 + n + 1)
                for b in range(2):
                    dve.wait_ge(ev("y_bank"), i * 4 + 2 * b + 1)
                    nc.vector.tensor_copy(M.y_lat[:, :, ds(i * P + 64 * b, 64)].rearrange("p t (g c) -> p g t c", g=4),
                                          ps[:, 2 * b, :].rearrange("p (g t c) -> p g t c", g=4, t=CH)).then_inc(ev("y_lat"), 1)
                assert c.n == K or K == 0, c.n
            rounds(dve, NBATCH, batch)

    clear(nc, ev)
    A.at = keep


S5_DVE_STEPS = 133


def stage_glu(nc, M, ins):
    A, ps = M.arena, M.ps
    keep = A.at
    K4 = DS // P
    wst = A.take(K4, DS)
    whi, wlo = A.take(K4, DS, dt=BF16), A.take(K4, DS, dt=BF16)
    bias = A.take(K4)
    y_nat = A.take(DS)
    yt = A.take(K4, T)
    g1 = A.take(K4, T)
    yhi, ylo = A.take(K4, T, dt=BF16), A.take(K4, T, dt=BF16)
    with ExitStack() as ctx:
        ev = Events(nc, ctx, "glu")
        block = ctx.enter_context(nc.Block())

        @block.sync
        def _(sp):
            sp.dma_start(wst, ins["w_glu"]).then_inc(ev("w"), 16)
            sp.dma_start(bias, ins["b_glu"]).then_inc(ev("w"), 16)
            sp.dma_start(y_nat, ins["y_bounce"]).then_inc(ev("ctx"), 16)

        @block.tensor
        def _(pe):
            for t in range(CH + 1):
                if t >= 2:
                    pe.wait_ge(ev("turned_read"), t - 1)
                if t == CH:
                    pe.wait_ge(ev("ctx"), 16)
                for k in range(K4):
                    src = M.y_lat[:, t, k * P:(k + 1) * P] if t < CH else y_nat[:, k * P:(k + 1) * P]
                    last = nc.tensor.transpose(ps[:, t % 2, k * P:(k + 1) * P], src, M.ident)
                last.then_inc(ev("turned"), 1)
            pe.wait_ge(ev("turned_read"), CH + 1)
            pe.wait_ge(ev("w_lo"), 1)
            pe.wait_ge(ev("y_lo"), K4)
            for o in range(K4):
                if o >= 2:
                    pe.wait_ge(ev("tanh_z"), o - 1)
                for g in range(TG):
                    for k in range(K4):
                        cols = slice(g * TW, (g + 1) * TW)
                        last = split_mm(nc, ps[:, 3 * (o % 2) + g, 0:TW], whi[:, k, o * P:(o + 1) * P],
                                        wlo[:, k, o * P:(o + 1) * P], yhi[:, k, cols], ylo[:, k, cols], k == 0, k == K4 - 1)
                last.then_inc(ev("z"), 1)

        @block.vector
        def _(dve):
            for t in range(CH + 1):
                dve.wait_ge(ev("turned"), t + 1)
                src = ps[:, t % 2, :].rearrange("p (k c) -> p k c", k=K4)
                dst = yt[:, :, t:NLAT:CH] if t < CH else yt[:, :, NLAT:T]
                nc.vector.tensor_copy(dst, src).then_inc(ev("turned_read"), 1)
            dve.wait_ge(ev("w"), 32)
            nc.vector.tensor_scalar(bias, bias, 0.5, None, ALU.mult).then_inc(ev("bias"), 1)
            c = Chain(ev("dve"))
            for k in range(K4):
                dve.wait_ge(ev("square"), k + 1)
                c.step(nc.vector.tensor_scalar(g1[:, k], g1[:, k], 0.044715, 1.0, ALU.mult, ALU.add))
                c.settle(dve)
                nc.vector.tensor_tensor(g1[:, k], g1[:, k], yt[:, k], ALU.mult).then_inc(ev("cubic"), 1)
            for k in range(K4):
                dve.wait_ge(ev("tanh"), k + 1)
                c.step(nc.vector.scalar_tensor_tensor(out=g1[:, k], in0=g1[:, k], scalar=1.0, in1=yt[:, k],
                                                      op0=ALU.add, op1=ALU.mult))
                c.settle(dve)
                nc.vector.tensor_scalar(yt[:, k], g1[:, k], 0.5, None, ALU.mult).then_inc(ev("gelu"), 1)
            for o in range(K4):
                dve.wait_ge(ev("tanh_z"), o + 1)
                c.step(nc.vector.tensor_scalar(g1[:, o], g1[:, o], 0.5, 0.5, ALU.mult, ALU.add))
                c.settle(dve)
                nc.vector.tensor_tensor(g1[:, o], g1[:, o], yt[:, o], ALU.mult).then_inc(ev("out"), 1)

        @block.scalar
        def _(act):
            act.wait_ge(ev("w"), 32)
            nc.scalar.activation(whi, wst, ACT.Copy).then_inc(ev("w_hi"), 1)
            act.wait_ge(ev("turned_read"), CH + 1)
            for k in range(K4):
                nc.scalar.activation(g1[:, k], yt[:, k], ACT.Square).then_inc(ev("square"), 1)
            for k in range(K4):
                act.wait_ge(ev("cubic"), k + 1)
                nc.scalar.activation(g1[:, k], g1[:, k], ACT.Tanh, scale=math.sqrt(2 / math.pi)).then_inc(ev("tanh"), 1)
            for k in range(K4):
                act.wait_ge(ev("gelu"), k + 1)
                nc.scalar.activation(yhi[:, k], yt[:, k], ACT.Copy).then_inc(ev("y_hi"), 1)
            act.wait_ge(ev("bias"), 1)
            for o in range(K4):
                act.wait_ge(ev("z"), o + 1)
                nc.scalar.activation(g1[:, o].rearrange("p (g c) -> p g c", g=TG), ps[:, 3 * (o % 2):3 * (o % 2) + 3, 0:TW],
                                     ACT.Tanh, bias=bias[:, o:o + 1], scale=0.5).then_inc(ev("tanh_z"), 1)
                act.wait_ge(ev("out"), o + 1)
                nc.scalar.activation(M.ys_hi[:, o], g1[:, o], ACT.Copy).then_inc(ev("out_hi"), 1)

        @block.gpsimd
        def _(pool):
            pool.wait_ge(ev("w_hi"), 1)
            nc.gpsimd.tensor_tensor(wlo, wst, whi, ALU.subtract).then_inc(ev("w_lo"), 1)
            for k in range(K4):
                pool.wait_ge(ev("y_hi"), k + 1)
                nc.gpsimd.tensor_tensor(ylo[:, k], yt[:, k], yhi[:, k], ALU.subtract).then_inc(ev("y_lo"), 1)
            for o in range(K4):
                pool.wait_ge(ev("out_hi"), o + 1)
                nc.gpsimd.tensor_tensor(M.ys_lo[:, o], g1[:, o], M.ys_hi[:, o], ALU.subtract).then_inc(ev("out_lo"), 1)
    clear(nc, ev)
    A.at = keep


def wide(ps, bank):
    return ps[:, bank:bank + TG, 0:TW]


def stage_lora(nc, M, ins):
    A, ps = M.arena, M.ps
    keep = A.at
    wst = A.take(KD, 3, P)
    whi, wlo = A.take(KD, 3, P, dt=BF16), A.take(KD, 3, P, dt=BF16)
    f = A.take(3, T)
    with ExitStack() as ctx:
        ev = Events(nc, ctx, "lora")
        block = ctx.enter_context(nc.Block())

        @block.sync
        def _(sp):
            sp.dma_start(wst.rearrange("p k a n -> p k (a n)"), ins["w_in"][:, :, OFF_WD:OFF_U]).then_inc(ev("w"), 16)

        @block.scalar
        def _(act):
            act.wait_ge(ev("w"), 16)
            nc.scalar.activation(whi, wst, ACT.Copy).then_inc(ev("w_hi"), 1)
            for n, (func, scale) in enumerate(((ACT.Tanh, 1.0), (ACT.Copy, 1.0), (ACT.Tanh, 0.5))):
                act.wait_ge(ev("z"), n + 1)
                nc.scalar.activation(f[:, n].rearrange("p (g c) -> p g c", g=TG), wide(ps, 3 * (n % 2)), func,
                                     scale=scale).then_inc(ev("f"), 1)
            for n in range(3):
                act.wait_ge(ev("f"), 3)
                if n == 2:
                    act.wait_ge(ev("sigmoid"), 1)
                nc.scalar.activation(M.lora_hi[:, n], f[:, n], ACT.Copy).then_inc(ev("hi"), 1)

        @block.gpsimd
        def _(pool):
            pool.wait_ge(ev("w_hi"), 1)
            nc.gpsimd.tensor_tensor(wlo, wst, whi, ALU.subtract).then_inc(ev("w_lo"), 1)
            for n in range(3):
                pool.wait_ge(ev("hi"), n + 1)
                nc.gpsimd.tensor_tensor(M.lora_lo[:, n], f[:, n], M.lora_hi[:, n], ALU.subtract).then_inc(ev("lo"), 1)

        @block.vector
        def _(dve):
            dve.wait_ge(ev("f"), 3)
            nc.vector.tensor_scalar(f[:, 2], f[:, 2], 0.5, 0.5, ALU.mult, ALU.add).then_inc(ev("sigmoid"), 1)

        @block.tensor
        def _(pe):
            pe.wait_ge(ev("w_lo"), 1)
            for n in range(3):
                if n == 2:
                    pe.wait_ge(ev("f"), 1)
                for g in range(TG):
                    cols = slice(g * TW, (g + 1) * TW)
                    for k in range(KD):
                        last = split_mm(nc, ps[:, 3 * (n % 2) + g, 0:TW], whi[:, k, n], wlo[:, k, n],
                                        M.hi[:, k, cols], M.lo[:, k, cols], k == 0, k == KD - 1)
                last.then_inc(ev("z"), 1)
    clear(nc, ev)
    A.at = keep


def stage_prepare(nc, M, ins, ct):
    A, ps, R = M.arena, M.ps, M.rwkv
    keep = A.at
    wst = A.take(KD, P)
    whi = [A.take(KD, P, dt=BF16) for _ in range(2)]
    wlo = [A.take(KD, P, dt=BF16) for _ in range(2)]
    up = A.take(3, P)
    r, k, kn, a, lw, c_, e, t = (A.take(T) for _ in range(8))
    m, tot, step = A.take(NB), A.take(NB), A.take(NB)
    hb = A.take(4)
    omka = A.take(1)
    par = R.par
    tiles = lambda v: v.rearrange("p (b t) -> p b t", b=NB)
    three = lambda v: v.rearrange("p (g c) -> p g c", g=TG)
    with ExitStack() as ctx:
        ev = Events(nc, ctx, "prep")
        block = ctx.enter_context(nc.Block())
        tt, ts, stt = nc.vector.tensor_tensor, nc.vector.tensor_scalar, nc.vector.scalar_tensor_tensor

        @block.sync
        def _(sp):
            sp.dma_start(par, ins["par"][ds(ct, 1)].squeeze(0)).then_inc(ev("par"), 16)
            sp.dma_start(up, ins["up"][ds(ct, 1)].squeeze(0)).then_inc(ev("up"), 16)
            for n, off in enumerate((OFF_R, OFF_K, OFF_V)):
                if n:
                    sp.wait_ge(ev("w_lo"), n)
                sp.dma_start(wst, ins["w_in"][:, :, ds(ct * P + off, P)]).then_inc(ev("w"), 16)

        @block.gpsimd
        def _(pool):
            pool.wait_ge(ev("up_hi"), 1)
            nc.gpsimd.tensor_tensor(R.up_lo, up, R.up_hi, ALU.subtract).then_inc(ev("up_lo"), 1)
            for n in range(3):
                pool.wait_ge(ev("w_hi"), n + 1)
                nc.gpsimd.tensor_tensor(wlo[n % 2], wst, whi[n % 2], ALU.subtract).then_inc(ev("w_lo"), 1)

        @block.tensor
        def _(pe):
            for n in range(2):
                pe.wait_ge(ev("w_lo"), n + 1)
                for g in range(TG):
                    cols = slice(g * TW, (g + 1) * TW)
                    for q in range(KD):
                        last = split_mm(nc, ps[:, 3 * n + g, 0:TW], whi[n][:, q], wlo[n][:, q],
                                        M.hi[:, q, cols], M.lo[:, q, cols], q == 0, q == KD - 1)
                last.then_inc(ev("rk"), 1)
            pe.wait_ge(ev("w_lo"), 3)
            for b in range(NB):
                if b == 8:
                    pe.wait_ge(ev("r"), 1)
                bank = (6, 7, 0)[b // 4]
                for q in range(KD):
                    cols = slice(b * P, (b + 1) * P)
                    last = split_mm(nc, ps[:, bank, b % 4 * P:(b % 4 + 1) * P], M.hi[:, q, cols], M.lo[:, q, cols],
                                    whi[0][:, q], wlo[0][:, q], q == 0, q == KD - 1)
                if b % 4 == 3 or b == 8:
                    last.then_inc(ev("v_bank"), 1)
            pe.wait_ge(ev("square"), 1)
            pe.wait_ge(ev("k"), 1)
            for g in range(TG):
                last = nc.tensor.matmul(ps[:, 3 + g, 0:TW], M.head_ones, e[:, g * TW:(g + 1) * TW], start=True, stop=True)
            last.then_inc(ev("norm"), 1)
            pe.wait_ge(ev("rkr"), 1)
            pe.wait_ge(ev("v"), 3)
            for b in range(NB):
                last = nc.tensor.matmul(ps[:, 6, 2 * b:2 * b + 2], c_[:, b * P:(b + 1) * P], M.head_ind, start=True, stop=True)
            last.then_inc(ev("bonus"), 1)
            pe.wait_ge(ev("up_lo"), 1)
            for d in range(2):
                rows = slice(64 * d, 64 * d + 64)
                for n in range(2):
                    if d == 0 and n == 1:
                        pe.wait_ge(ev("sqrt"), 1)
                    if d == 1:
                        pe.wait_ge(ev("tanh"), n + 1)
                    for g in range(TG):
                        cols = slice(g * TW, (g + 1) * TW)
                        last = split_mm(nc, ps[:, 3 * n + g, 0:TW], R.up_hi[rows, n], R.up_lo[rows, n],
                                        M.lora_hi[rows, n, cols], M.lora_lo[rows, n, cols], True, True)
                    last.then_inc(ev("lora"), 1)

        @block.scalar
        def _(act):
            act.wait_ge(ev("up"), 16)
            nc.scalar.activation(R.up_hi, up, ACT.Copy).then_inc(ev("up_hi"), 1)
            for n in range(3):
                act.wait_ge(ev("w"), 16 * n + 16)
                if n == 2:
                    act.wait_ge(ev("rk"), 1)
                nc.scalar.activation(whi[n % 2], wst, ACT.Copy).then_inc(ev("w_hi"), 1)
            act.wait_ge(ev("rk"), 1)
            nc.scalar.activation(three(r), wide(ps, 0), ACT.Copy).then_inc(ev("r"), 1)
            act.wait_ge(ev("kk"), 1)
            nc.scalar.activation(e, t, ACT.Square).then_inc(ev("square"), 1)
            for n, bank in enumerate((6, 7, 0)):
                act.wait_ge(ev("v_bank"), n + 1)
                w = 4 if n < 2 else 1
                nc.scalar.activation(R.v[:, 4 * n:4 * n + w, :].rearrange("p b c -> p (b c)"), ps[:, bank, 0:w * P],
                                     ACT.Copy).then_inc(ev("v"), 1)
            act.wait_ge(ev("norm"), 1)
            nc.scalar.activation(three(a), wide(ps, 3), ACT.Sqrt).then_inc(ev("sqrt"), 1)
            act.wait_ge(ev("bonus"), 1)
            nc.scalar.activation(R.bonus, ps[:, 6, 0:2 * NB], ACT.Copy).then_inc(ev("bonus_read"), 1)
            act.wait_ge(ev("half_bias"), 1)
            for d in range(2):
                if d == 1:
                    act.wait_ge(ev("x"), 4)
                else:
                    act.wait_ge(ev("kn"), 1)
                for n, v in enumerate((lw, a)):
                    act.wait_ge(ev("lora"), 2 * d + n + 1)
                    nc.scalar.activation(three(v), wide(ps, 3 * n), ACT.Tanh, bias=hb[:, 2 * n + d:2 * n + d + 1],
                                         scale=0.5).then_inc(ev("tanh"), 1)
                act.wait_ge(ev("sums"), d + 1)
                order = ((lw, 1.0), (c_, 1.0), (c_, -1.0)) if d == 0 else ((c_, -1.0), (lw, -1.0), (lw, 1.0))
                for n, (v, sign) in enumerate(order):
                    if n == 2:
                        act.wait_ge(ev("x"), 4 * d + 1)
                    nc.scalar.activation((e, t, e)[n], v, ACT.Exp, scale=sign).then_inc(ev("exp"), 1)
                nc.scalar.activation(R.pre[d] if d == 0 else R.post[d], m, ACT.Exp).then_inc(ev("edge"), 1)
                nc.scalar.activation(R.post[d] if d == 0 else R.pre[d], tot, ACT.Exp).then_inc(ev("edge"), 1)

        @block.vector
        def _(dve):
            c = Chain(ev("dve"))

            def op(ins_):
                c.step(ins_)
                c.settle(dve)
            dve.wait_ge(ev("par"), 16)
            op(ts(omka, par[:, 1:2], -1.0, 1.0, ALU.mult, ALU.add))
            ts(hb, par[:, 3:7], 0.5, None, ALU.mult).then_inc(ev("half_bias"), 1)
            dve.wait_ge(ev("rk"), 2)
            nc.vector.tensor_copy(three(k), wide(ps, 3)).then_inc(ev("k"), 1)
            dve.wait_ge(ev("k"), 1)
            ts(t, k, par[:, 0:1], None, ALU.mult).then_inc(ev("kk"), 1)
            dve.wait_ge(ev("r"), 1)
            stt(out=c_, in0=r, scalar=par[:, 2:3], in1=k, op0=ALU.mult, op1=ALU.mult).then_inc(ev("rkr"), 1)
            dve.wait_ge(ev("sqrt"), 1)
            op(ts(a, a, 1e-12, None, ALU.max))
            op(nc.vector.reciprocal(a, a))
            tt(kn, t, a, ALU.mult).then_inc(ev("kn"), 1)
            dve.wait_ge(ev("bonus"), 1)
            for d in range(2):
                x = R.x[d]
                dve.wait_ge(ev("tanh"), 2 * d + 2)
                c.step(ts(lw, lw, DECAY / 2, DECAY / 2, ALU.mult, ALU.add))
                c.step(ts(a, a, 0.5, 0.5, ALU.mult, ALU.add))
                c.settle(dve)
                if d == 1:
                    dve.wait_ge(ev("exp"), 3)
                    dve.wait_ge(ev("edge"), 2)
                for b in range(NB):
                    s = slice(b * P, (b + 1) * P)
                    c.step(nc.vector.tensor_tensor_scan(c_[:, s], M.one.broadcast_to([P, P]), lw[:, s], 0.0, ALU.mult, ALU.add))
                c.settle(dve)
                op(nc.vector.tensor_copy(m, tiles(c_)[:, :, 63]))
                op(tt(tiles(c_), tiles(c_), m.unsqueeze(2).broadcast_to([P, NB, P]), ALU.subtract))
                c.step(nc.vector.tensor_copy(tot, tiles(c_)[:, :, P - 1]))
                tt(lw, c_, lw, ALU.subtract).then_inc(ev("sums"), 1)
                dve.wait_ge(ev("sums"), d + 1)
                op(stt(out=x[:, :, 2, :], in0=tiles(kn), scalar=-1.0, in1=tiles(a), op0=ALU.mult, op1=ALU.mult))
                op(ts(x[:, :, 3, :], tiles(a), par[:, 1:2], omka, ALU.mult, ALU.add))
                op(tt(x[:, :, 3, :], x[:, :, 3, :], tiles(k), ALU.mult))
                for n, (src, v) in enumerate(((kn, e), (r, t))):
                    dve.wait_ge(ev("exp"), 3 * d + n + 1)
                    tt(x[:, :, n, :], tiles(src), tiles(v), ALU.mult).then_inc(ev("x"), 1)
                dve.wait_ge(ev("exp"), 3 * d + 3)
                for n in (2, 3):
                    tt(x[:, :, n, :], x[:, :, n, :], tiles(e), ALU.mult).then_inc(ev("x"), 1)
                dve.wait_ge(ev("edge"), 2 * d + 2)
                op(nc.vector.tensor_copy(step, R.post[d]))
                if d == 0:
                    op(tt(step[:, 0:LB - 1], R.post[d][:, 0:LB - 1], R.pre[d][:, 1:LB], ALU.mult))
                else:
                    op(tt(step[:, 1:LB], R.post[d][:, 1:LB], R.pre[d][:, 0:LB - 1], ALU.mult))
                op(tt(R.step[d], step.unsqueeze(2).broadcast_to([P, NB, 2]),
                      M.head_ind.unsqueeze(1).broadcast_to([P, NB, 2]), ALU.mult))
    clear(nc, ev)
    A.at = keep


def stage_chunks(nc, M, ins, outs, ct):
    A, ps, R = M.arena, M.ps, M.rwkv
    keep = A.at
    D2, H2 = range(2), range(2)
    double = lambda *shape: [[A.take(*shape) for _ in D2] for _ in range(2)]
    st = double(4, P)
    vs = double(P)
    tm = double(3, P)
    xx = double(2, 2, 64)
    ar = double(2, 2, P)
    mt = [[[A.take(2, 2, P) for _ in range(2)] for _ in D2] for _ in range(2)]
    lo = [A.take(2, NLEV - 1, 64) for _ in D2]
    qs = [A.take(2, 64) for _ in D2]
    rs = [A.take(2, 64) for _ in D2]
    u = [A.take(2, 64) for _ in D2]
    p = [A.take(2, 64) for _ in D2]
    pt = [A.take(2, 64) for _ in D2]
    enter = [A.take(2) for _ in D2]
    h0 = A.take(2, 64)
    fin = A.take(2, 64)
    half = [slice(0, 64), slice(64, P)]
    flat = lambda v: v.rearrange("p h c -> p (h c)")
    SPREAD, BESIDE = ((1, 0), (1, 1), (0, 0), (0, 1)), (1, 2)
    INV = lambda d: ps[:, 2 + d]
    REC = lambda d: ps[:, 4 + d]
    PROD = lambda d, j: ps[:, 6 * d + j]
    with ExitStack() as ctx:
        ev = Events(nc, ctx, "chunk")
        block = ctx.enter_context(nc.Block())

        def steps(eng, body, new=False, old=False):
            def known(s):
                latent = lambda t: (t, LB - 1 - t) if t >= 0 else (LB, LB)
                body(lambda o: s + o, s % 2, latent(s - 1) if s <= LB else None, latent(s - 2) if s else None)
            for s in range(3):
                known(s)
            with eng.Fori(1, LB // 2) as i:
                count = [eng.snap(i * 2 + o) for o in range(4)]
                for s in (1, 2):
                    tiles = [None, None]
                    for n, wanted in enumerate((new, old)):
                        tiles[n] = (eng.snap(i * 2 + (s - 1 - n)), eng.snap(LB - s + n - i * 2)) if wanted else (i, i)
                    body(lambda o, s=s: count[s + o], s % 2, *tiles)
            known(LB + 1)

        def first(eng):
            eng.wait_ge(ev("y_clear"), 1)

        @block.sync
        def _(sp):
            sp.dma_start(h0, ins["state"][ds(ct, 1)].squeeze(0)).then_inc(ev("h0"), 16)
            sp.wait_ge(ev("final"), 4)
            sp.dma_start(outs["rwkv"][ds(ct, 1)].squeeze(0), fin).then_inc(ev("out"), 16)
            sp.wait_ge(ev("out"), 16)

        @block.gpsimd
        def _(pool):
            nc.gpsimd.memset(R.y, 0.0).then_inc(ev("y_clear"), 1)
            for d in D2:
                nc.gpsimd.memset(p[d], 0.0).then_inc(ev("p_clear"), 1)

            def body(w, q, new, old):
                if not new:
                    return
                for d in D2:
                    first(pool)
                    need(pool, ev("rhs", d), w(-1))
                    nc.gpsimd.tensor_copy(st[q][d][:, 0:1], R.x[d][:, ds(new[d], 1), 0:1].rearrange("p b m t -> p (b m) t"))\
                        .then_inc(ev("st_a", d), 1)
                    nc.gpsimd.tensor_copy(st[q][d][:, 2:4], R.x[d][:, ds(new[d], 1), 2:4].rearrange("p b m t -> p (b m) t"))\
                        .then_inc(ev("st_bk", d), 1)
                for d in D2:
                    first(pool)
                    need(pool, ev("state", d), w(-1))
                    nc.gpsimd.tensor_copy(st[q][d][:, 1:2], R.x[d][:, ds(new[d], 1), 1:2].rearrange("p b m t -> p (b m) t"))\
                        .then_inc(ev("st_r", d), 1)
                    nc.gpsimd.tensor_copy(vs[q][d], R.v[:, ds(new[d], 1), :].rearrange("p b c -> p (b c)")).then_inc(ev("vs", d), 1)
                for d in D2:
                    first(pool)
                    pool.wait_ge(ev("turned_read", d), w(1))
                    need(pool, ev("q_last", d), w(0))
                    nc.gpsimd.tensor_tensor(lo[d], tm[q][d][:, 2].rearrange("p (h c) -> p h c", h=2).unsqueeze(2)
                                            .broadcast_to([P, 2, NLEV - 1, 64]),
                                            M.level_mask[:, d, 1:].unsqueeze(1).broadcast_to([P, 2, NLEV - 1, 64]), ALU.mult)\
                        .then_inc(ev("lo", d), 1)
            steps(pool, body, new=True)

        @block.tensor
        def _(pe):
            mm = nc.tensor.matmul

            def blocks(out, lhs, rhs):
                for b in range(2):
                    last = mm(out[half[b]], lhs[half[b]], rhs[half[b]], start=True, stop=True)
                return last

            def turn(w, q, d):
                first(pe)
                pe.wait_ge(ev("st_bk", d), w(1))
                need(pe, ev("x", d, NLEV - 1), w(0))
                pe.wait_ge(ev("ar_a", d), w(1))
                for j in range(2):
                    nc.tensor.transpose(INV(d)[:, j * P:(j + 1) * P], st[q][d][:, 2 + j], M.ident)
                for b in range(2):
                    last = mm(INV(d)[half[b], 2 * P:3 * P], st[q][d][:, 2, half[b]], ar[q][d][:, :, 0, half[b]],
                              start=True, stop=True)
                last.then_inc(ev("turned", d), 1)

            def score(w, q, d, j):
                first(pe)
                pe.wait_ge(ev("ar_r", d), w(1))
                need(pe, ev("masked", d, j), w(0))
                mm(PROD(d, j), st[q][d][:, 2 + j], ar[q][d].rearrange("p h m t -> p (h m t)"), start=True, stop=True)\
                    .then_inc(ev("scores", d, j), 1)

            def start_inverse(w, q, d):
                first(pe)
                pe.wait_ge(ev("xt0", d), w(1))
                pe.wait_ge(ev("turned_read", d), w(1))
                for h in H2:
                    last = blocks(INV(d)[:, 64 * h:64 * h + 64], xx[q][d][:, h, 1], M.ident64)
                last.then_inc(ev("x0", d), 1)

            def merge_q(w, q, d, l):
                first(pe)
                if l == 1:
                    pe.wait_ge(ev("lo", d), w(1))
                pe.wait_ge(ev("x", d, l - 1), w(1))
                for h in H2:
                    last = blocks(INV(d)[:, 64 * h:64 * h + 64], lo[d][:, h, l - 1], xx[q][d][:, h, 0])
                last.then_inc(ev("q", d, l) if l < NLEV - 1 else ev("q_last", d), 1)

            def merge_x(w, q, d, l):
                first(pe)
                pe.wait_ge(ev("q_read", d, l), w(1))
                for h in H2:
                    at = P + 128 * h
                    if l < NLEV - 1:
                        blocks(INV(d)[:, at:at + 64], xx[q][d][:, h, 1], qs[d][:, h])
                    last = blocks(INV(d)[:, at + 64:at + 128], qs[d][:, h], xx[q][d][:, h, 1])
                last.then_inc(ev("xq", d, l), 1)

            def right_side(w, q, d):
                first(pe)
                pe.wait_ge(ev("vs", d), w(0))
                need(pe, ev("p", d), w(-1))
                need(pe, ev("y_read", d), w(-1))
                pe.wait_ge(ev("x", d, NLEV - 1), w(0))
                mm(REC(d)[:, 0:P], st[q][d][:, 0], flat(p[d]), start=True, stop=False)
                for h in H2:
                    last = mm(REC(d)[:, half[h]], mt[q][d][1][:, h, 0], vs[q][d][:, half[h]], start=False, stop=h == 1)
                last.then_inc(ev("rhs", d), 1)

            def solve_first(w, q, d):
                F = half[d]
                first(pe)
                pe.wait_ge(ev("rhs_read", d), w(0))
                for h in H2:
                    last = mm(REC(d)[F, P + 64 * h:P + 64 * h + 64], xx[q][d][F, h, 1], rs[d][F, h], start=True, stop=True)
                last.then_inc(ev("u_head", d), 1)

            def carry(w, q, d):
                F, S = half[d], half[1 - d]
                first(pe)
                pe.wait_ge(ev("u_head_read", d), w(0))
                for h in H2:
                    last = mm(REC(d)[S, 256 + 64 * h:320 + 64 * h], mt[q][d][0][F, h, 0, S], u[d][F, h], start=True, stop=True)
                last.then_inc(ev("cross", d), 1)

            def solve_second(w, q, d):
                S = half[1 - d]
                first(pe)
                pe.wait_ge(ev("cross_read", d), w(0))
                for h in H2:
                    last = mm(REC(d)[S, 384 + 64 * h:448 + 64 * h], xx[q][d][S, h, 1], rs[d][S, h], start=True, stop=True)
                last.then_inc(ev("u_first", d), 1)

            def advance(w, q, d):
                first(pe)
                pe.wait_ge(ev("u_second_read", d), w(0))
                mm(REC(d)[:, 0:P], tm[q][d][:, 0], flat(u[d]), start=True, stop=False)
                mm(REC(d)[:, 0:P], tm[q][d][:, 1], vs[q][d], start=False, stop=True).then_inc(ev("p_sum", d), 1)

            def output(w, q, d):
                first(pe)
                pe.wait_ge(ev("p_read", d), w(0))
                mm(REC(d)[:, 0:P], st[q][d][:, 1], flat(p[d]), start=True, stop=False)
                for h in H2:
                    mm(REC(d)[:, half[h]], mt[q][d][0][:, h, 1], u[d][:, h], start=False, stop=False)
                    last = mm(REC(d)[:, half[h]], mt[q][d][1][:, h, 1], vs[q][d][:, half[h]], start=False,
                              stop=h == 1)
                last.then_inc(ev("state", d), 1)

            def body(w, q, new, old):
                o = 1 - q
                if new:
                    turn(w, q, 0)
                    turn(w, q, 1)
                if old:
                    right_side(w, o, 0)
                    right_side(w, o, 1)
                for d, j in SPREAD[:2] if old else SPREAD:
                    if new:
                        score(w, q, d, j)
                if old:
                    solve_first(w, o, 0)
                    solve_first(w, o, 1)
                if new:
                    start_inverse(w, q, 0)
                    start_inverse(w, q, 1)
                for l in range(1, NLEV):
                    beside = (None, carry, solve_second, advance, output, None)[l]
                    if new:
                        merge_q(w, q, 0, l)
                        merge_q(w, q, 1, l)
                        if old and l in BESIDE:
                            score(w, q, *SPREAD[2 + BESIDE.index(l)])
                    if old and beside:
                        beside(w, o, 0)
                    if new:
                        merge_x(w, q, 0, l)
                        merge_x(w, q, 1, l)
                    if old and beside:
                        beside(w, o, 1)
            pe.wait_ge(ev("p_clear"), 2)
            steps(pe, body)

        @block.scalar
        def _(act):
            def add_r(w, q, d):
                act.wait_ge(ev("st_r", d), w(1))
                for h in H2:
                    last = nc.scalar.activation(ar[q][d][half[h], h, 1], st[q][d][half[h], 1], ACT.Copy)
                last.then_inc(ev("ar_r", d), 1)

            def body(w, q, new, old):
                if new:
                    for d in D2:
                        act.wait_ge(ev("st_a", d), w(1))
                        for h in H2:
                            last = nc.scalar.activation(ar[q][d][half[h], h, 0], st[q][d][half[h], 0], ACT.Copy)
                        last.then_inc(ev("ar_a", d), 1)
                    for d in D2:
                        act.wait_ge(ev("turned", d), w(1))
                        nc.scalar.activation(tm[q][d].rearrange("p m t -> p (m t)"), INV(d)[:, 0:3 * P], ACT.Copy)\
                            .then_inc(ev("turned_read", d), 1)
                    add_r(w, q, 1)
                if old:
                    for d in D2:
                        act.wait_ge(ev("rhs", d), w(0))
                        nc.scalar.activation(flat(rs[d]), REC(d)[:, 0:P], ACT.Copy).then_inc(ev("rhs_read", d), 1)
                if new:
                    add_r(w, q, 0)
                    for d in D2:
                        act.wait_ge(ev("x0", d), w(1))
                        nc.scalar.activation(xx[q][d][:, :, 0, :], INV(d)[:, 0:P].rearrange("p (h c) -> p h c", h=2), ACT.Copy)\
                            .then_inc(ev("x", d, 0), 1)
                    for l in range(1, NLEV):
                        for d in D2:
                            act.wait_ge(ev("q", d, l) if l < NLEV - 1 else ev("q_last", d), w(1))
                            nc.scalar.activation(flat(qs[d]), INV(d)[:, 0:P], ACT.Copy).then_inc(ev("q_read", d, l), 1)
            act.wait_ge(ev("ar_clear"), 4)
            steps(act, body)

        @block.vector
        def _(dve):
            tt = nc.vector.tensor_tensor
            for q in range(2):
                for d in D2:
                    nc.vector.memset(ar[q][d], 0.0).then_inc(ev("ar_clear"), 1)
            for d in D2:
                begin = (0, LB - 1)[d]
                tt(enter[d], M.head_ind, R.pre[d][:, begin:begin + 1].broadcast_to([P, 2]), ALU.mult).then_inc(ev("enter"), 1)
            dve.wait_ge(ev("y_clear"), 1)
            dve.wait_ge(ev("h0"), 16)

            def mask(w, q, d, j):
                dve.wait_ge(ev("scores", d, j), w(1))
                tt(mt[q][d][j].rearrange("p h m t -> p (h m) t"), PROD(d, j).rearrange("p (m t) -> p m t", m=4),
                   M.score_mask[:, d], ALU.mult).then_inc(ev("masked", d, j), 1)

            def first_read(w, d, tile):
                F = half[d]
                dve.wait_ge(ev("u_head", d), w(0))
                nc.vector.tensor_copy(flat(u[d][F]), REC(d)[F, P:2 * P]).then_inc(ev("u_head_read", d), 1)

            def carried(w, d, tile):
                S = half[1 - d]
                dve.wait_ge(ev("cross", d), w(0))
                tt(flat(rs[d][S]), flat(rs[d][S]), REC(d)[S, 2 * P:3 * P], ALU.add).then_inc(ev("cross_read", d), 1)

            def second_read(w, d, tile):
                S = half[1 - d]
                dve.wait_ge(ev("u_first", d), w(0))
                nc.vector.tensor_copy(flat(u[d][S]), REC(d)[S, 3 * P:4 * P]).then_inc(ev("u_second_read", d), 1)

            def advanced(w, d, tile):
                dve.wait_ge(ev("p_sum", d), w(0))
                tt(flat(pt[d]), REC(d)[:, 0:P], flat(p[d]), ALU.add).then_inc(ev("p_read", d), 1)

            def put_out(w, d, tile):
                first(dve)
                dve.wait_ge(ev("state", d), w(0))
                dve.wait_ge(ev("p_read", d), w(0))
                if isinstance(tile[d], int) and tile[d] == LB:
                    for h in H2:
                        nc.vector.tensor_scalar(fin[half[h], d], pt[d][half[h], h], R.post[d][half[h], LB:LB + 1], None, ALU.mult)\
                            .then_inc(ev("final"), 1)
                    dve.wait_ge(ev("enter"), 2)
                    tt(p[d], h0[:, d].unsqueeze(1).broadcast_to([P, 2, 64]), enter[d].unsqueeze(2).broadcast_to([P, 2, 64]),
                       ALU.mult).then_inc(ev("p", d), 1)
                else:
                    tt(p[d], pt[d], R.step[d][:, ds(tile[d], 1), :].rearrange("p b h -> p (b h)").unsqueeze(2)
                       .broadcast_to([P, 2, 64]), ALU.mult).then_inc(ev("p", d), 1)
                first(dve)
                if d == 1:
                    dve.wait_ge(ev("y_read", 0), w(0))
                need(dve, ev("y_read", 1), w(-1))
                y = R.y[:, ds(tile[d], 1), :].rearrange("p b (h c) -> p (b h) c", h=2)
                tt(y, y, REC(d)[:, 0:P].rearrange("p (h c) -> p h c", h=2), ALU.add).then_inc(ev("y_read", d), 1)

            def body(w, q, new, old):
                if new:
                    for d in D2:
                        xt = xx[q][d][:, :, 1, :]
                        dve.wait_ge(ev("turned_read", d), w(1))
                        tt(xt, tm[q][d][:, 2].rearrange("p (h c) -> p h c", h=2),
                           M.level_mask[:, d, 0:1].broadcast_to([P, 2, 64]), ALU.mult).then_inc(ev("xt_masked", d), 1)
                        dve.wait_ge(ev("xt_masked", d), w(1))
                        tt(xt, xt, M.ident64.unsqueeze(1).broadcast_to([P, 2, 64]), ALU.add).then_inc(ev("xt0", d), 1)
                    for d, j in SPREAD[:2] if old else SPREAD:
                        mask(w, q, d, j)
                if old:
                    first_read(w, 0, old)
                    first_read(w, 1, old)
                for l in range(1, NLEV):
                    beside = (None, carried, second_read, advanced, put_out, None)[l]
                    if old and beside:
                        beside(w, 0, old)
                    if new:
                        for d in D2:
                            dve.wait_ge(ev("xq", d, l), w(1))
                            z = INV(d)[:, P:3 * P].rearrange("p (h m c) -> p h m c", h=2, m=2)
                            ms = slice(0, 2) if l < NLEV - 1 else slice(1, 2)
                            xd = xx[q][d][:, :, ms]
                            tt(xd, xd, z[:, :, ms], ALU.add).then_inc(ev("x", d, l), 1)
                    if old and beside:
                        beside(w, 1, old)
                    if new and old and l in BESIDE:
                        mask(w, q, *SPREAD[2 + BESIDE.index(l)])
            steps(dve, body, old=True)
    clear(nc, ev)
    A.at = keep


def stage_finish(nc, M, ins, ct):
    A, ps, R = M.arena, M.ps, M.rwkv
    keep = A.at
    NH = 2 * NB
    g = A.take(NB, P)
    t = A.take(NB, P)
    ln = A.take(2, P)
    mean, var, rstd = A.take(NH), A.take(NH), A.take(NH)
    yt = A.take(T)
    y = R.y
    heads = lambda v: v.rearrange("p b (h c) -> p (b h) c", h=2)
    row = lambda n: ln[:, n:n + 1, :].broadcast_to([P, NB, P])
    each = lambda v: v.unsqueeze(2).broadcast_to([P, NH, HEAD])
    with ExitStack() as ctx:
        ev = Events(nc, ctx, "fin")
        block = ctx.enter_context(nc.Block())
        tt, ts = nc.vector.tensor_tensor, nc.vector.tensor_scalar

        @block.sync
        def _(sp):
            sp.dma_start(ln, ins["ln"][ds(ct, 1)].squeeze(0)).then_inc(ev("ln"), 16)

        @block.tensor
        def _(pe):
            for b in range(NB):
                cols = slice(b * P, (b + 1) * P)
                last = split_mm(nc, ps[:, b // 4, b % 4 * P:(b % 4 + 1) * P], M.lora_hi[:, 2, cols], M.lora_lo[:, 2, cols],
                                R.up_hi[:, 2], R.up_lo[:, 2], True, True)
                if b % 4 == 3 or b == NB - 1:
                    last.then_inc(ev("gate"), 1)
            pe.wait_ge(ev("y"), 1)
            for b in range(NB):
                last = nc.tensor.transpose(ps[:, 4 + b // 4, b % 4 * P:(b % 4 + 1) * P], y[:, b], M.ident)
                if b % 4 == 3 or b == NB - 1:
                    last.then_inc(ev("turned"), 1)

        @block.scalar
        def _(act):
            for n in range(3):
                w = 4 if n < 2 else 1
                act.wait_ge(ev("gate"), n + 1)
                nc.scalar.activation(g[:, 4 * n:4 * n + w].rearrange("p b c -> p (b c)"), ps[:, n, 0:w * P], ACT.Copy)\
                    .then_inc(ev("gate_read"), 1)
            act.wait_ge(ev("centred"), 1)
            nc.scalar.activation(t, y, ACT.Square).then_inc(ev("square"), 1)
            act.wait_ge(ev("turned_read"), 3)
            nc.scalar.activation(M.yr_hi[:, ds(ct, 1)].rearrange("p a t -> p (a t)"), yt, ACT.Copy).then_inc(ev("hi"), 1)

        @block.gpsimd
        def _(pool):
            pool.wait_ge(ev("var"), 1)
            nc.gpsimd.tensor_tensor(rstd, var, M.neg_half.broadcast_to([P, NH]), ALU.pow).then_inc(ev("rstd"), 1)
            pool.wait_ge(ev("hi"), 1)
            nc.gpsimd.tensor_tensor(M.yr_lo[:, ds(ct, 1)].rearrange("p a t -> p (a t)"), yt,
                                    M.yr_hi[:, ds(ct, 1)].rearrange("p a t -> p (a t)"), ALU.subtract).then_inc(ev("lo"), 1)

        @block.vector
        def _(dve):
            c = Chain(ev("dve"))

            def op(ins_):
                c.step(ins_)
                c.settle(dve)
            op(nc.vector.reduce_sum(mean, heads(y), mybir.AxisListType.X))
            op(ts(mean, mean, 1.0 / HEAD, None, ALU.mult))
            tt(heads(y), heads(y), each(mean), ALU.subtract).then_inc(ev("centred"), 1)
            dve.wait_ge(ev("square"), 1)
            op(nc.vector.reduce_sum(var, heads(t), mybir.AxisListType.X))
            ts(var, var, 1.0 / HEAD, GN_EPS, ALU.mult, ALU.add).then_inc(ev("var"), 1)
            dve.wait_ge(ev("rstd"), 1)
            c.step(tt(heads(t), heads(R.v), each(R.bonus), ALU.mult))
            op(tt(heads(y), heads(y), each(rstd), ALU.mult))
            dve.wait_ge(ev("ln"), 16)
            op(tt(y, y, row(0), ALU.mult))
            op(tt(y, y, row(1), ALU.add))
            op(tt(y, y, t, ALU.add))
            dve.wait_ge(ev("gate_read"), 3)
            tt(y, y, g, ALU.mult).then_inc(ev("y"), 1)
            for n in range(3):
                w = (4 if n < 2 else 1) * P
                dve.wait_ge(ev("turned"), n + 1)
                nc.vector.tensor_copy(yt[:, 4 * n * P:4 * n * P + w], ps[:, 4 + n, 0:w]).then_inc(ev("turned_read"), 1)
    clear(nc, ev)
    A.at = keep


def stage_rwkv(nc, M, ins, outs):
    A = M.arena
    R = M.rwkv = Memory()
    M.yr_hi, M.yr_lo = A.take(NCT, T, dt=BF16), A.take(NCT, T, dt=BF16)
    keep = A.at
    M.lora_hi, M.lora_lo = A.take(3, T, dt=BF16), A.take(3, T, dt=BF16)
    stage_lora(nc, M, ins)
    R.x = [A.take(NB, 4, P) for _ in range(2)]
    R.v, R.y = A.take(NB, P), A.take(NB, P)
    R.bonus = A.take(2 * NB)
    R.pre, R.post = ([A.take(NB) for _ in range(2)] for _ in range(2))
    R.step = [A.take(NB, 2) for _ in range(2)]
    R.par = A.take(7)
    R.up_hi, R.up_lo = A.take(3, P, dt=BF16), A.take(3, P, dt=BF16)
    with nc.Fori(0, NCT) as ct:
        stage_prepare(nc, M, ins, ct)
        stage_chunks(nc, M, ins, outs, ct)
        stage_finish(nc, M, ins, ct)
    A.at = keep


def pairs(eng, body):
    def two(i):
        body(0, i, i * 2, 0)
        body(1, i, i * 2 + 1, 0)
    rounds(eng, LB // 2, two)
    body(0, LB // 2, LB, 1)


def stage_out(nc, M, ins):
    A, ps = M.arena, M.ps
    keep = A.at
    wst = A.take(KD, 512)
    whi = [A.take(KD, 512, dt=BF16) for _ in range(2)]
    wlo = [A.take(KD, 512, dt=BF16) for _ in range(2)]
    gate = A.take(2, D)
    xt, pt, t = ([A.take(D) for _ in range(2)] for _ in range(3))
    with ExitStack() as ctx:
        ev = Events(nc, ctx, "out")
        block = ctx.enter_context(nc.Block())

        @block.sync
        def _(sp):
            sp.dma_start(gate, ins["gates"][0].partition_broadcast(P)).then_inc(ev("gate"), 16)
            for h in range(2):
                if h:
                    sp.wait_ge(ev("w_lo"), 1)
                sp.dma_start(wst, ins["w_out"][:, :, h * 512:(h + 1) * 512]).then_inc(ev("w"), 16)

            def tile(q, n, b, w):
                need(sp, ev("stored", q), n * 16)
                sp.dma_start(xt[q], ins["x"][ds(b, 1)].squeeze(0)).then_inc(ev("x", q), 16)
                sp.dma_start(pt[q], ins["pos"][ds(b, 1)].squeeze(0)).then_inc(ev("x", q), 16)
            pairs(sp, tile)

        @block.scalar
        def _(act):
            for h in range(2):
                act.wait_ge(ev("w"), 16 * h + 16)
                nc.scalar.activation(whi[h], wst, ACT.Copy).then_inc(ev("w_hi"), 1)

            def tile(q, n, b, w):
                act.wait_ge(ev("sum", q), n + 1)
                act.dma_start(ins["x1"][ds(b, 1)].squeeze(0), xt[q]).then_inc(ev("stored", q), 16)
            pairs(act, tile)
            act.wait_ge(ev("stored", 0), 16 * 5)
            act.wait_ge(ev("stored", 1), 16 * 4)

        @block.gpsimd
        def _(pool):
            for h in range(2):
                pool.wait_ge(ev("w_hi"), h + 1)
                nc.gpsimd.tensor_tensor(wlo[h], wst, whi[h], ALU.subtract).then_inc(ev("w_lo"), 1)

            def tile(q, n, b, w):
                pool.wait_ge(ev("x", q), n * 32 + 32)
                nc.gpsimd.tensor_tensor(xt[q], xt[q], pt[q], ALU.add).then_inc(ev("x_pos", q), 1)
            pairs(pool, tile)

        @block.tensor
        def _(pe):
            pe.wait_ge(ev("w_lo"), 2)

            def tile(q, n, b, w):
                need(pe, ev("gated", q), n)
                cols = ds(b * P, P)
                for h in range(2):
                    for k in range(KD):
                        hi, lo = (M.yr_hi, M.yr_lo) if k < NCT else (M.ys_hi, M.ys_lo)
                        last = split_mm(nc, ps[:, 2 * q + h, :], hi[:, k % NCT, cols], lo[:, k % NCT, cols],
                                        whi[h][:, k], wlo[h][:, k], k == 0, k == KD - 1)
                last.then_inc(ev("product", q), 1)
            pairs(pe, tile)

        @block.vector
        def _(dve):
            dve.wait_ge(ev("gate"), 16)

            def tile(q, n, b, w):
                dve.wait_ge(ev("product", q), n + 1)
                need(dve, ev("sum", q), n)
                nc.vector.tensor_tensor(t[q].rearrange("p (h c) -> p h c", h=2), ps[:, 2 * q:2 * q + 2, :],
                                        gate[:, w].rearrange("p (h c) -> p h c", h=2), ALU.mult).then_inc(ev("gated", q), 1)
                dve.wait_ge(ev("x_pos", q), n + 1)
                dve.wait_ge(ev("gated", q), n + 1)
                nc.vector.tensor_tensor(xt[q], xt[q], t[q], ALU.add).then_inc(ev("sum", q), 1)
            pairs(dve, tile)
    clear(nc, ev)
    A.at = keep


def stage_mlp(nc, M, ins):
    A, ps = M.arena, M.ps
    FW = 512
    ROUNDS, O = FF // FW, FW // P
    M.acc = A.take(NB, D)
    keep = A.at
    w1s = A.take(KD, FW)
    w2s = A.take(O, D)
    w1hi, w1lo = A.take(KD, FW, dt=BF16), A.take(KD, FW, dt=BF16)
    w2hi, w2lo = A.take(O, D, dt=BF16), A.take(O, D, dt=BF16)
    f = [A.take(T) for _ in range(2)]
    hhi, hlo = A.take(O, T, dt=BF16), A.take(O, T, dt=BF16)
    with ExitStack() as ctx:
        ev = Events(nc, ctx, "mlp")
        block = ctx.enter_context(nc.Block())

        @block.sync
        def _(sp):
            def load1(j):
                sp.dma_start(w1s, ins["w_ff1"][:, :, ds(j * FW, FW)]).then_inc(ev("w1"), 16)

            def load2(j):
                sp.dma_start(w2s, ins["w_ff2"][:, ds(j * O, O), :]).then_inc(ev("w2"), 16)
            load1(0)
            load2(0)
            with sp.Fori(0, ROUNDS - 1) as j:
                sp.wait_ge(ev("w1_lo"), j + 1)
                load1(j + 1)
                sp.wait_ge(ev("w2_lo"), j + 1)
                load2(j + 1)

        @block.gpsimd
        def _(pool):
            nc.gpsimd.memset(M.acc, 0.0).then_inc(ev("acc_clear"), 1)
            with pool.Fori(0, ROUNDS) as j:
                pool.wait_ge(ev("w1_hi"), j + 1)
                nc.gpsimd.tensor_tensor(w1lo, w1s, w1hi, ALU.subtract).then_inc(ev("w1_lo"), 1)
                pool.wait_ge(ev("w2_hi"), j + 1)
                nc.gpsimd.tensor_tensor(w2lo, w2s, w2hi, ALU.subtract).then_inc(ev("w2_lo"), 1)

        @block.scalar
        def _(act):
            def split1(j):
                act.wait_ge(ev("w1"), j * 16 + 16)
                nc.scalar.activation(w1hi, w1s, ACT.Copy).then_inc(ev("w1_hi"), 1)

            def body(j, more):
                act.wait_ge(ev("w2"), j * 16 + 16)
                need(act, ev("ff2"), j * (2 * NB))
                nc.scalar.activation(w2hi, w2s, ACT.Copy).then_inc(ev("w2_hi"), 1)
                for o in range(O):
                    act.wait_ge(ev("ff1"), j * O + (o + 1))
                    if o >= 2:
                        act.wait_ge(ev("h_lo"), j * O + (o - 1))
                    else:
                        need(act, ev("h_lo"), j * O)
                    nc.scalar.activation(f[o % 2].rearrange("p (g c) -> p g c", g=TG), wide(ps, 3 * (o % 2)),
                                         ACT.Relu).then_inc(ev("relu"), 1)
                    act.wait_ge(ev("square"), j * O + (o + 1))
                    nc.scalar.activation(hhi[:, o], f[o % 2], ACT.Copy).then_inc(ev("h_hi"), 1)
                if more:
                    split1(j + 1)
            split1(0)
            rounds(act, ROUNDS - 1, lambda j: body(j, True))
            body(ROUNDS - 1, False)

        @block.vector
        def _(dve):
            dve.wait_ge(ev("acc_clear"), 1)
            with dve.Fori(0, ROUNDS) as j:
                for o in range(O):
                    dve.wait_ge(ev("relu"), j * O + (o + 1))
                    nc.vector.tensor_tensor(f[o % 2], f[o % 2], f[o % 2], ALU.mult).then_inc(ev("square"), 1)
                    dve.wait_ge(ev("h_hi"), j * O + (o + 1))
                    nc.vector.tensor_tensor(hlo[:, o], f[o % 2], hhi[:, o], ALU.subtract).then_inc(ev("h_lo"), 1)
                for b in range(NB):
                    for h in range(2):
                        n = 2 * b + h
                        dve.wait_ge(ev("ff2"), j * (2 * NB) + (n + 1))
                        a = M.acc[:, b, h * 512:(h + 1) * 512]
                        nc.vector.tensor_tensor(a, a, ps[:, 6 + h, :], ALU.add).then_inc(ev("acc"), 1)

        @block.tensor
        def _(pe):
            with pe.Fori(0, ROUNDS) as j:
                pe.wait_ge(ev("w1_lo"), j + 1)
                for o in range(O):
                    if o >= 2:
                        pe.wait_ge(ev("relu"), j * O + (o - 1))
                    for g in range(TG):
                        cols = slice(g * TW, (g + 1) * TW)
                        for k in range(KD):
                            last = split_mm(nc, ps[:, 3 * (o % 2) + g, 0:TW], w1hi[:, k, o * P:(o + 1) * P],
                                            w1lo[:, k, o * P:(o + 1) * P], M.hi[:, k, cols], M.lo[:, k, cols],
                                            k == 0, k == KD - 1)
                    last.then_inc(ev("ff1"), 1)
                pe.wait_ge(ev("w2_lo"), j + 1)
                pe.wait_ge(ev("h_lo"), j * O + O)
                for b in range(NB):
                    cols = slice(b * P, (b + 1) * P)
                    for h in range(2):
                        n = 2 * b + h
                        if n >= 2:
                            pe.wait_ge(ev("acc"), j * (2 * NB) + (n - 1))
                        for k in range(O):
                            last = split_mm(nc, ps[:, 6 + h, :], hhi[:, k, cols], hlo[:, k, cols],
                                            w2hi[:, k, h * 512:(h + 1) * 512], w2lo[:, k, h * 512:(h + 1) * 512],
                                            k == 0, k == O - 1)
                        last.then_inc(ev("ff2"), 1)
    clear(nc, ev)
    A.at = keep


def stage_last(nc, M, ins, outs):
    A = M.arena
    keep = A.at
    gate, gf = A.take(2, D), A.take(D)
    xt = [A.take(D) for _ in range(2)]
    junk = [A.take(D) for _ in range(2)]
    ss, ms, rs = ([A.take(1) for _ in range(2)] for _ in range(3))
    with ExitStack() as ctx:
        ev = Events(nc, ctx, "last")
        block = ctx.enter_context(nc.Block())

        @block.sync
        def _(sp):
            sp.dma_start(gate, ins["gates"][1].partition_broadcast(P)).then_inc(ev("gate"), 16)
            sp.dma_start(gf, ins["norm_f_g"]).then_inc(ev("gate"), 16)

            def tile(q, n, b, w):
                need(sp, ev("stored", q), n * 16)
                sp.dma_start(xt[q], ins["x1"][ds(b, 1)].squeeze(0)).then_inc(ev("x", q), 16)
            pairs(sp, tile)

        @block.gpsimd
        def _(pool):
            def tile(q, n, b, w):
                pool.wait_ge(ev("mean_sq", q), n + 1)
                nc.gpsimd.tensor_tensor(rs[q], ms[q], M.neg_half, ALU.pow).then_inc(ev("rstd", q), 1)
                pool.wait_ge(ev("y", q), n + 1)
                pool.dma_start(outs["y"][ds(b, 1)].squeeze(0), xt[q]).then_inc(ev("stored", q), 16)
            pairs(pool, tile)
            pool.wait_ge(ev("stored", 0), 16 * 5)
            pool.wait_ge(ev("stored", 1), 16 * 4)

        @block.scalar
        def _(act):
            def tile(q, n, b, w):
                act.wait_ge(ev("sum", q), n + 1)
                nc.scalar.activation(junk[q], xt[q], ACT.Square, accum_out=ss[q]).then_inc(ev("squares", q), 1)
                act.wait_ge(ev("squares", q), n + 1)
                need(act, ev("rstd", q), n)
                nc.scalar.activation(ms[q], ss[q], ACT.Copy, scale=1.0 / D, bias=RMS_EPS).then_inc(ev("mean_sq", q), 1)
            pairs(act, tile)

        @block.vector
        def _(dve):
            dve.wait_ge(ev("gate"), 32)

            def add(q, n, b, w):
                a = M.acc[:, ds(b, 1)].rearrange("p b c -> p (b c)")
                nc.vector.tensor_tensor(a, a, gate[:, w], ALU.mult).then_inc(ev("gated", q), 1)
                dve.wait_ge(ev("x", q), n * 16 + 16)
                dve.wait_ge(ev("gated", q), n + 1)
                nc.vector.tensor_tensor(xt[q], xt[q], a, ALU.add).then_inc(ev("sum", q), 1)

            def scale(q, n):
                dve.wait_ge(ev("rstd", q), n + 1)
                dve.wait_ge(ev("squares", q), n + 1)
                nc.vector.scalar_tensor_tensor(out=xt[q], in0=xt[q], scalar=rs[q], in1=gf, op0=ALU.mult,
                                               op1=ALU.mult).then_inc(ev("y", q), 1)
            with dve.Fori(0, LB // 2) as i:
                add(0, i, i * 2, 0)
                add(1, i, i * 2 + 1, 0)
                scale(0, i)
                scale(1, i)
            add(0, LB // 2, LB, 1)
            scale(0, LB // 2)
    A.at = keep


class Memory:
    pass


def program(nc, ins, outs, scratch, upto=99):
    M = Memory()
    M.arena = A = Arena(nc, 51200)
    M.ps = nc.alloc_psum_tensor("psum", [P, 8, 512], F32)
    M.const = A.take(P + 64 + 2 * 4 * P + 2 * NLEV * 64 + P + 2 + 1 + 1 + 1)
    at = 0

    def part(n, shape=None):
        nonlocal at
        v = M.const[:, at:at + n]
        at += n
        return v
    M.ident = part(P)
    M.ident64 = part(64)
    M.score_mask = part(2 * 4 * P).rearrange("p (d m t) -> p d m t", d=2, m=4)
    M.level_mask = part(2 * NLEV * 64).rearrange("p (d l t) -> p d l t", d=2, l=NLEV)
    M.head_ones = part(P)
    M.head_ind = part(2)
    M.neg_half = part(1)
    M.one = part(1)
    M.zero = part(1)
    M.scale = [A.take(KD, 2) for _ in range(2)]
    M.shift = [A.take(KD, 2) for _ in range(2)]
    ins.update(scratch)
    stage_modulation(nc, M, ins)
    M.hi = A.take(KD, T, dt=BF16)
    M.lo = A.take(KD, T, dt=BF16)
    stage_norm(nc, M, "norm1", ins["x"], ins["pos"], 0, (M.hi, M.lo))
    keep_front = A.at
    stage_s5_tables(nc, M, ins)
    M.u = A.take(G, NC_)
    stage_u(nc, M, ins)
    stage_s5(nc, M, ins, outs)
    if upto == 2:
        dump(nc, scratch["dbg"], [M.u, M.y_lat])
        return
    after = A.at
    A.at = keep_front
    M.ys_hi, M.ys_lo = A.take(DS // P, T, dt=BF16), A.take(DS // P, T, dt=BF16)
    front = A.at
    A.at = after
    stage_glu(nc, M, ins)
    A.at = front
    stage_rwkv(nc, M, ins, outs)
    if upto == 3:
        dump(nc, scratch["dbg"], [M.ys_hi.bitcast(F32), M.ys_lo.bitcast(F32), M.yr_hi.bitcast(F32), M.yr_lo.bitcast(F32)])
        return
    stage_out(nc, M, ins)
    A.at = keep_front
    stage_norm(nc, M, "norm2", ins["x1"], None, 1, (M.hi, M.lo))
    stage_mlp(nc, M, ins)
    stage_last(nc, M, ins, outs)


def dump(nc, dbg, views):
    with ExitStack() as ctx:
        s = ctx.enter_context(nc.semaphore("dbg"))
        block = ctx.enter_context(nc.Block())

        @block.sync
        def _(sp):
            at = 0
            for v in views:
                n = int(np.prod(v.shape[1:]))
                names = " ".join(f"d{i}" for i in range(len(v.shape) - 1))
                src = dbg[0:v.shape[0], at:at + n]
                if len(v.shape) > 2:
                    src = src.rearrange(f"p ({names}) -> p {names}", **{f"d{i}": v.shape[i + 1] for i in range(len(v.shape) - 1)})
                sp.dma_start(src, v).then_inc(s, 16)
                at += n
            sp.wait_ge(s, 16 * len(views))


def constants():
    s, t = np.meshgrid(np.arange(P), np.arange(P), indexing="ij")
    before, upto = (s < t), (s <= t)
    after, down = (s > t), (s >= t)
    score = np.stack([np.stack([before, upto, before, upto]), np.stack([after, down, after, down])])
    s, t = np.meshgrid(np.arange(P) % 64, np.arange(64), indexing="ij")
    level = np.zeros((2, NLEV, P, 64))
    for l in range(NLEV):
        b = 2 << l
        off = (s // b == t // b) & (s // (b // 2) != t // (b // 2))
        level[0, l] = off & (s < t)
        level[1, l] = off & (s > t)
    ones = np.kron(np.eye(2), np.ones((64, 64)))
    ind = np.kron(np.eye(2), np.ones((64, 1)))
    return np.concatenate([np.eye(P), np.tile(np.eye(64), (2, 1)), score.transpose(2, 0, 1, 3).reshape(P, -1),
                           level.transpose(2, 0, 1, 3).reshape(P, -1), ones, ind, np.full((P, 1), -0.5),
                           np.ones((P, 1)), np.zeros((P, 1))], axis=1).astype(np.float32)


def position_embedding():
    rows, width, nf = NLAT // 64, 64, D // 4
    omega = (np.float32(1.0) / (np.float32(10000.0) ** (np.arange(nf, dtype=np.float32) / np.float32(nf)))).astype(np.float32)
    ar = (np.arange(rows, dtype=np.float32)[:, None] * omega).astype(np.float32)
    ac = (np.arange(width, dtype=np.float32)[:, None] * omega).astype(np.float32)
    er, ec = (np.concatenate([np.sin(a), np.cos(a)], axis=-1) for a in (ar, ac))
    pe = np.concatenate([np.broadcast_to(er[:, None], (rows, width, D // 2)),
                         np.broadcast_to(ec[None], (rows, width, D // 2))], axis=-1).reshape(LB, P, D)
    return np.concatenate([pe, np.zeros((1, P, D))]).astype(np.float32)


def kernel(**inputs):
    import concourse.bacc as bacc
    from concourse.bass_utils import run_bass_kernel_spmd

    x = {k: np.asarray(v) for k, v in inputs.items()}

    def cols(v, n):
        return v.reshape(n, P).T

    a = {
        "consts": constants(),
        "pos": position_embedding(),
        "x": np.concatenate([x["x_sample"][0], x["x_prompt"][0]]).reshape(NB, P, D),
        "cond": np.stack([cols(x["c"][0], KD), cols(x["c_ctx"], KD)], axis=2),
        "norm_g": np.stack([cols(x["norm1_g"][0], KD), cols(x["norm2_g"][0], KD)], axis=1),
        "b_ada": np.stack([x["b_ada"][0]] * 2),
        "w_ada": x["w_ada"][0],
    }
    a.update(more_inputs(x, cols))
    a = {k: np.ascontiguousarray(v) for k, v in a.items()}
    nc = bacc.Bacc("TRN2", target_bir_lowering=False, num_devices=1)
    ins = {k: nc.dram_tensor("in_" + k, v.shape, F32, kind="ExternalInput").ap() for k, v in a.items()}
    for w in ("w_ada", "w_in", "w_glu", "w_out", "w_ff1", "w_ff2"):
        if w in ins:
            ins[w] = ins[w].rearrange("(k p) n -> p k n", p=P)
    shapes = {"y": (NB, P, D), "rwkv": (NCT, P, 2, 64), "ssm": (P, 2, G)}
    outs = {k: nc.dram_tensor("out_" + k, v, F32, kind="ExternalOutput").ap() for k, v in shapes.items()}
    scratch = {"x1": nc.dram_tensor("x1", (NB, P, D), F32, kind="Internal").ap(),
               "gates": nc.dram_tensor("gates", (2, 2, D), F32, kind="Internal").ap(),
               "y_bounce": nc.dram_tensor("y_bounce", (P, DS), F32, kind="Internal").ap(),
               "u_bounce": nc.dram_tensor("u_bounce", (P, DS), F32, kind="Internal").ap()}
    if UPTO < 99:
        scratch["dbg"] = nc.dram_tensor("dbg", (P, 51200), F32, kind="ExternalOutput").ap()
    program(nc, ins, outs, scratch, UPTO)
    r = run_bass_kernel_spmd(nc, [{"in_" + k: v for k, v in a.items()}], core_ids=[0]).results[0]
    y = r["out_y"].reshape(T, D)
    rw = r["out_rwkv"].reshape(NCT, 2, 64, 2, 64)
    rw = rw.transpose(3, 0, 1, 4, 2).reshape(1, 1, 2, 8, 64, 64)
    sm = r["out_ssm"].reshape(2, NS, 2, G)
    return (y[NLAT:].reshape(1, NCTX, D), y[:NLAT].reshape(1, NLAT, D), rw,
            sm[:, :, 0].transpose(0, 2, 1).reshape(1, 1, 2, G, NS),
            sm[:, :, 1].transpose(0, 2, 1).reshape(1, 1, 2, G, NS))


def more_inputs(x, cols):
    def lanes(v):
        v = v.transpose(0, 2, 1, *range(3, v.ndim))
        return v.reshape(P, *v.shape[2:])
    both = lambda v: np.broadcast_to(v[None], (2, *v.shape))
    return {
        "w_in": x["w_in"][0],
        "ssm_par": np.stack([lanes(both(x["ssm_lambda_re"][0])), lanes(both(x["ssm_lambda_im"][0])),
                             lanes(np.broadcast_to(x["ssm_log_dt"][0][:, :, None], (2, G, NS)))], axis=1),
        "ssm_b_re": lanes(x["ssm_b_re"][0]), "ssm_b_im": lanes(x["ssm_b_im"][0]),
        "ssm_c_re": lanes(x["ssm_c_re"][0].transpose(0, 1, 3, 2)),
        "ssm_c_im": lanes(x["ssm_c_im"][0].transpose(0, 1, 3, 2)),
        "ssm_h_re": lanes(x["state_ssm_re"][0, 0]), "ssm_h_im": lanes(x["state_ssm_im"][0, 0]),
        "ssm_d": x["ssm_d"][0].reshape(G, GC).T,
        "w_out": x["w_out"][0], "w_ff1": x["w_ff1"][0], "w_ff2": x["w_ff2"][0],
        "norm_f_g": np.broadcast_to(x["norm_f_g"], (P, D)),
        "w_glu": x["w_glu"][0], "b_glu": cols(x["b_glu"][0], DS // P),
        "par": np.stack([x["k_k"][0], x["k_a"][0], x["r_k"][0].reshape(DR), *x["decay_base"][0], *x["iclr_base"][0]],
                        axis=1).reshape(NCT, P, 7),
        "up": np.stack([x["w_decay_up"][0].reshape(P, DR), x["w_iclr_up"][0].reshape(P, DR), x["w_gate_up"][0]],
                       axis=1).reshape(P, 3, NCT, P).transpose(2, 0, 1, 3),
        "state": x["state_rwkv"][0, 0].reshape(2, NCT, 2, HEAD, HEAD).transpose(1, 2, 4, 0, 3).reshape(NCT, P, 2, HEAD),
        "ln": np.broadcast_to(np.stack([x["lnx_g"][0], x["lnx_b"][0]]).reshape(2, NCT, 1, P).transpose(1, 2, 0, 3),
                              (NCT, P, 2, P)),
    }


UPTO = 99
```
